# Optimizing a Trainium2 kernel written in Bass

```python
import jax, jax.numpy as jnp
from jax import lax
import numpy as np

D_MODEL = 2048
BATCH = 1
SEQ = 256
DEPTH = 1
DEC_BATCH = 1
DEC_SEQ = 64
PAST_LEN = 256

CHUNK = 64
N_HEADS = 8
QK_NOPE = 128
ROPE_DIM = 64
V_DIM = 128
Q_LORA = 512
KV_LORA = 512
ATTN_W = N_HEADS * V_DIM
CONV_CH = D_MODEL - ATTN_W
D_MIX = ATTN_W + CONV_CH
CONV_W = 3
D_IN = Q_LORA + KV_LORA + ROPE_DIM + 3 * CONV_CH
IN_SPLITS = (Q_LORA, Q_LORA + KV_LORA, Q_LORA + KV_LORA + ROPE_DIM,
             Q_LORA + KV_LORA + ROPE_DIM + CONV_CH, Q_LORA + KV_LORA + ROPE_DIM + 2 * CONV_CH)
N_GROUPS = 4
EXPERTS_PER_GROUP = 8
N_EXPERTS = N_GROUPS * EXPERTS_PER_GROUP
TOP_K = 2
D_FF_EXPERT = 512
MOE_BLOCK = 128
QBLK = 128
ROPE_THETA = 10000.0
EPS = 1e-6
ATTN_SCALE = (QK_NOPE + ROPE_DIM) ** -0.5

kernel_name = 'hymba_mla_shortconv_hiermoe_stream_step'

def rmsnorm(x, g):
    xf = x.astype(jnp.float32)
    y = xf * lax.rsqrt(jnp.mean(xf * xf, axis=-1, keepdims=True) + EPS)
    return (y * g.astype(jnp.float32)).astype(x.dtype)

def rope(x, pos):
    inv = ROPE_THETA ** (-jnp.arange(0, ROPE_DIM, 2, dtype=jnp.float32) / ROPE_DIM)
    ang = pos.astype(jnp.float32)[:, None] * inv[None, :]
    cos = jnp.cos(ang)[:, None, :]
    sin = jnp.sin(ang)[:, None, :]
    xf = x.astype(jnp.float32)
    x1, x2 = xf[..., :ROPE_DIM // 2], xf[..., ROPE_DIM // 2:]
    return jnp.concatenate([x1 * cos - x2 * sin, x1 * sin + x2 * cos], axis=-1).astype(x.dtype)

def mla_attend(q_lat, q_rope, ckv, krope, q_pos, k_pos):
    B, Tq, H, L = q_lat.shape
    blk = min(QBLK, Tq)
    nb = Tq // blk
    k_chunk = k_pos // CHUNK

    def one_block(args):
        ql, qr, qp = args
        s = (jnp.einsum('bqhl,bkl->bhqk', ql, ckv) + jnp.einsum('bqhr,bkr->bhqk', qr, krope))
        s = s.astype(jnp.float32) * ATTN_SCALE
        mask = (qp[:, None] // CHUNK) >= k_chunk[None, :]
        p = jax.nn.softmax(jnp.where(mask, s, -jnp.inf), axis=-1).astype(ckv.dtype)
        return jnp.einsum('bhqk,bkl->bqhl', p, ckv)

    qlb = q_lat.reshape(B, nb, blk, H, L).swapaxes(0, 1)
    qrb = q_rope.reshape(B, nb, blk, H, ROPE_DIM).swapaxes(0, 1)
    o = lax.map(one_block, (qlb, qrb, q_pos.reshape(nb, blk)))
    return o.swapaxes(0, 1).reshape(B, Tq, H, L)

def token_mixer(xn, pos, past_ckv, past_krope, conv_state, w_in, g_q, w_uq, g_kv, w_uk, w_uv,
                conv_w, g_ao, g_co, w_o):
    B, T, _ = xn.shape
    z = xn @ w_in
    c_q, c_kv, k_r, gate_b, gate_c, h = jnp.split(z, IN_SPLITS, axis=-1)
    q = (rmsnorm(c_q, g_q) @ w_uq).reshape(B, T, N_HEADS, QK_NOPE + ROPE_DIM)
    q_nope = q[..., :QK_NOPE]
    q_rope = rope(q[..., QK_NOPE:], pos)
    c_kv = rmsnorm(c_kv, g_kv)
    k_rope = rope(k_r[:, :, None, :], pos)[:, :, 0, :]
    q_lat = jnp.einsum('bthn,lhn->bthl', q_nope, w_uk)
    if past_ckv is None:
        keys_ckv, keys_kr = c_kv, k_rope
    else:
        keys_ckv = jnp.concatenate([past_ckv, c_kv], axis=1)
        keys_kr = jnp.concatenate([past_krope, k_rope], axis=1)
    k_pos = jnp.arange(keys_ckv.shape[1], dtype=jnp.int32)
    o_lat = mla_attend(q_lat, q_rope, keys_ckv, keys_kr, pos, k_pos)
    attn = jnp.einsum('bthl,lhv->bthv', o_lat, w_uv).reshape(B, T, ATTN_W)
    u = gate_c * h
    u_ext = jnp.concatenate([conv_state, u], axis=1)
    conv = sum(conv_w[j] * u_ext[:, j:j + T] for j in range(CONV_W))
    conv_out = gate_b * conv
    y = jnp.concatenate([rmsnorm(attn, g_ao), rmsnorm(conv_out, g_co)], axis=-1) @ w_o
    return y, c_kv, k_rope, u_ext[:, -(CONV_W - 1):]

def hier_moe(x2, w_rg, b_rg, w_re, b_re, w_gate, w_up, w_down):
    T, D = x2.shape
    xf = x2.astype(jnp.float32)
    tok = jnp.arange(T)
    g_logits = xf @ w_rg.astype(jnp.float32) + b_rg.astype(jnp.float32)
    g_prob = jax.nn.softmax(g_logits, axis=-1)
    g_idx = jnp.argmax(g_logits, axis=-1).astype(jnp.int32)
    g_p = g_prob[tok, g_idx][:, None]
    e_logits = jnp.einsum('td,dge->tge', xf, w_re.astype(jnp.float32)) + b_re.astype(jnp.float32)
    e_prob = jax.nn.softmax(e_logits[tok, g_idx], axis=-1)
    top_p, top_i = lax.top_k(e_prob, TOP_K)
    gate = (g_p * top_p / jnp.sum(top_p, axis=-1, keepdims=True)).astype(x2.dtype)
    expert_idx = g_idx[:, None] * EXPERTS_PER_GROUP + top_i.astype(jnp.int32)
    A = T * TOP_K
    flat_e = expert_idx.reshape(A)
    flat_tok = jnp.arange(A, dtype=jnp.int32) // TOP_K
    flat_g = gate.reshape(A)
    order = jnp.argsort(flat_e)
    se = flat_e[order]
    counts = jnp.bincount(flat_e, length=N_EXPERTS)
    padded = (counts + MOE_BLOCK - 1) // MOE_BLOCK * MOE_BLOCK
    pad_end = jnp.cumsum(padded)
    pad_start = pad_end - padded
    start = jnp.cumsum(counts) - counts
    dest = pad_start[se] + jnp.arange(A) - start[se]
    n_blocks = -(-A // MOE_BLOCK) + N_EXPERTS
    P = n_blocks * MOE_BLOCK
    row_tok = jnp.full((P,), T, jnp.int32).at[dest].set(flat_tok[order])
    row_gate = jnp.zeros((P,), x2.dtype).at[dest].set(flat_g[order])
    block_e = jnp.minimum(jnp.searchsorted(pad_end, jnp.arange(n_blocks) * MOE_BLOCK, side='right'),
                          N_EXPERTS - 1)
    x_pad = jnp.concatenate([x2, jnp.zeros((1, D), x2.dtype)], axis=0)

    def expert_block(args):
        rt, rg, e = args
        xb = x_pad[rt]
        hb = jax.nn.silu(xb @ w_gate[e]) * (xb @ w_up[e])
        return (hb @ w_down[e]) * rg[:, None]

    out = lax.map(expert_block, (row_tok.reshape(n_blocks, MOE_BLOCK),
                                 row_gate.reshape(n_blocks, MOE_BLOCK), block_e))
    return jax.ops.segment_sum(out.reshape(P, D), row_tok, num_segments=T + 1)[:T]

def trunk_layer(x, pos, past_ckv, past_krope, conv_state, norm_mix, w_in, norm_q, w_uq, norm_kv,
                w_uk, w_uv, conv_w, norm_attn_out, norm_conv_out, w_o, norm_ffn, w_router_group,
                b_router_group, w_router_expert, b_router_expert, w_gate, w_up, w_down):
    mix, c_kv, k_rope, new_conv = token_mixer(rmsnorm(x, norm_mix), pos, past_ckv, past_krope,
                                              conv_state, w_in, norm_q, w_uq, norm_kv, w_uk, w_uv,
                                              conv_w, norm_attn_out, norm_conv_out, w_o)
    h = x + mix
    B, T, D = h.shape
    ffn = hier_moe(rmsnorm(h, norm_ffn).reshape(B * T, D), w_router_group, b_router_group,
                   w_router_expert, b_router_expert, w_gate, w_up, w_down).reshape(B, T, D)
    return h + ffn, c_kv, k_rope, new_conv

def setup_inputs(seed: int = 0) -> dict:
    key = jax.random.key(seed)
    ks = jax.random.split(key, 26)

    def nrm(k, shape, scale):
        return jax.random.normal(k, shape, jnp.float32) * scale

    def gain(k, shape):
        return 1.0 + 0.01 * jax.random.normal(k, shape, jnp.float32)

    return {
        'x_prompt': nrm(ks[0], (BATCH, SEQ, D_MODEL), 1.0),
        'x_sample': nrm(ks[1], (DEC_BATCH, DEC_SEQ, D_MODEL), 1.0),
        'cache_kv_latent': nrm(ks[2], (DEPTH, DEC_BATCH, PAST_LEN, KV_LORA), 1.0),
        'cache_k_rope': nrm(ks[3], (DEPTH, DEC_BATCH, PAST_LEN, ROPE_DIM), 1.0),
        'state_conv': nrm(ks[4], (DEPTH, DEC_BATCH, CONV_W - 1, CONV_CH), 1.0),
        'norm_mix': gain(ks[5], (DEPTH, D_MODEL)),
        'w_in': nrm(ks[6], (DEPTH, D_MODEL, D_IN), D_MODEL ** -0.5),
        'norm_q': gain(ks[7], (DEPTH, Q_LORA)),
        'w_uq': nrm(ks[8], (DEPTH, Q_LORA, N_HEADS * (QK_NOPE + ROPE_DIM)), Q_LORA ** -0.5),
        'norm_kv': gain(ks[9], (DEPTH, KV_LORA)),
        'w_uk': nrm(ks[10], (DEPTH, KV_LORA, N_HEADS, QK_NOPE), KV_LORA ** -0.5),
        'w_uv': nrm(ks[11], (DEPTH, KV_LORA, N_HEADS, V_DIM), KV_LORA ** -0.5),
        'conv_w': nrm(ks[12], (DEPTH, CONV_W, CONV_CH), CONV_W ** -0.5),
        'norm_attn_out': gain(ks[13], (DEPTH, ATTN_W)),
        'norm_conv_out': gain(ks[14], (DEPTH, CONV_CH)),
        'w_o': nrm(ks[15], (DEPTH, D_MIX, D_MODEL), D_MIX ** -0.5),
        'norm_ffn': gain(ks[16], (DEPTH, D_MODEL)),
        'w_router_group': nrm(ks[17], (DEPTH, D_MODEL, N_GROUPS), D_MODEL ** -0.5),
        'b_router_group': nrm(ks[18], (DEPTH, N_GROUPS), 0.01),
        'w_router_expert': nrm(ks[19], (DEPTH, D_MODEL, N_GROUPS, EXPERTS_PER_GROUP), D_MODEL ** -0.5),
        'b_router_expert': nrm(ks[20], (DEPTH, N_GROUPS, EXPERTS_PER_GROUP), 0.01),
        'w_gate': nrm(ks[21], (DEPTH, N_EXPERTS, D_MODEL, D_FF_EXPERT), D_MODEL ** -0.5),
        'w_up': nrm(ks[22], (DEPTH, N_EXPERTS, D_MODEL, D_FF_EXPERT), D_MODEL ** -0.5),
        'w_down': nrm(ks[23], (DEPTH, N_EXPERTS, D_FF_EXPERT, D_MODEL), D_FF_EXPERT ** -0.5),
        'norm_final': gain(ks[24], (D_MODEL,)),
    }

def reference(x_prompt, x_sample, cache_kv_latent, cache_k_rope, state_conv, norm_mix, w_in, norm_q,
              w_uq, norm_kv, w_uk, w_uv, conv_w, norm_attn_out, norm_conv_out, w_o, norm_ffn,
              w_router_group, b_router_group, w_router_expert, b_router_expert, w_gate, w_up, w_down,
              norm_final):
    pos_p = jnp.arange(x_prompt.shape[1], dtype=jnp.int32)
    pos_s = cache_kv_latent.shape[2] + jnp.arange(x_sample.shape[1], dtype=jnp.int32)
    xp, xs = x_prompt, x_sample
    kvp, krp, cvp, kvs, krs, cvs = [], [], [], [], [], []
    for l in range(DEPTH):
        lw = (norm_mix[l], w_in[l], norm_q[l], w_uq[l], norm_kv[l], w_uk[l], w_uv[l], conv_w[l],
              norm_attn_out[l], norm_conv_out[l], w_o[l], norm_ffn[l], w_router_group[l],
              b_router_group[l], w_router_expert[l], b_router_expert[l], w_gate[l], w_up[l], w_down[l])
        zero_conv = jnp.zeros((xp.shape[0], CONV_W - 1, CONV_CH), xp.dtype)
        xp, a, b, c = trunk_layer(xp, pos_p, None, None, zero_conv, *lw)
        kvp.append(a); krp.append(b); cvp.append(c)
        xs, a, b, c = trunk_layer(xs, pos_s, cache_kv_latent[l], cache_k_rope[l], state_conv[l], *lw)
        kvs.append(a); krs.append(b); cvs.append(c)
    y_prompt = rmsnorm(xp, norm_final)
    y_sample = rmsnorm(xs, norm_final)
    return (y_prompt, y_sample, jnp.stack(kvp), jnp.stack(krp), jnp.stack(cvp),
            jnp.stack(kvs), jnp.stack(krs), jnp.stack(cvs))


_drawn_inputs = setup_inputs


def setup_inputs(seed=0):
    import zlib

    import numpy as np

    out = dict(_drawn_inputs(seed))
    spreads = {}
    factors = {'norm_q': 3.716,
     'norm_kv': 4.751,
     'norm_attn_out': 4.083,
     'norm_conv_out': 4.44,
     'norm_ffn': 3.287,
     'b_router_group': 5.936,
     'b_router_expert': 3.357,
     'norm_final': 32.143,
     'cache_kv_latent': 8.0,
     'cache_k_rope': 8.0}
    for name, (base, spread) in spreads.items():
        noise = np.random.default_rng([zlib.crc32(name.encode()), seed]).standard_normal(out[name].shape)
        drawn = base * np.exp(spread * noise) if base else spread * noise
        out[name] = __import__('jax').numpy.asarray(drawn.astype(out[name].dtype))
    for name, factor in factors.items():
        out[name] = (out[name] * factor).astype(out[name].dtype)
    return out
```

```python
from contextlib import ExitStack

import concourse.bass as bass
from concourse import mybir

F32 = mybir.dt.float32
I32 = mybir.dt.int32
U32 = mybir.dt.uint32
ALU = mybir.AluOpType
ACT = mybir.ActivationFunctionType
AX = mybir.AxisListType.X

P = 128
D = 2048
SEQ, DEC, PAST = 256, 64, 256
T = SEQ + DEC
TILES = ((0, 128), (128, 128), (256, 64))
CHUNK = 64
H = 8
NOPE, ROPE, VD = 128, 64, 128
QKD = NOPE + ROPE
QL, KL = 512, 512
CH = 1024
NCH = CH // P
KC = D // P
LC = QL // P
KEYS = T + PAST
G, EPG = 4, 8
NE = G * EPG
FF = 512
B = 32
MAXB = -(-T // B)
EPS = 1e-6
SCALE = float(QKD) ** -0.5
SLOTS = 6
SLOT = 4096
RB = 6
SSQ_BANK, ACC_BANK = 6, 7
NEG = -3.0e38

C_ID, C_ROT, C_TRI, C_DUP, C_DROT = 0, 128, 256, 384, 512
C_FOLD, C_IOTA, C_THR, C_COS = 640, 704, 736, 736 + MAXB
C_SIN = C_COS + T
C_ALL = C_SIN + T
P_MIX, P_Q, P_KV, P_CONV, P_AO, P_CO, P_ST = 0, 16, 20, 24, 48, 56, 64
P_ALL = 80

W_CQ, W_KV, W_KR, W_CONV, W_UV, W_PAIR, W_O = 0, 2, 4, 5, 17, 18, 22
W_END = 30

KT = ((0, 128), (128, 128), (256, 128), (384, 128), (512, 64))


def psum_jobs():
    jobs = [("par", "act")]
    jobs += [(f"xt{i}_{k}", "dve") for i in range(3) for k in range(4)]
    jobs += [(f"cq{m}", "act") for m in range(LC)] + [(f"ckv{m}", "act") for m in range(LC)]
    jobs += [("kr", "act"), ("cc0", "act"), ("cc1", "act"), ("ckr", "act"), ("krdup", "dve"), ("krrot", "dve")]
    for j in range(NCH // 2):
        jobs += [(f"C{2 * j + k}", "act") for k in range(2)]
        jobs += [(f"h{2 * j + k}", "dve") for k in range(2)]
        jobs += [(f"B{2 * j + k}", "dve") for k in range(2)]
        if j == 0:
            jobs += [("okv0", "act"), ("okv1", "act"), ("okv2", "act"), ("okr", "act")]
    jobs += [(f"V{t}_{v}", "act") for t in range(5) for v in range(2)]
    jobs += [("ulast", "act")]

    def pair_jobs(p):
        return ([(f"q{2 * p + i}", "act") for i in range(2)] + [(f"qr{p}", "act")]
                + [(f"K{2 * p + i}_{s}", "dve") for i in range(2) for s in range(2)] + [(f"qrot{p}", "dve")])

    jobs += pair_jobs(0)
    for p in range(H // 2):
        jobs += [(f"S{2 * p + i}{s}", "act") for i in range(2) for s in "ab"]
        if p + 1 < H // 2:
            jobs += pair_jobs(p + 1)
        for h in (2 * p, 2 * p + 1):
            jobs += [(f"PT{h}a", "dve"), (f"PT{h}b", "dve"), (f"PV{h}", "act")]
    for n in range(4):
        jobs += [(f"wo{n}_{i}", "dve") for i in range(3)]
        if n >= 1:
            jobs += [(f"rt{n - 1}_{i}", "act") for i in range(3)]
    jobs += [(f"rt3_{i}", "act") for i in range(3)]
    return jobs


def trunk_layer_kernel(nc: bass.Bass, a):
    jobs = psum_jobs()
    job_index = {name: i for i, (name, _) in enumerate(jobs)}
    drain_count = {}
    for name, engine in jobs:
        drain_count[name] = 1 + sum(1 for n, e in jobs[:job_index[name]] if e == engine)

    with ExitStack() as ctx:
        def sb(name, shape, dt=F32):
            return ctx.enter_context(nc.sbuf_tensor(name, shape, dt))

        def sem(name):
            return ctx.enter_context(nc.semaphore(name))

        ring = sb("ring", [P, SLOTS, SLOT])
        hreg = sb("hreg", [P, 3 * D])
        r2 = sb("r2", [P, 3 * D])
        mix = sb("mix", [P, KC, T])
        ckv = sb("ckv", [P, LC, KEYS])
        cq = sb("cq", [P, LC, T])
        krt = sb("krt", [P, KEYS])
        const = sb("const", [P, C_ALL])
        par = sb("par", [P, P_ALL])
        ones = sb("ones", [P, P])
        work = sb("work", [P, 5200])
        small = sb("small", [P, 64])
        tables = sb("tables", [1, 3, NE], I32)

        ps = ctx.enter_context(nc.psum_tensor("ps", [P, 8, 512], F32))

        ident = const[:, C_ID:C_ID + P]
        cos, sin = const[:, C_COS:C_COS + T], const[:, C_SIN:C_SIN + T]
        xtile = hreg[:, :].rearrange("p (i d) -> p i d", i=3)
        xT = r2[:, 0:KC * T].rearrange("p (c t) -> p c t", c=KC)
        xnorm = mix[:, :, :].rearrange("p c t -> p (c t)")[:, 0:2 * D].rearrange("p (i d) -> p i d", i=2)
        sq_q = mix[:, 0:4, :]
        sq_kv = mix[:, 4:8, :]
        cstage = work[:, 0:2 * KL].rearrange("p (i l) -> p i l", i=2)
        ckrstage = work[:, 1024:1280].rearrange("p (i r) -> p i r", i=2)
        csb = work[:, 0:2 * T].rearrange("p (i t) -> p i t", i=2)
        UE = T + 4
        uext = work[:, 640:640 + NCH * UE].rearrange("p (c u) -> p c u", c=NCH)
        cv = work[:, 3232:3232 + UE - 2]
        sq = work[:, 3554:3554 + 2 * T].rearrange("p (i t) -> p i t", i=2)
        rs = work[:, 4194:4194 + T]
        rot_a = work[:, 4514:4514 + T]
        rot_b = work[:, 4834:4834 + T]
        kraw = cv[0:ROPE, 0:T]
        ulast = small[:, 0:32].rearrange("p (r c) -> p r c", r=4)
        eps_col = small[:, 62:63]
        xss, xsd, xrs = small[:, 32:35], small[:, 35:38], small[:, 38:41]
        okv = hreg[:, 0:3 * KL].rearrange("p (i l) -> p i l", i=3)
        okr = hreg[:, 1536:1536 + 3 * ROPE].rearrange("p (i r) -> p i r", i=3)
        oul = hreg[0:32, 5120:5120 + P]
        par_rows = work[0:P_ALL, 1280:1280 + P]
        vals = hreg[:, 0:5 * CH].rearrange("p (k v) -> p k v", k=5)
        qt = r2[:, 0:1920].rearrange("p (b i t) -> p b i t", b=2, i=3)
        kt = r2[:, 1920:4224].rearrange("p (b i k) -> p b i k", b=2, i=2)
        qraw = r2[:, 4224:4544]
        att_a = r2[:, 4544:4864]
        att_b = r2[:, 4864:5184]
        pb = [work[:, 0:704], work[:, 704:1408]]
        ptb = [work[:, 1408:1984], work[:, 1984:2560]]
        mx = [small[:, 44 + 3 * k:47 + 3 * k] for k in range(2)]
        nb_ = [small[:, 50 + 3 * k:53 + 3 * k] for k in range(2)]
        sm = [small[:, 56 + 3 * k:59 + 3 * k] for k in range(2)]
        xn = r2[:, :].rearrange("p (i c q) -> p i c q", i=3, c=KC)
        wr = cq[:, :, :].rearrange("p c t -> p (c t)")[:, 0:KC * 36].rearrange("p (c e) -> p c e", c=KC)
        brow = cq[:, :, :].rearrange("p c t -> p (c t)")[:, 576:612]
        gain = ckv[:, :, :].rearrange("p c t -> p (c t)")[:, 0:D]
        rtb = [work[:, 2560:3072].rearrange("p (c t) -> p c t", c=4), work[:, 0:512].rearrange("p (c t) -> p c t", c=4)]
        junk = work[:, 512:1024]
        w0 = 1024
        hss = work[:, w0:w0 + 12].rearrange("p (i n) -> p i n", i=3)
        hsum, hsd, hrs = (work[:, w0 + 12 + 3 * k:w0 + 15 + 3 * k] for k in range(3))
        w0 += 24
        lg = work[:, w0:w0 + 24].rearrange("p (i g) -> p i g", i=3)
        le = work[:, w0 + 24:w0 + 120].rearrange("p (i e) -> p i e", i=3)
        m8 = work[:, w0 + 120:w0 + 144].rearrange("p (i e) -> p i e", i=3)
        v8 = work[:, w0 + 144:w0 + 168].rearrange("p (i e) -> p i e", i=3)
        el = work[:, w0 + 168:w0 + 192].rearrange("p (i e) -> p i e", i=3)
        gx = work[:, w0 + 192:w0 + 204].rearrange("p (i g) -> p i g", i=3)
        ghot = work[:, w0 + 204:w0 + 216].rearrange("p (i g) -> p i g", i=3)
        gidx, gsum, gp, dv, ev, den, rden = (work[:, w0 + 216 + 3 * k:w0 + 219 + 3 * k] for k in range(7))
        eidx = work[:, w0 + 240:w0 + 246].rearrange("p (i k) -> p i k", i=3)
        eid = work[:, w0 + 246:w0 + 252].rearrange("p (i k) -> p i k", i=3)
        gate = work[:, w0 + 252:w0 + 258].rearrange("p (i k) -> p i k", i=3)
        dest = work[:, w0 + 258:w0 + 264].rearrange("p (i k) -> p i k", i=3)
        w0 += 264
        hot = work[:, w0:w0 + 192].rearrange("p (i k e) -> p i k e", i=3, k=2)
        hot2 = work[:, w0 + 192:w0 + 288].rearrange("p (i e) -> p i e", i=3)
        slot_of = work[:, w0 + 288:w0 + 384].rearrange("p (i e) -> p i e", i=3)
        prod_flat = work[:, w0 + 384:w0 + 576]
        prod = work[:, w0 + 384:w0 + 576].rearrange("p (i k e) -> p i k e", i=3, k=2)
        cmp = work[:, w0 + 576:w0 + 576 + NE * (MAXB - 1)].rearrange("p (e j) -> p e j", e=NE)
        w0 += 576 + NE * (MAXB - 1)
        nblk, sincl, sexcl = (work[:, w0 + NE * k:w0 + NE * k + NE] for k in range(3))
        w0 += 3 * NE
        i8 = sb("i8", [P, 2, 3, 8], U32)
        assert w0 <= 2560, w0
        mflat = mix[:, :, :].rearrange("p c t -> p (c t)")
        xg = mflat[:, 0:512].rearrange("p (c s) -> p c s", c=KC)
        hsb = mflat[:, 512:1024].rearrange("p (c q) -> p c q", c=4)
        hT = mflat[:, 1024:1152].rearrange("p (c s) -> p c s", c=4)
        sil = mflat[:, 1152:1280].rearrange("p (c s) -> p c s", c=4)
        ysb = mflat[:, 1280:1792]
        gT = mflat[:, 1792:2112]
        eq = mflat[:, 2112:2304].rearrange("p (i k s) -> p i k s", i=3, k=2)
        pick = mflat[:, 2304:2400].rearrange("p (i s) -> p i s", i=3)
        pickr = mflat[:, 2400:2496].rearrange("p (i s) -> p i s", i=3)
        geq = mflat[:, 2496:2688].rearrange("p (i k s) -> p i k s", i=3, k=2)
        gpick = mflat[:, 2688:3072].rearrange("p (i j s) -> p i j s", i=3, j=4)
        gpick2 = mflat[:, 2688:3072].rearrange("p (i m) -> p i m", i=3)

        s_const, s_par, s_cache = sem("s_const"), sem("s_par"), sem("s_cache")
        s_x = [sem(f"s_x{i}") for i in range(3)]
        slot_full = [sem(f"slot_full{i}") for i in range(SLOTS)]
        psum_full = sem("psum_full")
        drained = {"act": sem("drained_act"), "dve": sem("drained_dve")}
        s_ones = sem("s_ones")
        x_squared, x_rooted, x_scaled = sem("x_squared"), sem("x_rooted"), sem("x_scaled")
        ssq_full, rooted, normed = sem("ssq_full"), sem("rooted"), sem("normed")
        kr_ready, conv_squared = sem("kr_ready"), sem("conv_squared")
        ulast_ready = sem("ulast_ready")
        q_ready, max_ready, p_ready = sem("q_ready"), sem("max_ready"), sem("p_ready")
        wo_half_used = sem("wo_half_used")
        s_xagain, s_router, s_gffn, s_gfin = sem("s_xagain"), sem("s_router"), sem("s_gffn"), sem("s_gfin")
        hg_ready, h_squared, logits_full = sem("hg_ready"), sem("h_squared"), sem("logits_full")
        hot_ready, route_in, route_act, route_pe = sem("hot_ready"), sem("route_in"), sem("route_act"), sem("route_pe")
        routed = sem("routed")
        dve_step = sem("dve_step")
        conv_summed = sem("conv_summed")
        pick_ready, gathered, gt_full = sem("pick_ready"), sem("gathered"), sem("gt_full")
        xg_ready, gt_copied, weights_used, h_copied = sem("xg_ready"), sem("gt_copied"), sem("weights_used"), sem("h_copied")
        folded, silu_ready, hT_ready, y_copied = sem("folded"), sem("silu_ready"), sem("hT_ready"), sem("y_copied")
        comb_full, comb_added = sem("comb_full"), sem("comb_added")
        blk_step = sem("blk_step")
        fin_squared, fin_rooted, fin_ready = sem("fin_squared"), sem("fin_rooted"), sem("fin_ready")
        s_out, s_stage, s_final = sem("s_out"), sem("s_stage"), sem("s_final")

        xp, xs = a["x_prompt"][0], a["x_sample"][0]
        x_src = (xp[0:128, :], xp[128:256, :], xs)
        w_in = a["w_in"][0].rearrange("(c p) n -> p c n", p=P)
        w_uq = a["w_uq"][0].rearrange("(c p) n -> p c n", p=P)
        w_uk = a["w_uk"][0].rearrange("(c p) h n -> p c (h n)", p=P)
        w_uv = a["w_uv"][0].rearrange("(c p) h n -> p c (h n)", p=P)
        w_o = a["w_o"][0].rearrange("(c p) n -> p c n", p=P)

        def bank(name):
            return ps[:, job_index[name] % RB, :]

        def full(name):
            return job_index[name] + 1

        def claim(pe, name):
            n = job_index[name] - RB
            if n >= 0:
                before, engine = jobs[n]
                pe.wait_ge(drained[engine], drain_count[before])
            return bank(name)

        def slot_count(n):
            return 32 * (n // SLOTS + 1)

        def wslot(n):
            return ring[:, n % SLOTS, :]

        def phase1_weights():
            def cols(n, first, count, last):
                v = wslot(n)[:, 0:KC * count].rearrange("p (c n) -> p c n", c=KC)
                return n, [(v[:, k:k + 8, :], w_in[:, k:k + 8, first:first + count]) for k in (0, 8)], last

            for m in range(2):
                yield cols(W_CQ + m, 256 * m, 256, f"cq{2 * m + 1}")
            for m in range(2):
                yield cols(W_KV + m, QL + 256 * m, 256, f"ckv{2 * m + 1}")
            yield cols(W_KR, QL + KL, ROPE, "kr")
            base = QL + KL + ROPE
            for j in range(NCH // 2):
                for k, (first, job) in enumerate(((base + CH, "C"), (base + 2 * CH, "h"), (base, "B"))):
                    yield cols(W_CONV + 3 * j + k, first + 256 * j, 256, f"{job}{2 * j + 1}")
            v = wslot(W_UV).rearrange("p (c n) -> p c n", c=LC)
            yield W_UV, [(v[:, k:k + 2, :], w_uv[:, k:k + 2, :]) for k in (0, 2)], "V4_1"
            for p in range(H // 2):
                s = wslot(W_PAIR + p)
                yield W_PAIR + p, [
                    (s[:, 0:1536].rearrange("p (c n) -> p c n", c=LC), w_uq[:, :, 2 * QKD * p:2 * QKD * (p + 1)]),
                    (s[:, 1536:2560].rearrange("p (c n) -> p c n", c=LC), w_uk[:, :, 256 * p:256 * (p + 1)]),
                ], f"K{2 * p + 1}_1"
            for n in range(4):
                for half in range(2):
                    v = wslot(W_O + 2 * n + half).rearrange("p (c n) -> p c n", c=8)
                    k0 = 8 * (1 - half)
                    yield W_O + 2 * n + half, [
                        (v[:, k:k + 4, :], w_o[:, k0 + k:k0 + k + 4, 512 * n:512 * n + 512]) for k in (0, 4)
                    ], (f"half{n}" if half == 0 else f"wo{n}_2")

        w1 = list(phase1_weights())
        assert [n for n, _, _ in w1] == list(range(W_END))

        def expert_slot(i, gate_w, up_w, down_w):
            if i < 4:
                s = ring[:, i, :].rearrange("p (m c n) -> p m c n", m=2, c=4)
                return [(s[:, m], w[512 * i:512 * i + 512, :].rearrange("(p c) n -> p c n", c=4))
                        for m, w in enumerate((gate_w, up_w))]
            s = ring[:, i, :].rearrange("p (c n) -> p c n", c=2)
            v = down_w.rearrange("(p c) n -> p c n", c=4)
            return [(s[:, c], v[:, 2 * (i - 4) + c, :]) for c in range(2)]

        def wait_slot_free(sp, last):
            if last.startswith("half"):
                sp.wait_ge(wo_half_used, int(last[4:]) + 1)
            else:
                sp.wait_ge(psum_full, full(last))

        block = ctx.enter_context(nc.Block())

        @block.sync
        def _(sp):
            sp.dma_start(xtile[:, 0, :], x_src[0]).then_inc(s_x[0], 16)
            sp.dma_start(const[:, :], a["const"]).then_inc(s_const, 16)
            sp.dma_start(xtile[:, 1, :], x_src[1]).then_inc(s_x[1], 16)
            sp.dma_start(xtile[0:64, 2, :], x_src[2]).then_inc(s_x[2], 16)
            used_by = {n: last for n, _, last in w1}
            for n, parts, _ in w1:
                if n >= SLOTS:
                    wait_slot_free(sp, used_by[n - SLOTS])
                for dst, src in parts:
                    sp.dma_start(dst, src).then_inc(slot_full[n % SLOTS], 16)
            for i in range(SLOTS):
                wait_slot_free(sp, used_by[W_END - SLOTS + i])
                for dst, src in expert_slot(i, a["w_gate"][0, 0], a["w_up"][0, 0], a["w_down"][0, 0]):
                    sp.dma_start(dst, src).then_inc(slot_full[i], 16)
            sp.wait_ge(routed, 3)
            with sp.Fori(1, NE) as e:
                before = sp.value_load(tables[0:1, 2, bass.ds(e, 1)], min_val=0, max_val=6 * 64)
                for i in range(SLOTS):
                    sp.wait_ge(weights_used, before + (i + 1))
                    w = [a[k][0, bass.ds(e, 1)].rearrange("a b c -> (a b) c") for k in ("w_gate", "w_up", "w_down")]
                    for dst, src in expert_slot(i, *w):
                        sp.dma_start(dst, src).then_inc(slot_full[i], 16)
            for i, (t0, tn) in enumerate(TILES):
                sp.wait_ge(fin_ready, i + 1)
                out = a["y_prompt"][0][t0:t0 + tn, :] if i < 2 else a["y_sample"][0]
                sp.dma_start(out, xtile[0:tn, i, :]).then_inc(s_final, 16)
            sp.wait_ge(s_final, 48)
            sp.wait_ge(s_out, 64)
            sp.wait_ge(s_stage, 64)

        @block.gpsimd
        def _(pool):
            loads = ((P_MIX, a["norm_mix"], 16), (P_Q, a["norm_q"], 4), (P_KV, a["norm_kv"], 4),
                     (P_AO, a["norm_attn_out"], 8), (P_CO, a["norm_conv_out"], 8))
            for first, src, n in loads:
                pool.dma_start(par_rows[first:first + n, :], src.rearrange("a (c p) -> (a c) p", p=P)).then_inc(s_par, 16)
            pool.dma_start(par_rows[P_CONV:P_CONV + 24, :],
                           a["conv_w"][0].rearrange("j (c p) -> (j c) p", p=P)).then_inc(s_par, 16)
            pool.dma_start(par_rows[P_ST:P_ST + 16, :],
                           a["state_conv"][0, 0].rearrange("j (c p) -> (j c) p", p=P)).then_inc(s_par, 16)
            pool.dma_start(cstage, a["cache_kv_latent"][0, 0].rearrange("(i p) l -> p i l", p=P)).then_inc(s_cache, 16)
            for k in range(2):
                pool.dma_start(ckrstage[:, :, ROPE * k:ROPE * (k + 1)],
                               a["cache_k_rope"][0, 0].rearrange("(i p) r -> p i r", p=P)).then_inc(s_cache, 16)
            pool.wait_ge(drained["act"], drain_count["okr"])
            pool.dma_start(a["kv_prompt"][0, 0].rearrange("(i p) l -> p i l", p=P), okv[:, 0:2, :]).then_inc(s_out, 16)
            pool.dma_start(a["kv_sample"][0, 0], okv[0:64, 2, :]).then_inc(s_out, 16)
            pool.dma_start(a["kr_prompt"][0, 0].rearrange("(i p) r -> p i r", p=P), okr[:, 0:2, :]).then_inc(s_out, 16)
            pool.dma_start(a["kr_sample"][0, 0], okr[0:64, 2, :]).then_inc(s_out, 16)
            pool.wait_ge(drained["act"], drain_count["ulast"])
            for s, name in enumerate(("conv_prompt", "conv_sample")):
                for k in range(2):
                    r = 2 * s + k
                    pool.dma_start(a[name][0, 0, k:k + 1].rearrange("a (c p) -> (a c) p", p=P),
                                   hreg[8 * r:8 * r + 8, 5120:5120 + P]).then_inc(s_stage, 16)
            pool.wait_ge(psum_full, full(f"K{H - 1}_1"))
            for i in range(4):
                v = a["w_router_group"][0].rearrange("(i p c) e -> i p c e", p=P, c=4)
                pool.dma_start(wr[:, 4 * i:4 * i + 4, 0:G], v[i]).then_inc(s_router, 16)
                v = a["w_router_expert"][0].rearrange("(i p c) g e -> i p c (g e)", p=P, c=4)
                pool.dma_start(wr[:, 4 * i:4 * i + 4, G:G + NE], v[i]).then_inc(s_router, 16)
            pool.dma_start(brow[:, 0:G], a["b_router_group"].to_broadcast([P, G])).then_inc(s_router, 16)
            pool.dma_start(brow[:, G:G + NE],
                           a["b_router_expert"].rearrange("a g e -> a (g e)").to_broadcast([P, NE])).then_inc(s_router, 16)
            pool.dma_start(gain, a["norm_ffn"].to_broadcast([P, D])).then_inc(s_gffn, 16)
            pool.wait_ge(psum_full, full(f"PV{H - 1}"))
            pool.wait_ge(s_stage, 64)
            for i, (t0, tn) in enumerate(TILES):
                pool.dma_start(xtile[0:tn, i, :], x_src[i]).then_inc(s_xagain, 16)
            pool.wait_ge(hg_ready, 12)
            pool.dma_start(gain, a["norm_final"].rearrange("(a d) -> a d", a=1).to_broadcast([P, D])).then_inc(s_gfin, 16)

        @block.tensor
        def _(pe):
            def wait_weights(n):
                pe.wait_ge(slot_full[n % SLOTS], slot_count(n))

            pe.wait_ge(s_const, 16)
            pe.wait_ge(s_par, 16 * 7)
            pe.transpose(claim(pe, "par")[:, 0:P_ALL], par_rows, ident[0:P_ALL, 0:P_ALL]).then_inc(psum_full, 1)
            for i, (t0, tn) in enumerate(TILES):
                pe.wait_ge(x_scaled, i + 1)
                for k in range(4):
                    b = claim(pe, f"xt{i}_{k}")
                    for c in range(4):
                        f = P * (4 * k + c)
                        last = pe.transpose(b[:, c * tn:(c + 1) * tn], xnorm[0:tn, i % 2, f:f + P], ident[0:tn, 0:tn])
                    last.then_inc(psum_full, 1)

            def project(name, n, col, width=P):
                b = claim(pe, name)
                w = wslot(n)[:, 0:KC * (256 if width == P else width)].rearrange("p (c n) -> p c n", c=KC)
                for c in range(KC):
                    last = pe.matmul(b[0:width, 0:T], w[:, c, col:col + width], xT[:, c, :], start=c == 0, stop=c == KC - 1)
                last.then_inc(psum_full, 1)

            def sum_squares(src, count):
                for m in range(count):
                    last = pe.matmul(ps[:, SSQ_BANK, 0:T], ones[:, :], src[:, m, :], start=m == 0, stop=m == count - 1)
                last.then_inc(ssq_full, 1)

            pe.wait_ge(drained["dve"], drain_count["xt2_3"])
            for m in range(LC):
                if m % 2 == 0:
                    wait_weights(W_CQ + m // 2)
                project(f"cq{m}", W_CQ + m // 2, P * (m % 2))
            for m in range(LC):
                if m % 2 == 0:
                    wait_weights(W_KV + m // 2)
                project(f"ckv{m}", W_KV + m // 2, P * (m % 2))
                if m == 0:
                    pe.wait_ge(s_ones, 2)
                    pe.wait_ge(drained["act"], drain_count["cq3"])
                    sum_squares(sq_q, LC)
            wait_weights(W_KR)
            project("kr", W_KR, 0, ROPE)
            pe.wait_ge(s_cache, 48)
            for i in range(2):
                b = claim(pe, f"cc{i}")
                for c in range(LC):
                    last = pe.transpose(b[:, P * c:P * (c + 1)], cstage[:, i, P * c:P * (c + 1)], ident)
                last.then_inc(psum_full, 1)
            b = claim(pe, "ckr")
            for i in range(2):
                last = pe.transpose(b[:, P * i:P * (i + 1)], ckrstage[:, i, :], ident)
            last.then_inc(psum_full, 1)
            pe.wait_ge(drained["act"], drain_count["ckv3"])
            pe.wait_ge(rooted, 1)
            sum_squares(sq_kv, LC)
            pe.wait_ge(drained["act"], drain_count["kr"])
            for name, col in (("krdup", C_DUP), ("krrot", C_DROT)):
                pe.matmul(claim(pe, name)[:, 0:T], const[0:ROPE, col:col + P], kraw, start=True, stop=True).then_inc(psum_full, 1)
            def conv_squares(c):
                pe.wait_ge(conv_squared, c + 1)
                last = pe.matmul(ps[:, ACC_BANK, 0:T], ones[:, :], sq[:, c % 2, :], start=c == 0, stop=c == NCH - 1)
                last.then_inc(conv_summed, 1)

            for j in range(NCH // 2):
                for k, name in enumerate("ChB"):
                    n = W_CONV + 3 * j + k
                    wait_weights(n)
                    for i in range(2):
                        project(f"{name}{2 * j + i}", n, P * i)
                        if j and k == 0:
                            conv_squares(2 * (j - 1) + i)
                if j == 0:
                    pe.wait_ge(normed, 2 * LC)
                    for i, (t0, tn) in enumerate(TILES):
                        b = claim(pe, f"okv{i}")
                        for m in range(LC):
                            last = pe.transpose(b[0:tn, P * m:P * (m + 1)], ckv[:, m, t0:t0 + tn], ident)
                        last.then_inc(psum_full, 1)
                    pe.wait_ge(kr_ready, 1)
                    b = claim(pe, "okr")
                    for i, (t0, tn) in enumerate(TILES):
                        last = pe.transpose(b[0:tn, ROPE * i:ROPE * (i + 1)], krt[0:ROPE, t0:t0 + tn], ident[0:ROPE, 0:ROPE])
                    last.then_inc(psum_full, 1)
            wait_weights(W_UV)
            wv = wslot(W_UV).rearrange("p (c n) -> p c n", c=LC)
            pe.wait_ge(drained["act"], drain_count["cc1"])
            for k, (k0, kn) in enumerate(KT):
                for v in range(2):
                    b = claim(pe, f"V{k}_{v}")
                    for c in range(LC):
                        last = pe.matmul(b[0:kn, :], ckv[:, c, k0:k0 + kn], wv[:, c, 512 * v:512 * v + 512], start=c == 0, stop=c == LC - 1)
                    last.then_inc(psum_full, 1)
                if k < 2:
                    conv_squares(NCH - 2 + k)
            pe.wait_ge(ulast_ready, 1)
            pe.transpose(claim(pe, "ulast")[0:32, 0:P], small[:, 0:32], ident).then_inc(psum_full, 1)

            def queries_and_keys(p):
                wait_weights(W_PAIR + p)
                wq = wslot(W_PAIR + p)[:, 0:1536].rearrange("p (c n) -> p c n", c=LC)
                wk = wslot(W_PAIR + p)[:, 1536:2560].rearrange("p (c n) -> p c n", c=LC)
                for i in range(2):
                    b = claim(pe, f"q{2 * p + i}")
                    for c in range(LC):
                        last = pe.matmul(b[:, 0:T], wq[:, c, QKD * i:QKD * i + NOPE], cq[:, c, :], start=c == 0, stop=c == LC - 1)
                    last.then_inc(psum_full, 1)
                b = claim(pe, f"qr{p}")
                for c in range(LC):
                    for i in range(2):
                        last = pe.matmul(b[64 * i:64 * i + 64, 0:T], wq[:, c, QKD * i + NOPE:QKD * (i + 1)], cq[:, c, :],
                                         start=c == 0, stop=c == LC - 1)
                last.then_inc(psum_full, 1)
                for i in range(2):
                    for s, (k0, kn) in enumerate(((0, 256), (256, 320))):
                        b = claim(pe, f"K{2 * p + i}_{s}")
                        for c in range(LC):
                            last = pe.matmul(b[:, 0:kn], wk[:, c, NOPE * i:NOPE * (i + 1)], ckv[:, c, k0:k0 + kn], start=c == 0, stop=c == LC - 1)
                        last.then_inc(psum_full, 1)
                pe.wait_ge(drained["act"], drain_count[f"qr{p}"])
                pe.matmul(claim(pe, f"qrot{p}")[:, 0:T], const[:, C_ROT:C_ROT + P], qraw, start=True, stop=True).then_inc(psum_full, 1)

            def scores(h):
                p, i = h // 2, h % 2
                q, k = qt[:, p % 2], kt[:, p % 2]
                pe.wait_ge(q_ready, p + 1)
                pe.wait_ge(drained["dve"], drain_count[f"K{h}_1"])

                def score(out, t0, tn, k0, kn):
                    pe.matmul(out, q[:, i, t0:t0 + tn], k[:, i, k0:k0 + kn], start=True, stop=False)
                    return pe.matmul(out, q[64 * i:64 * i + 64, 2, t0:t0 + tn], krt[64 * i:64 * i + 64, k0:k0 + kn], start=False, stop=True)

                b = claim(pe, f"S{h}a")
                score(b[:, 0:128], 0, 128, 0, 128)
                score(b[:, 128:384], 128, 128, 0, 256).then_inc(psum_full, 1)
                b = claim(pe, f"S{h}b")
                score(b[0:64, 0:320], 256, 64, 256, 320).then_inc(psum_full, 1)

            def head_squares(h):
                pe.wait_ge(drained["act"], drain_count[f"PV{h}"])
                if h == 0:
                    pe.wait_ge(rooted, 2)
                last = pe.matmul(ps[:, SSQ_BANK, 0:T], ones[:, :], sq[:, h % 2, :], start=h == 0, stop=h == H - 1)
                last.then_inc(ssq_full, 1)

            def attend(h):
                pe.wait_ge(p_ready, h + 1)
                b, pr = claim(pe, f"PT{h}a"), pb[h % 2]
                for k in range(3):
                    last = pe.transpose(b[:, P * k:P * (k + 1)], pr[:, P * k:P * (k + 1)], ident)
                last.then_inc(psum_full, 1)
                b = claim(pe, f"PT{h}b")
                for k in range(3):
                    kn = KT[2 + k][1]
                    last = pe.transpose(b[0:kn, 64 * k:64 * k + 64], pr[0:64, 384 + P * k:384 + P * k + kn], ident[0:64, 0:64])
                last.then_inc(psum_full, 1)
                b, pt = claim(pe, f"PV{h}"), ptb[h % 2]
                pe.wait_ge(drained["dve"], drain_count[f"PT{h}b"])
                v = vals[:, :, VD * h:VD * (h + 1)]
                pe.matmul(b[:, 0:128], v[:, 0, :], pt[:, 0:128], start=True, stop=True)
                for k in range(2):
                    pe.matmul(b[:, 128:256], v[:, k, :], pt[:, 128 * (k + 1):128 * (k + 2)], start=k == 0, stop=k == 1)
                for k in range(3):
                    kn = KT[2 + k][1]
                    last = pe.matmul(b[:, 256:320], v[0:kn, 2 + k, :], pt[0:kn, 384 + 64 * k:448 + 64 * k], start=k == 0, stop=k == 2)
                last.then_inc(psum_full, 1)
                if h:
                    head_squares(h - 1)

            pe.wait_ge(normed, 2 * LC)
            pe.wait_ge(kr_ready, 1)
            pe.wait_ge(drained["act"], drain_count["ckr"])
            queries_and_keys(0)
            for p in range(H // 2):
                scores(2 * p)
                scores(2 * p + 1)
                if p + 1 < H // 2:
                    queries_and_keys(p + 1)
                attend(2 * p)
                attend(2 * p + 1)
            head_squares(H - 1)

            def output(n):
                b = [claim(pe, f"wo{n}_{i}") for i in range(3)]
                for half in range(2):
                    wait_weights(W_O + 2 * n + half)
                    w = wslot(W_O + 2 * n + half).rearrange("p (c n) -> p c n", c=8)
                    if n == 0:
                        pe.wait_ge(normed, 16 + 8 * half)
                    for j in range(8):
                        c = 8 * (1 - half) + j
                        first, final = half == 0 and j == 0, half == 1 and j == 7
                        for i in range(2):
                            last = pe.matmul(b[i], mix[:, c, P * i:P * (i + 1)], w[:, j, :], start=first, stop=final)
                            if final:
                                last.then_inc(psum_full, 1)
                        if j % 2:
                            for k in range(2):
                                last = pe.matmul(b[2][64 * k:64 * k + 64, :], mix[:, c - 1 + k, 256:320], w[:, j - 1 + k, :],
                                                 start=half == 0 and j == 1, stop=final)
                            if final:
                                last.then_inc(psum_full, 1)
                            elif j == 7:
                                last.then_inc(wo_half_used, 1)

            def router_transpose(n, i):
                tn = TILES[i][1]
                pe.wait_ge(hg_ready, 3 * n + i + 1)
                b = claim(pe, f"rt{n}_{i}")
                for c in range(4):
                    last = pe.transpose(b[:, c * tn:(c + 1) * tn], xn[0:tn, i, 4 * n + c, :], ident[0:tn, 0:tn])
                last.then_inc(psum_full, 1)

            def router_logits(n, i):
                tn = TILES[i][1]
                pe.wait_ge(drained["act"], drain_count[f"rt{n}_{i}"])
                for c in range(4):
                    last = pe.matmul(ps[0:tn, ACC_BANK, 36 * i:36 * i + 36], rtb[(3 * n + i) % 2][:, c, 0:tn], wr[:, 4 * n + c, :],
                                     start=n == 0 and i == 0 and c == 0, stop=n == 3 and c == 3, skip_group_check=True)
                last.then_inc(logits_full, 1)

            def router(n):
                router_transpose(n, 0)
                router_transpose(n, 1)
                router_logits(n, 0)
                router_transpose(n, 2)
                router_logits(n, 1)
                router_logits(n, 2)

            for n in range(4):
                output(n)
                if n == 0:
                    pe.wait_ge(s_router, 160)
                    pe.wait_ge(rooted, 3)
                else:
                    router(n - 1)
            router(3)

            pe.wait_ge(hot_ready, 1)
            tri = const[:, C_TRI:C_TRI + P]
            b = ps[:, SSQ_BANK, :]
            pe.matmul(b[:, 0:32], tri, hot2[:, 0, :], start=True, stop=True)
            pe.matmul(b[:, 32:64], ones[:, :], hot2[:, 0, :], start=True, stop=False)
            pe.matmul(b[:, 32:64], tri, hot2[:, 1, :], start=False, stop=True)
            pe.matmul(b[0:64, 64:96], ones[:, 0:64], hot2[:, 0, :], start=True, stop=False)
            pe.matmul(b[0:64, 64:96], ones[:, 0:64], hot2[:, 1, :], start=False, stop=False)
            pe.matmul(b[0:64, 64:96], tri[0:64, 0:64], hot2[0:64, 2, :], start=False, stop=True)
            for i, (t0, tn) in enumerate(TILES):
                last = pe.matmul(b[:, 96:128], ones[0:tn, :], hot2[0:tn, i, :], start=i == 0, stop=i == 2)
            last.then_inc(route_pe, 1)

            pe.sem_inc(comb_full, 1)
            pe.wait_ge(routed, 3)
            with pe.Fori(0, NE) as e:
                first = pe.value_load(tables[0:1, 0, bass.ds(e, 1)], min_val=0, max_val=64)
                count = pe.value_load(tables[0:1, 1, bass.ds(e, 1)], min_val=1, max_val=MAXB)
                with pe.Fori(0, count) as k:
                    g = first + k
                    pe.wait_ge(pick_ready, g + 1)
                    for c in range(KC):
                        for i, (t0, tn) in enumerate(TILES):
                            last = pe.matmul(ps[:, 0, B * c:B * (c + 1)], xn[0:tn, i, c, :], pickr[0:tn, i, :], start=i == 0, stop=i == 2)
                    last.then_inc(gathered, 1)
                    pe.wait_ge(y_copied, g + 1)
                    for i, (t0, tn) in enumerate(TILES):
                        last = pe.transpose(ps[:, 3, t0:t0 + tn], gpick2[0:tn, i, :], ident[0:tn, 0:tn])
                    last.then_inc(gt_full, 1)
                    pe.wait_ge(xg_ready, g + 1)
                    for s in range(4):
                        pe.wait_ge(slot_full[s], e * 32 + (slot_count(W_END + s)))
                        w = ring[:, s, :].rearrange("p (m c n) -> p m c n", m=2, c=4)
                        for c in (0, 2):
                            for m in range(2):
                                for o in range(2):
                                    q = B * (2 * m + o)
                                    last = pe.matmul(ps[q:q + B, 1, :], xg[:, 4 * s + c + o, :], w[:, m, c + o, :],
                                                     start=s == 0 and c == 0, stop=s == 3 and c == 2)
                        last.then_inc(weights_used, 1)
                    pe.wait_ge(h_copied, g + 1)
                    for c in range(4):
                        last = pe.matmul(ps[:, 2, 64 * c:64 * c + 64], hsb[:, c, :], const[:, C_FOLD:C_FOLD + 64], start=True, stop=True)
                    last.then_inc(folded, 1)
                    pe.wait_ge(hT_ready, g + 2)
                    pe.wait_ge(gt_copied, g + 1)
                    for s in (4, 5):
                        pe.wait_ge(slot_full[s], e * 32 + (slot_count(W_END + s)))
                        w = ring[:, s, :].rearrange("p (c n) -> p c n", c=2)
                        for c in range(2):
                            for j in range(4):
                                last = pe.matmul(ps[B * j:B * (j + 1), 3, :], hT[:, 2 * (s - 4) + c, :], w[:, c, 512 * j:512 * j + 512],
                                                 start=s == 4 and c == 0, stop=s == 5 and c == 1)
                        last.then_inc(weights_used, 1)
                    pe.wait_ge(y_copied, g + 2)
                    for i, (t0, tn) in enumerate(TILES):
                        pe.wait_ge(comb_added, g * 3 + (i + 1))
                        for j in range(4):
                            last = pe.matmul(ps[0:tn, 4 + j, :], gT[B * j:B * (j + 1), t0:t0 + tn], ysb[B * j:B * (j + 1), :], start=True, stop=True)
                        last.then_inc(comb_full, 1)

        @block.scalar
        def _(act):
            def drain(name, ins):
                ins.then_inc(drained["act"], 1)

            act.wait_ge(psum_full, full("par"))
            drain("par", act.copy(par[:, :], bank("par")[:, 0:P_ALL]))
            act.wait_ge(s_ones, 2)
            for i, (t0, tn) in enumerate(TILES):
                act.wait_ge(s_x[i], 16)
                if i == 2:
                    act.wait_ge(psum_full, full("xt0_3"))
                act.activation(xnorm[0:tn, i % 2, :], xtile[0:tn, i, :], ACT.Square, accum_out=xss[0:tn, i:i + 1]).then_inc(x_squared, 1)
                act.wait_ge(x_squared, i + 1)
                act.activation(xsd[0:tn, i:i + 1], xss[0:tn, i:i + 1], ACT.Sqrt, bias=eps_col[0:tn, :], scale=1.0 / D).then_inc(x_rooted, 1)

            def root_of(which, src, width):
                act.activation(rs, src, ACT.Sqrt, bias=eps_col[:, :], scale=1.0 / width).then_inc(rooted, 1)

            def latent(name, dst, sqd):
                for m in range(LC):
                    act.wait_ge(psum_full, full(f"{name}{m}"))
                    act.copy(dst[:, m, 0:T], bank(f"{name}{m}")[:, 0:T])
                    drain("", act.activation(sqd[:, m, :], bank(f"{name}{m}")[:, 0:T], ACT.Square))

            latent("cq", cq, sq_q)
            act.wait_ge(ssq_full, 1)
            root_of("q", ps[:, SSQ_BANK, 0:T], QL)
            latent("ckv", ckv, sq_kv)
            act.wait_ge(psum_full, full("kr"))
            drain("kr", act.copy(kraw, bank("kr")[0:ROPE, 0:T]))
            for i in range(2):
                act.wait_ge(psum_full, full(f"cc{i}"))
                drain("cc", act.copy(ckv[:, :, T + P * i:T + P * (i + 1)], bank(f"cc{i}").rearrange("p (c k) -> p c k", c=LC)))
            act.wait_ge(psum_full, full("ckr"))
            drain("ckr", act.copy(krt[:, T:T + 256], bank("ckr")[:, 0:256]))
            act.wait_ge(ssq_full, 2)
            act.wait_ge(normed, LC)
            root_of("kv", ps[:, SSQ_BANK, 0:T], KL)

            def conv_square(c):
                act.wait_ge(drained["dve"], drain_count[f"B{c}"])
                if c >= 2:
                    act.wait_ge(conv_summed, c - 1)
                act.activation(sq[:, c % 2, :], mix[:, 8 + c, :], ACT.Square).then_inc(conv_squared, 1)

            for j in range(NCH // 2):
                for i in range(2):
                    act.wait_ge(psum_full, full(f"C{2 * j + i}"))
                    if j:
                        act.wait_ge(drained["dve"], drain_count[f"h{2 * (j - 1) + i}"])
                    drain("C", act.copy(csb[:, i, :], bank(f"C{2 * j + i}")[:, 0:T]))
                    if j:
                        conv_square(2 * (j - 1) + i)
                if j == 0:
                    for i, (t0, tn) in enumerate(TILES):
                        act.wait_ge(psum_full, full(f"okv{i}"))
                        drain("okv", act.copy(okv[0:tn, i, :], bank(f"okv{i}")[0:tn, :]))
                    act.wait_ge(psum_full, full("okr"))
                    act.copy(okr[:, 0:2, :], bank("okr")[:, 0:2 * ROPE].rearrange("p (i r) -> p i r", i=2))
                    drain("okr", act.copy(okr[0:64, 2, :], bank("okr")[0:64, 2 * ROPE:3 * ROPE]))
            act.wait_ge(s_out, 64)
            for k, (k0, kn) in enumerate(KT):
                for v in range(2):
                    act.wait_ge(psum_full, full(f"V{k}_{v}"))
                    drain("V", act.copy(vals[0:kn, k, 512 * v:512 * v + 512], bank(f"V{k}_{v}")[0:kn, :]))
                if k < 1:
                    conv_square(NCH - 2)
                    conv_square(NCH - 1)
            act.wait_ge(conv_summed, NCH)
            act.wait_ge(normed, 2 * LC)
            root_of("conv", ps[:, ACC_BANK, 0:T], CH)
            act.wait_ge(psum_full, full("ulast"))
            drain("ulast", act.copy(oul, bank("ulast")[0:32, 0:P]))

            def queries(p):
                for i in range(2):
                    act.wait_ge(psum_full, full(f"q{2 * p + i}"))
                    drain("q", act.copy(qt[:, p % 2, i, :], bank(f"q{2 * p + i}")[:, 0:T]))
                act.wait_ge(psum_full, full(f"qr{p}"))
                if p:
                    act.wait_ge(q_ready, p)
                drain("qr", act.copy(qraw, bank(f"qr{p}")[:, 0:T]))

            def exps(h):
                i, pr = h % 2, pb[h % 2]
                a_, b_ = bank(f"S{h}a"), bank(f"S{h}b")
                act.wait_ge(max_ready, h + 1)
                if h >= 2:
                    act.wait_ge(psum_full, full(f"PT{h - 2}b"))

                def e(out, src, r0, rn, col):
                    return act.activation(out, src, ACT.Exp, bias=nb_[i][r0:r0 + rn, col:col + 1], scale=SCALE,
                                          accum_out=sm[i][r0:r0 + rn, col:col + 1])
                e(pr[0:64, 0:64], a_[0:64, 0:64], 0, 64, 0)
                e(pr[64:128, 0:128], a_[64:128, 0:128], 64, 64, 0)
                e(pr[0:64, 128:320], a_[0:64, 128:320], 0, 64, 1)
                drain("Sa", e(pr[64:128, 128:384], a_[64:128, 128:384], 64, 64, 1))
                drain("Sb", e(pr[0:64, 384:704], b_[0:64, 0:320], 0, 64, 2))

            def head_out(h):
                act.wait_ge(psum_full, full(f"PV{h}"))
                b = bank(f"PV{h}")
                act.copy(mix[:, h, :], b[:, 0:T])
                if h >= 2:
                    act.wait_ge(ssq_full, 2 + h - 1)
                drain("PV", act.activation(sq[:, h % 2, :], b[:, 0:T], ACT.Square))

            queries(0)
            for p in range(H // 2):
                exps(2 * p)
                exps(2 * p + 1)
                if p + 1 < H // 2:
                    queries(p + 1)
                head_out(2 * p)
                head_out(2 * p + 1)
            act.wait_ge(ssq_full, 2 + H)
            act.wait_ge(normed, 16)
            root_of("attn", ps[:, SSQ_BANK, 0:T], H * VD)

            def squares(n):
                for i, (t0, tn) in enumerate(TILES):
                    act.wait_ge(drained["dve"], drain_count[f"wo{n}_{i}"])
                    if n or i:
                        act.wait_ge(h_squared, 3 * n + i)
                    act.activation(junk[0:tn, :], xtile[0:tn, i, 512 * n:512 * n + 512], ACT.Square,
                                   accum_out=hss[0:tn, i, n:n + 1]).then_inc(h_squared, 1)

            def router_copies(n):
                for i, (t0, tn) in enumerate(TILES):
                    act.wait_ge(psum_full, full(f"rt{n}_{i}"))
                    u = 3 * n + i
                    if u >= 2:
                        act.wait_ge(logits_full, u - 1)
                    drain("rt", act.copy(rtb[u % 2][:, :, 0:tn], bank(f"rt{n}_{i}")[:, 0:4 * tn].rearrange("p (c t) -> p c t", c=4)))

            for n in range(4):
                if n:
                    squares(n - 1)
                    router_copies(n - 1)
            squares(3)
            router_copies(3)
            act.wait_ge(route_in, 1)
            act.activation(hsd, hsum, ACT.Sqrt, bias=eps_col[:, :], scale=1.0 / D).then_inc(route_act, 1)
            act.wait_ge(route_in, 2)
            act.activation(gx, gx, ACT.Exp).then_inc(route_act, 1)
            act.wait_ge(route_in, 3)
            act.activation(ev, dv, ACT.Exp).then_inc(route_act, 1)

            act.sem_inc(y_copied, 1)
            act.wait_ge(routed, 3)
            with act.Fori(0, NE) as e:
                first = act.value_load(tables[0:1, 0, bass.ds(e, 1)], min_val=0, max_val=64)
                count = act.value_load(tables[0:1, 1, bass.ds(e, 1)], min_val=1, max_val=MAXB)
                with act.Fori(0, count) as k:
                    g = first + k
                    act.wait_ge(gathered, g + 1)
                    act.copy(xg.rearrange("p c s -> p (c s)"), ps[:, 0, :]).then_inc(xg_ready, 1)
                    act.wait_ge(gt_full, g + 1)
                    act.wait_ge(comb_full, g * 3 + 1)
                    act.copy(gT, ps[:, 3, 0:T]).then_inc(gt_copied, 1)
                    act.wait_ge(weights_used, g * 6 + 4)
                    act.copy(hsb.rearrange("p c q -> p q c"), ps[:, 1, :].rearrange("p (q c) -> p q c", c=4)).then_inc(h_copied, 1)
                    act.wait_ge(folded, g + 1)
                    act.wait_ge(hT_ready, g + 1)
                    act.activation(sil, ps[:, 2, 0:256].rearrange("p (c m s) -> p c m s", c=4, m=2)[:, :, 0, :], ACT.Silu).then_inc(silu_ready, 1)
                    act.wait_ge(weights_used, g * 6 + 6)
                    act.copy(ysb, ps[:, 3, :]).then_inc(y_copied, 1)

            last_block = act.value_load(tables[0:1, 0, NE - 1:NE], min_val=0, max_val=64)
            last_count = act.value_load(tables[0:1, 1, NE - 1:NE], min_val=1, max_val=MAXB)
            act.wait_ge(comb_added, (last_block + last_count) * 3 + 1)
            for i, (t0, tn) in enumerate(TILES):
                act.activation(r2[0:tn, D * i:D * (i + 1)], xtile[0:tn, i, :], ACT.Square, accum_out=xss[0:tn, i:i + 1]).then_inc(fin_squared, 1)
                act.wait_ge(fin_squared, i + 1)
                act.activation(xsd[0:tn, i:i + 1], xss[0:tn, i:i + 1], ACT.Sqrt, bias=eps_col[0:tn, :], scale=1.0 / D).then_inc(fin_rooted, 1)

        @block.vector
        def _(dve):
            step = [0]

            def link(ins):
                step[0] += 1
                ins.then_inc(dve_step, 1)
                dve.wait_ge(dve_step, step[0])

            def drain(name, ins):
                ins.then_inc(drained["dve"], 1)

            dve.memset(ones[:, :], 1.0).then_inc(s_ones, 1)
            dve.memset(eps_col, EPS).then_inc(s_ones, 1)

            def scale_x(i):
                tn = TILES[i][1]
                dve.wait_ge(x_rooted, i + 1)
                link(dve.reciprocal(xrs[0:tn, i:i + 1], xsd[0:tn, i:i + 1]))
                dve.tensor_scalar(xnorm[0:tn, i % 2, :], xtile[0:tn, i, :], xrs[0:tn, i:i + 1], None, ALU.mult).then_inc(x_scaled, 1)

            def xT_tile(i):
                t0, tn = TILES[i]
                for k in range(4):
                    dve.wait_ge(psum_full, full(f"xt{i}_{k}"))
                    drain("xt", dve.tensor_tensor(
                        xT[:, 4 * k:4 * k + 4, t0:t0 + tn], bank(f"xt{i}_{k}")[:, 0:4 * tn].rearrange("p (c t) -> p c t", c=4),
                        par[:, P_MIX + 4 * k:P_MIX + 4 * k + 4].unsqueeze(2).to_broadcast([P, 4, tn]), ALU.mult))

            scale_x(0)
            scale_x(1)
            dve.wait_ge(drained["act"], drain_count["par"])
            xT_tile(0)
            scale_x(2)
            xT_tile(1)
            xT_tile(2)

            def scale_chunks(which, chunks, gains):
                dve.wait_ge(rooted, which)
                link(dve.reciprocal(rs, rs))
                for m, dst in enumerate(chunks):
                    dve.scalar_tensor_tensor(dst, dst, par[:, gains + m:gains + m + 1], rs, ALU.mult, ALU.mult).then_inc(normed, 1)

            def rotate(out, plain, swapped, a_, b_, name):
                if name == "krrot":
                    dve.wait_ge(psum_full, full("krdup"))
                    drain("krdup", dve.tensor_tensor(a_, plain, cos, ALU.mult))
                else:
                    link(dve.tensor_tensor(a_, plain, cos, ALU.mult))
                dve.wait_ge(psum_full, full(name))
                drain(name, dve.tensor_tensor(b_, swapped, sin, ALU.mult))
                dve.wait_ge(drained["dve"], drain_count[name])
                return dve.tensor_tensor(out, a_, b_, ALU.add)

            scale_chunks(1, [cq[:, m, :] for m in range(LC)], P_Q)
            rotate(krt[:, 0:T], bank("krdup")[:, 0:T], bank("krrot")[:, 0:T], rot_a, rot_b, "krrot").then_inc(kr_ready, 1)
            scale_chunks(2, [ckv[:, m, 0:T] for m in range(LC)], P_KV)

            link(dve.memset(uext[:, :, 0:2], 0.0))
            for k in range(2):
                link(dve.tensor_copy(uext[:, :, SEQ + 2 + k], par[:, P_ST + NCH * k:P_ST + NCH * (k + 1)]))

            def conv_input(c):
                dve.wait_ge(psum_full, full(f"h{c}"))
                dve.wait_ge(drained["act"], drain_count[f"C{c}"])
                b = bank(f"h{c}")
                link(dve.tensor_tensor(uext[:, c, 2:SEQ + 2], b[:, 0:SEQ], csb[:, c % 2, 0:SEQ], ALU.mult))
                drain("h", dve.tensor_tensor(uext[:, c, SEQ + 4:UE], b[:, SEQ:T], csb[:, c % 2, SEQ:T], ALU.mult))
                dve.wait_ge(drained["dve"], drain_count[f"h{c}"])

            def conv(c):
                tap = [par[:, P_CONV + NCH * j + c:P_CONV + NCH * j + c + 1] for j in range(3)]
                link(dve.tensor_scalar(cv, uext[:, c, 2:UE], tap[2], None, ALU.mult))
                for j in (1, 0):
                    link(dve.scalar_tensor_tensor(cv, uext[:, c, j:j + UE - 2], tap[j], cv, ALU.mult, ALU.add))
                dve.wait_ge(psum_full, full(f"B{c}"))
                b = bank(f"B{c}")
                link(dve.tensor_tensor(mix[:, 8 + c, 0:SEQ], b[:, 0:SEQ], cv[:, 0:SEQ], ALU.mult))
                drain("B", dve.tensor_tensor(mix[:, 8 + c, SEQ:T], b[:, SEQ:T], cv[:, SEQ + 2:UE - 2], ALU.mult))
                dve.wait_ge(drained["dve"], drain_count[f"B{c}"])

            for j in range(NCH // 2):
                for c in (2 * j, 2 * j + 1):
                    conv_input(c)
                for c in (2 * j, 2 * j + 1):
                    conv(c)
            link(dve.tensor_copy(ulast[:, 0:2, :], uext[:, :, SEQ:SEQ + 2].rearrange("p c k -> p k c")))
            dve.tensor_copy(ulast[:, 2:4, :], uext[:, :, UE - 2:UE].rearrange("p c k -> p k c")).then_inc(ulast_ready, 1)
            dve.wait_ge(ulast_ready, 1)
            for k in range(2):
                link(dve.memset(pb[k][0:64, 64:128], 0.0))
                link(dve.memset(pb[k][0:64, 320:384], 0.0))
                link(dve.memset(mx[k], 0.0))
                link(dve.memset(sm[k], 1.0))
            scale_chunks(3, [mix[:, 8 + c, :] for c in range(NCH)], P_CO)

            def keys(p):
                for i in range(2):
                    for s, (k0, kn) in enumerate(((0, 256), (256, 320))):
                        name = f"K{2 * p + i}_{s}"
                        dve.wait_ge(psum_full, full(name))
                        drain(name, dve.tensor_copy(kt[:, p % 2, i, k0:k0 + kn], bank(name)[:, 0:kn]))
                dve.wait_ge(drained["act"], drain_count[f"qr{p}"])
                rotate(qt[:, p % 2, 2, :], qraw, bank(f"qrot{p}")[:, 0:T], att_a, att_b, f"qrot{p}").then_inc(q_ready, 1)

            def maxima(h):
                i = h % 2
                a_, b_ = bank(f"S{h}a"), bank(f"S{h}b")
                dve.wait_ge(psum_full, full(f"S{h}b"))
                for out, src in ((mx[i][0:64, 0:1], a_[0:64, 0:64]), (mx[i][64:128, 0:1], a_[64:128, 0:128]),
                                 (mx[i][0:64, 1:2], a_[0:64, 128:320]), (mx[i][64:128, 1:2], a_[64:128, 128:384])):
                    dve.tensor_reduce(out, src, AX, ALU.max)
                link(dve.tensor_reduce(mx[i][0:64, 2:3], b_[0:64, 0:320], AX, ALU.max))
                dve.tensor_scalar(nb_[i], mx[i], -SCALE, None, ALU.mult).then_inc(max_ready, 1)

            def normalise(h):
                i, pr = h % 2, pb[h % 2]
                dve.wait_ge(drained["act"], drain_count[f"S{h}b"])
                link(dve.reciprocal(sm[i], sm[i]))
                dve.tensor_scalar(pr[:, 0:128], pr[:, 0:128], sm[i][:, 0:1], None, ALU.mult)
                dve.tensor_scalar(pr[:, 128:384], pr[:, 128:384], sm[i][:, 1:2], None, ALU.mult)
                dve.tensor_scalar(pr[0:64, 384:704], pr[0:64, 384:704], sm[i][0:64, 2:3], None, ALU.mult).then_inc(p_ready, 1)

            def probs_T(h):
                pt = ptb[h % 2]
                dve.wait_ge(psum_full, full(f"PT{h}a"))
                drain("PTa", dve.tensor_copy(pt[:, 0:384], bank(f"PT{h}a")[:, 0:384]))
                dve.wait_ge(psum_full, full(f"PT{h}b"))
                dve.tensor_copy(pt[:, 384:512], bank(f"PT{h}b")[:, 0:128])
                drain("PTb", dve.tensor_copy(pt[0:64, 512:576], bank(f"PT{h}b")[0:64, 128:192]))

            keys(0)
            for p in range(H // 2):
                for h in (2 * p, 2 * p + 1):
                    maxima(h)
                for h in (2 * p, 2 * p + 1):
                    normalise(h)
                if p + 1 < H // 2:
                    keys(p + 1)
                for h in (2 * p, 2 * p + 1):
                    probs_T(h)
            scale_chunks(4, [mix[:, h, :] for h in range(H)], P_AO)

            dve.wait_ge(psum_full, full(f"PV{H - 1}"))
            link(dve.memset(work[:, 1024:2560], 0.0))
            dve.wait_ge(s_xagain, 48)
            dve.wait_ge(s_gffn, 16)
            for n in range(4):
                f = slice(512 * n, 512 * n + 512)
                for i, (t0, tn) in enumerate(TILES):
                    name = f"wo{n}_{i}"
                    dve.wait_ge(psum_full, full(name))
                    h, b = xtile[0:tn, i, f], bank(name)
                    if i < 2:
                        drain(name, dve.tensor_tensor(h, b, h, ALU.add))
                    else:
                        link(dve.tensor_tensor(h, b[0:64, :], h, ALU.add))
                        drain(name, dve.tensor_tensor(h, b[64:128, :], h, ALU.add))
                    dve.wait_ge(drained["dve"], drain_count[name])
                    dve.tensor_tensor(xn[0:tn, i, 4 * n:4 * n + 4, :].rearrange("t c q -> t q c"),
                                      h.rearrange("t (q c) -> t q c", c=4), gain[0:tn, f].rearrange("t (q c) -> t q c", c=4),
                                      ALU.mult).then_inc(hg_ready, 1)

            dve.wait_ge(h_squared, 12)
            dve.tensor_reduce(hsum, hss, AX, ALU.add).then_inc(route_in, 1)
            dve.wait_ge(route_act, 1)
            link(dve.reciprocal(hrs, hsd))
            link(dve.memset(lg, NEG))
            dve.wait_ge(logits_full, 12)
            for i, (t0, tn) in enumerate(TILES):
                b = ps[0:tn, ACC_BANK, 36 * i:36 * i + 36]
                for dst, c0, cn in ((lg, 0, G), (le, G, NE)):
                    link(dve.scalar_tensor_tensor(dst[0:tn, i, 0:cn], b[:, c0:c0 + cn], hrs[0:tn, i:i + 1],
                                                  brow[0:tn, c0:c0 + cn], ALU.mult, ALU.add))
            for i in range(3):
                link(dve.max(m8[:, i, :], lg[:, i, :]))
                link(dve.max_index(i8[:, 0, i, :], m8[:, i, :], lg[:, i, :]))
            dve.tensor_tensor(gx, lg[:, :, 0:G], m8[:, :, 0:1].to_broadcast([P, 3, G]), ALU.subtract).then_inc(route_in, 1)
            link(dve.tensor_copy(gidx, i8[:, 0, :, 0]))
            iota = const[:, C_IOTA:C_IOTA + NE]
            link(dve.tensor_tensor(ghot, iota[:, 0:G].unsqueeze(1).to_broadcast([P, 3, G]),
                                   gidx.unsqueeze(2).to_broadcast([P, 3, G]), ALU.is_equal))
            gsel = prod_flat[:, 0:96].rearrange("p (i g e) -> p i g e", i=3, g=G)
            link(dve.tensor_tensor(gsel, le.rearrange("p i (g e) -> p i g e", g=G),
                                   ghot.unsqueeze(3).to_broadcast([P, 3, G, EPG]), ALU.mult))
            link(dve.tensor_reduce(el, gsel.rearrange("p i g e -> p i e g"), AX, ALU.add))
            for i in range(3):
                link(dve.max(v8[:, i, :], el[:, i, :]))
                link(dve.max_index(i8[:, 1, i, :], v8[:, i, :], el[:, i, :]))
            dve.tensor_tensor(dv, v8[:, :, 1], v8[:, :, 0], ALU.subtract).then_inc(route_in, 1)
            link(dve.tensor_copy(eidx, i8[:, 1, :, 0:2]))
            link(dve.scalar_tensor_tensor(eid, gidx.unsqueeze(2).to_broadcast([P, 3, 2]), float(EPG), eidx, ALU.mult, ALU.add))
            link(dve.tensor_tensor(hot, iota.unsqueeze(1).unsqueeze(1).to_broadcast([P, 3, 2, NE]),
                                   eid.unsqueeze(3).to_broadcast([P, 3, 2, NE]), ALU.is_equal))
            dve.tensor_tensor(hot2, hot[:, :, 0, :], hot[:, :, 1, :], ALU.add).then_inc(hot_ready, 1)
            dve.wait_ge(route_act, 2)
            link(dve.tensor_reduce(gsum, gx, AX, ALU.add))
            link(dve.reciprocal(gp, gsum))
            dve.wait_ge(route_act, 3)
            link(dve.tensor_scalar(den, ev, 1.0, None, ALU.add))
            link(dve.reciprocal(rden, den))
            link(dve.tensor_tensor(gate[:, :, 0], gp, rden, ALU.mult))
            link(dve.tensor_tensor(gate[:, :, 1], gate[:, :, 0], ev, ALU.mult))
            dve.wait_ge(route_pe, 1)
            b = ps[:, SSQ_BANK, :]
            link(dve.tensor_tensor(cmp, b[:, 96:128].unsqueeze(2).to_broadcast([P, NE, MAXB - 1]),
                                   const[:, C_THR:C_THR + MAXB - 1].unsqueeze(1).to_broadcast([P, NE, MAXB - 1]), ALU.is_gt))
            link(dve.tensor_reduce(nblk, cmp, AX, ALU.add))
            link(dve.tensor_scalar(nblk, nblk, 1.0, None, ALU.add))
            link(dve.tensor_tensor_scan(sincl, nblk, nblk, 0.0, ALU.add, ALU.bypass))
            link(dve.tensor_tensor(sexcl, sincl, nblk, ALU.subtract))
            dve.tensor_copy(tables[0:1, 0, :], sexcl[0:1, :]).then_inc(routed, 1)
            dve.tensor_copy(tables[0:1, 1, :], nblk[0:1, :]).then_inc(routed, 1)
            dve.tensor_scalar(tables[0:1, 2, :], sexcl[0:1, :], 6.0, -6.0, ALU.mult, ALU.add).then_inc(routed, 1)
            link(dve.scalar_tensor_tensor(slot_of[:, 0:2, :], sexcl.unsqueeze(1).to_broadcast([P, 2, NE]), float(B),
                                          b[:, 0:64].rearrange("p (i e) -> p i e", i=2), ALU.mult, ALU.add))
            link(dve.scalar_tensor_tensor(slot_of[0:64, 2, :], sexcl[0:64, :], float(B), b[0:64, 64:96], ALU.mult, ALU.add))
            for k in range(2):
                link(dve.tensor_tensor(prod[:, :, k, :], hot[:, :, k, :], slot_of, ALU.mult))
            link(dve.tensor_reduce(dest, prod, AX, ALU.add))

            def pick_tokens(link):
                link(dve.tensor_tensor(eq, iota.unsqueeze(1).unsqueeze(1).to_broadcast([P, 3, 2, B]),
                                       dest.unsqueeze(3).to_broadcast([P, 3, 2, B]), ALU.is_equal))
                link(dve.tensor_tensor(pick, eq[:, :, 0, :], eq[:, :, 1, :], ALU.add))
                link(dve.tensor_tensor(geq, eq, gate.unsqueeze(3).to_broadcast([P, 3, 2, B]), ALU.mult))
                link(dve.tensor_tensor(gpick, geq[:, :, 0, :].unsqueeze(2).to_broadcast([P, 3, 4, B]),
                                       geq[:, :, 1, :].unsqueeze(2).to_broadcast([P, 3, 4, B]), ALU.add))
                dve.tensor_tensor(pickr, pick, hrs.unsqueeze(2).to_broadcast([P, 3, B]), ALU.mult).then_inc(pick_ready, 1)

            pick_tokens(link)
            links = 5
            dve.sem_inc(comb_added, 1)
            dve.sem_inc(hT_ready, 1)
            dve.wait_ge(routed, 3)
            with dve.Fori(0, NE) as e:
                first = dve.value_load(tables[0:1, 0, bass.ds(e, 1)], min_val=0, max_val=64)
                count = dve.value_load(tables[0:1, 1, bass.ds(e, 1)], min_val=1, max_val=MAXB)
                with dve.Fori(0, count) as k:
                    g = first + k
                    done = [0]

                    def link_block(ins):
                        done[0] += 1
                        ins.then_inc(blk_step, 1)
                        dve.wait_ge(blk_step, g * links + done[0])

                    dve.wait_ge(silu_ready, g + 1)
                    dve.tensor_tensor(hT, sil, ps[:, 2, 0:256].rearrange("p (c m s) -> p c m s", c=4, m=2)[:, :, 1, :],
                                      ALU.mult).then_inc(hT_ready, 1)
                    dve.wait_ge(gt_full, g + 1)
                    link_block(dve.tensor_scalar(dest, dest, float(-B), None, ALU.add))
                    pick_tokens(link_block)
                    assert done[0] == links
                    for i, (t0, tn) in enumerate(TILES):
                        dve.wait_ge(comb_full, g * 3 + (i + 2))
                        h = xtile[0:tn, i, :].rearrange("t (j n) -> t j n", j=4)
                        dve.tensor_tensor(h, ps[0:tn, 4:8, :], h, ALU.add).then_inc(comb_added, 1)

            dve.wait_ge(s_gfin, 16)
            for i, (t0, tn) in enumerate(TILES):
                dve.wait_ge(fin_rooted, i + 1)
                link(dve.reciprocal(xrs[0:tn, i:i + 1], xsd[0:tn, i:i + 1]))
                dve.scalar_tensor_tensor(xtile[0:tn, i, :], xtile[0:tn, i, :], xrs[0:tn, i:i + 1], gain[0:tn, :],
                                         ALU.mult, ALU.mult).then_inc(fin_ready, 1)


def shape_constants():
    import numpy as np

    c = np.zeros((P, C_ALL), np.float32)
    c[:, C_ID:C_ID + P] = np.eye(P)
    half = ROPE // 2
    swap = np.zeros((ROPE, ROPE), np.float32)
    swap[np.arange(half) + half, np.arange(half)] = -1
    swap[np.arange(half), np.arange(half) + half] = 1
    for i in range(2):
        s = slice(ROPE * i, ROPE * (i + 1))
        c[s, C_ROT + ROPE * i:C_ROT + ROPE * (i + 1)] = swap
        c[0:ROPE, C_DUP + ROPE * i:C_DUP + ROPE * (i + 1)] = np.eye(ROPE)
        c[0:ROPE, C_DROT + ROPE * i:C_DROT + ROPE * (i + 1)] = swap
    c[:, C_TRI:C_TRI + P] = np.triu(np.ones((P, P)), 1)
    for q in range(4):
        c[B * q + np.arange(B), C_FOLD + B * (q // 2) + np.arange(B)] = 1
    c[:, C_IOTA:C_IOTA + NE] = np.arange(NE)
    c[:, C_THR:C_THR + MAXB - 1] = B * np.arange(1, MAXB)
    inv = np.float32(10000.0) ** (-np.arange(0, ROPE, 2, dtype=np.float32) / np.float32(ROPE))
    angle = np.arange(T, dtype=np.float32)[None, :] * inv[:, None]
    c[:, C_COS:C_COS + T] = np.tile(np.cos(angle), (4, 1))
    c[:, C_SIN:C_SIN + T] = np.tile(np.sin(angle), (4, 1))
    return c


_INS = ["x_prompt", "x_sample", "cache_kv_latent", "cache_k_rope", "state_conv", "norm_mix", "w_in", "norm_q",
        "w_uq", "norm_kv", "w_uk", "w_uv", "conv_w", "norm_attn_out", "norm_conv_out", "w_o", "norm_ffn",
        "w_router_group", "b_router_group", "w_router_expert", "b_router_expert", "w_gate", "w_up", "w_down",
        "norm_final"]
_OUTS = {
    "y_prompt": (1, SEQ, D), "y_sample": (1, DEC, D),
    "kv_prompt": (1, 1, SEQ, KL), "kr_prompt": (1, 1, SEQ, ROPE), "conv_prompt": (1, 1, 2, CH),
    "kv_sample": (1, 1, DEC, KL), "kr_sample": (1, 1, DEC, ROPE), "conv_sample": (1, 1, 2, CH),
}


def kernel(**inputs):
    import numpy as np
    import concourse.bacc as bacc
    from concourse.bass_utils import run_bass_kernel_spmd

    nc = bacc.Bacc("TRN2", target_bir_lowering=False, num_devices=1)
    arrays = {f"in_{name}": np.ascontiguousarray(inputs[name]) for name in _INS}
    arrays["in_const"] = shape_constants()
    a = {name[3:]: nc.dram_tensor(name, v.shape, mybir.dt.from_np(v.dtype), kind="ExternalInput").ap()
         for name, v in arrays.items()}
    for name, shape in _OUTS.items():
        a[name] = nc.dram_tensor(f"out_{name}", shape, F32, kind="ExternalOutput").ap()
    trunk_layer_kernel(nc, a)
    r = run_bass_kernel_spmd(nc, [arrays], core_ids=[0])
    return tuple(r.results[0][f"out_{name}"] for name in _OUTS)
```

```python
from contextlib import ExitStack

import concourse.bass as bass
from concourse import mybir

F32 = mybir.dt.float32
I32 = mybir.dt.int32
U32 = mybir.dt.uint32
ALU = mybir.AluOpType
ACT = mybir.ActivationFunctionType
AX = mybir.AxisListType.X

P = 128
D = 2048
SEQ, DEC, PAST = 256, 64, 256
T = SEQ + DEC
TILES = ((0, 128), (128, 128), (256, 64))
CHUNK = 64
H = 8
NOPE, ROPE, VD = 128, 64, 128
QKD = NOPE + ROPE
QL, KL = 512, 512
CH = 1024
NCH = CH // P
KC = D // P
LC = QL // P
KEYS = T + PAST
G, EPG = 4, 8
NE = G * EPG
FF = 512
B = 32
MAXB = -(-T // B)
EPS = 1e-6
SCALE = float(QKD) ** -0.5
SLOTS = 6
SLOT = 4096
RB = 6
SSQ_BANK, ACC_BANK = 6, 7
NEG = -3.0e38

C_ID, C_ROT, C_TRI, C_DUP, C_DROT = 0, 128, 256, 384, 512
C_FOLD, C_THR, C_IOTA, C_COS = 640, 704, 704 + MAXB, 704 + MAXB + P
C_SIN = C_COS + T
C_ALL = C_SIN + T
P_MIX, P_Q, P_KV, P_CONV, P_AO, P_CO, P_ST = 0, 16, 20, 24, 48, 56, 64
P_ALL = 80

W_CQ, W_KV, W_KR, W_CONV, W_UV, W_PAIR, W_O = 0, 2, 4, 5, 17, 18, 22
W_END = 30

KT = ((0, 128), (128, 128), (256, 128), (384, 128), (512, 64))


def psum_jobs():
    jobs = [("par", "act")]
    jobs += [(f"xt{i}_{k}", "dve") for i in range(3) for k in range(4)]
    jobs += [(f"cq{m}", "act") for m in range(LC)] + [(f"ckv{m}", "act") for m in range(LC)]
    jobs += [("kr", "act"), ("cc0", "act"), ("cc1", "act"), ("ckr", "act"), ("krdup", "dve"), ("krrot", "dve")]
    for j in range(NCH // 2):
        jobs += [(f"C{2 * j + k}", "act") for k in range(2)]
        jobs += [(f"h{2 * j + k}", "dve") for k in range(2)]
        jobs += [(f"B{2 * j + k}", "dve") for k in range(2)]
        if j == 0:
            jobs += [("okv0", "act"), ("okv1", "act"), ("okv2", "act"), ("okr", "act")]
    jobs += [(f"V{t}_{v}", "act") for t in range(5) for v in range(2)]
    jobs += [("ulast", "act")]

    def pair_jobs(p):
        return ([(f"q{2 * p + i}", "act") for i in range(2)] + [(f"qr{p}", "act")]
                + [(f"K{2 * p + i}_{s}", "dve") for i in range(2) for s in range(2)] + [(f"qrot{p}", "dve")])

    jobs += pair_jobs(0)
    for p in range(H // 2):
        jobs += [(f"S{2 * p + i}{s}", "act") for i in range(2) for s in "ab"]
        if p + 1 < H // 2:
            jobs += pair_jobs(p + 1)
        for h in (2 * p, 2 * p + 1):
            jobs += [(f"PT{h}a", "dve"), (f"PT{h}b", "dve"), (f"PV{h}", "act")]
    for n in range(4):
        jobs += [(f"wo{n}_{i}", "dve") for i in range(3)]
        if n >= 1:
            jobs += [(f"rt{n - 1}_{i}", "act") for i in range(3)]
    jobs += [(f"rt3_{i}", "act") for i in range(3)]
    return jobs


def trunk_layer_kernel(nc: bass.Bass, a):
    jobs = psum_jobs()
    job_index = {name: i for i, (name, _) in enumerate(jobs)}
    drain_count = {}
    for name, engine in jobs:
        drain_count[name] = 1 + sum(1 for n, e in jobs[:job_index[name]] if e == engine)

    with ExitStack() as ctx:
        def sb(name, shape, dt=F32):
            return ctx.enter_context(nc.sbuf_tensor(name, shape, dt))

        def sem(name):
            return ctx.enter_context(nc.semaphore(name))

        ring = sb("ring", [P, SLOTS, SLOT])
        hreg = sb("hreg", [P, 3 * D])
        r2 = sb("r2", [P, 3 * D])
        mix = sb("mix", [P, KC, T])
        ckv = sb("ckv", [P, LC, KEYS])
        cq = sb("cq", [P, LC, T])
        krt = sb("krt", [P, KEYS])
        const = sb("const", [P, C_ALL])
        par = sb("par", [P, P_ALL])
        ones = sb("ones", [P, P])
        work = sb("work", [P, 5160])
        small = sb("small", [P, 64])
        tables = sb("tables", [1, 3, NE], I32)

        ps = ctx.enter_context(nc.psum_tensor("ps", [P, 8, 512], F32))

        ident = const[:, C_ID:C_ID + P]
        cos, sin = const[:, C_COS:C_COS + T], const[:, C_SIN:C_SIN + T]
        xtile = hreg[:, :].rearrange("p (i d) -> p i d", i=3)
        xT = r2[:, 0:KC * T].rearrange("p (c t) -> p c t", c=KC)
        xnorm = mix[:, :, :].rearrange("p c t -> p (c t)")[:, 0:2 * D].rearrange("p (i d) -> p i d", i=2)
        sq_q = mix[:, 0:4, :]
        sq_kv = mix[:, 4:8, :]
        cstage = work[:, 0:2 * KL].rearrange("p (i l) -> p i l", i=2)
        ckrstage = work[:, 1024:1280].rearrange("p (i r) -> p i r", i=2)
        csb = work[:, 0:2 * T].rearrange("p (i t) -> p i t", i=2)
        UE = T + 4
        uext = work[:, 640:640 + NCH * UE].rearrange("p (c u) -> p c u", c=NCH)
        cv = work[:, 3232:3232 + UE - 2]
        sq = work[:, 3554:3554 + 2 * T].rearrange("p (i t) -> p i t", i=2)
        rs = work[:, 4194:4194 + T]
        rot_a = work[:, 4514:4514 + T]
        rot_b = work[:, 4834:4834 + T]
        kraw = cv[0:ROPE, 0:T]
        ulast = small[:, 0:32].rearrange("p (r c) -> p r c", r=4)
        eps_col = small[:, 62:63]
        xss, xsd, xrs = small[:, 32:35], small[:, 35:38], small[:, 38:41]
        okv = hreg[:, 0:3 * KL].rearrange("p (i l) -> p i l", i=3)
        okr = hreg[:, 1536:1536 + 3 * ROPE].rearrange("p (i r) -> p i r", i=3)
        oul = hreg[0:32, 5120:5120 + P]
        par_rows = work[0:P_ALL, 1280:1280 + P]
        vals = hreg[:, 0:5 * CH].rearrange("p (k v) -> p k v", k=5)
        qt = r2[:, 0:1920].rearrange("p (b i t) -> p b i t", b=2, i=3)
        kt = r2[:, 1920:4224].rearrange("p (b i k) -> p b i k", b=2, i=2)
        qraw = r2[:, 4224:4544]
        att_a = r2[:, 4544:4864]
        att_b = r2[:, 4864:5184]
        pb = [work[:, 0:704], work[:, 704:1408]]
        ptb = [work[:, 1408:1984], work[:, 1984:2560]]
        mx = [small[:, 44 + 3 * k:47 + 3 * k] for k in range(2)]
        nb_ = [small[:, 50 + 3 * k:53 + 3 * k] for k in range(2)]
        sm = [small[:, 56 + 3 * k:59 + 3 * k] for k in range(2)]
        xn = r2[:, :].rearrange("p (i c q) -> p i c q", i=3, c=KC)
        wr = cq[:, :, :].rearrange("p c t -> p (c t)")[:, 0:KC * 36].rearrange("p (c e) -> p c e", c=KC)
        brow = cq[:, :, :].rearrange("p c t -> p (c t)")[:, 576:612]
        gain = ckv[:, :, :].rearrange("p c t -> p (c t)")[:, 0:D]
        rtb = [work[:, 2560:3072].rearrange("p (c t) -> p c t", c=4), work[:, 0:512].rearrange("p (c t) -> p c t", c=4)]
        junk = work[:, 512:1024]
        w0 = 1024
        hss = work[:, w0:w0 + 12].rearrange("p (i n) -> p i n", i=3)
        hsum, hsd, hrs = (work[:, w0 + 12 + 3 * k:w0 + 15 + 3 * k] for k in range(3))
        w0 += 24
        lg = work[:, w0:w0 + 24].rearrange("p (i g) -> p i g", i=3)
        le = work[:, w0 + 24:w0 + 120].rearrange("p (i e) -> p i e", i=3)
        m8 = work[:, w0 + 120:w0 + 144].rearrange("p (i e) -> p i e", i=3)
        v8 = work[:, w0 + 144:w0 + 168].rearrange("p (i e) -> p i e", i=3)
        el = work[:, w0 + 168:w0 + 192].rearrange("p (i e) -> p i e", i=3)
        gx = work[:, w0 + 192:w0 + 204].rearrange("p (i g) -> p i g", i=3)
        ghot = work[:, w0 + 204:w0 + 216].rearrange("p (i g) -> p i g", i=3)
        gidx, gsum, gp, dv, ev, den, rden = (work[:, w0 + 216 + 3 * k:w0 + 219 + 3 * k] for k in range(7))
        eidx = work[:, w0 + 240:w0 + 246].rearrange("p (i k) -> p i k", i=3)
        eid = work[:, w0 + 246:w0 + 252].rearrange("p (i k) -> p i k", i=3)
        gate = work[:, w0 + 252:w0 + 258].rearrange("p (i k) -> p i k", i=3)
        dest, rank, high, place, placex = (
            work[:, w0 + 258 + 6 * k:w0 + 264 + 6 * k].rearrange("p (i k) -> p i k", i=3) for k in range(5))
        w0 += 288
        hot = work[:, w0:w0 + 192].rearrange("p (i k e) -> p i k e", i=3, k=2)
        hot2 = work[:, w0 + 192:w0 + 288].rearrange("p (i e) -> p i e", i=3)
        slot_of = work[:, w0 + 288:w0 + 384].rearrange("p (i e) -> p i e", i=3)
        prod_flat = work[:, w0 + 384:w0 + 576]
        prod = work[:, w0 + 384:w0 + 576].rearrange("p (i k e) -> p i k e", i=3, k=2)
        cmp = work[:, w0 + 576:w0 + 576 + NE * (MAXB - 1)].rearrange("p (e j) -> p e j", e=NE)
        w0 += 576 + NE * (MAXB - 1)
        extra, xincl, xexcl = (work[:, w0 + NE * k:w0 + NE * k + NE] for k in range(3))
        w0 += 3 * NE
        i8 = sb("i8", [P, 2, 3, 8], U32)
        assert w0 <= 2560, w0
        mflat = mix[:, :, :].rearrange("p c t -> p (c t)")
        xg = mflat[:, 0:512].rearrange("p (c j s) -> p c j s", c=4, j=4)
        gsb = mflat[:, 512:1024]
        hsb = mflat[:, 1024:1536].rearrange("p (c q) -> p c q", c=4)
        hT = mflat[:, 1536:1664].rearrange("p (c s) -> p c s", c=4)
        sil = mflat[:, 1664:1792].rearrange("p (c s) -> p c s", c=4)
        yg = mflat[:, 1792:3840]
        gT = mflat[:, 3840:4160]
        xx = mflat[:, 4160:4672].rearrange("p (c j s) -> p c j s", c=4, j=4)
        gTx = mflat[0:B, 4672:4992]
        cqflat = cq[:, :, :].rearrange("p c t -> p (c t)")
        yx = [work[0:B, 0:512], work[0:B, 512:1024], cqflat[0:B, 0:512], cqflat[0:B, 512:1024]]
        eq = work[:, 2560:3328].rearrange("p (i k s) -> p i k s", i=3, k=2)
        pick = work[:, 3328:3712].rearrange("p (i s) -> p i s", i=3)
        pickr = work[:, 3712:4096].rearrange("p (i s) -> p i s", i=3)
        gpick = work[:, 4096:4480].rearrange("p (i s) -> p i s", i=3)
        eqx = work[:, 4480:4672].rearrange("p (i k s) -> p i k s", i=3, k=2)
        pickx = work[:, 4672:4768].rearrange("p (i s) -> p i s", i=3)
        pickrx = work[:, 4768:4864].rearrange("p (i s) -> p i s", i=3)
        gpickx = work[:, 4864:4960].rearrange("p (i s) -> p i s", i=3)

        s_const, s_par, s_cache = sem("s_const"), sem("s_par"), sem("s_cache")
        s_x = [sem(f"s_x{i}") for i in range(3)]
        slot_full = [sem(f"slot_full{i}") for i in range(SLOTS)]
        psum_full = sem("psum_full")
        drained = {"act": sem("drained_act"), "dve": sem("drained_dve")}
        s_ones = sem("s_ones")
        x_squared, x_rooted, x_scaled = sem("x_squared"), sem("x_rooted"), sem("x_scaled")
        ssq_full, rooted, normed = sem("ssq_full"), sem("rooted"), sem("normed")
        kr_ready, conv_squared = sem("kr_ready"), sem("conv_squared")
        ulast_ready = sem("ulast_ready")
        q_ready, max_ready, p_ready = sem("q_ready"), sem("max_ready"), sem("p_ready")
        wo_half_used = sem("wo_half_used")
        s_xagain, s_router, s_gffn, s_gfin = sem("s_xagain"), sem("s_router"), sem("s_gffn"), sem("s_gfin")
        hg_ready, h_squared, logits_full = sem("hg_ready"), sem("h_squared"), sem("logits_full")
        hot_ready, route_in, route_act, route_pe = sem("hot_ready"), sem("route_in"), sem("route_act"), sem("route_pe")
        routed = sem("routed")
        dve_step = sem("dve_step")
        conv_summed = sem("conv_summed")
        pick_ready, gathered, g_copied, transposed = sem("pick_ready"), sem("gathered"), sem("g_copied"), sem("transposed")
        xg_ready, weights_used, h_copied, folded = sem("xg_ready"), sem("weights_used"), sem("h_copied"), sem("folded")
        silu_ready, hT_ready, y_copied = sem("silu_ready"), sem("hT_ready"), sem("y_copied")
        gt_full, gt_copied, comb_full, comb_added = sem("gt_full"), sem("gt_copied"), sem("comb_full"), sem("comb_added")
        x_pick, x_gathered, x_copied, x_transposed = sem("x_pick"), sem("x_gathered"), sem("x_copied"), sem("x_transposed")
        x_ready, x_gu, x_hcopied, x_folded = sem("x_ready"), sem("x_gu"), sem("x_hcopied"), sem("x_folded")
        x_silu, x_hT, x_ycopied, extra_done = sem("x_silu"), sem("x_hT"), sem("x_ycopied"), sem("extra_done")
        x_gtfull, x_gtcopied, x_full, x_added = sem("x_gtfull"), sem("x_gtcopied"), sem("x_full"), sem("x_added")
        blk_step, x_step = sem("blk_step"), sem("x_step")
        fin_squared, fin_rooted, fin_ready = sem("fin_squared"), sem("fin_rooted"), sem("fin_ready")
        s_out, s_stage, s_final = sem("s_out"), sem("s_stage"), sem("s_final")

        xp, xs = a["x_prompt"][0], a["x_sample"][0]
        x_src = (xp[0:128, :], xp[128:256, :], xs)
        w_in = a["w_in"][0].rearrange("(c p) n -> p c n", p=P)
        w_uq = a["w_uq"][0].rearrange("(c p) n -> p c n", p=P)
        w_uk = a["w_uk"][0].rearrange("(c p) h n -> p c (h n)", p=P)
        w_uv = a["w_uv"][0].rearrange("(c p) h n -> p c (h n)", p=P)
        w_o = a["w_o"][0].rearrange("(c p) n -> p c n", p=P)

        def bank(name):
            return ps[:, job_index[name] % RB, :]

        def full(name):
            return job_index[name] + 1

        def claim(pe, name):
            n = job_index[name] - RB
            if n >= 0:
                before, engine = jobs[n]
                pe.wait_ge(drained[engine], drain_count[before])
            return bank(name)

        def slot_count(n):
            return 32 * (n // SLOTS + 1)

        def wslot(n):
            return ring[:, n % SLOTS, :]

        def phase1_weights():
            def cols(n, first, count, last):
                v = wslot(n)[:, 0:KC * count].rearrange("p (c n) -> p c n", c=KC)
                return n, [(v[:, k:k + 8, :], w_in[:, k:k + 8, first:first + count]) for k in (0, 8)], last

            for m in range(2):
                yield cols(W_CQ + m, 256 * m, 256, f"cq{2 * m + 1}")
            for m in range(2):
                yield cols(W_KV + m, QL + 256 * m, 256, f"ckv{2 * m + 1}")
            yield cols(W_KR, QL + KL, ROPE, "kr")
            base = QL + KL + ROPE
            for j in range(NCH // 2):
                for k, (first, job) in enumerate(((base + CH, "C"), (base + 2 * CH, "h"), (base, "B"))):
                    yield cols(W_CONV + 3 * j + k, first + 256 * j, 256, f"{job}{2 * j + 1}")
            v = wslot(W_UV).rearrange("p (c n) -> p c n", c=LC)
            yield W_UV, [(v[:, k:k + 2, :], w_uv[:, k:k + 2, :]) for k in (0, 2)], "V4_1"
            for p in range(H // 2):
                s = wslot(W_PAIR + p)
                yield W_PAIR + p, [
                    (s[:, 0:1536].rearrange("p (c n) -> p c n", c=LC), w_uq[:, :, 2 * QKD * p:2 * QKD * (p + 1)]),
                    (s[:, 1536:2560].rearrange("p (c n) -> p c n", c=LC), w_uk[:, :, 256 * p:256 * (p + 1)]),
                ], f"K{2 * p + 1}_1"
            for n in range(4):
                for half in range(2):
                    v = wslot(W_O + 2 * n + half).rearrange("p (c n) -> p c n", c=8)
                    k0 = 8 * (1 - half)
                    yield W_O + 2 * n + half, [
                        (v[:, k:k + 4, :], w_o[:, k0 + k:k0 + k + 4, 512 * n:512 * n + 512]) for k in (0, 4)
                    ], (f"half{n}" if half == 0 else f"wo{n}_2")

        w1 = list(phase1_weights())
        assert [n for n, _, _ in w1] == list(range(W_END))

        def expert_slot(i, gate_w, up_w, down_w):
            if i < 4:
                s = ring[:, i, :].rearrange("p (m c n) -> p m c n", m=2, c=4)
                return [(s[:, m], w[512 * i:512 * i + 512, :].rearrange("(p c) n -> p c n", c=4))
                        for m, w in enumerate((gate_w, up_w))]
            s = ring[:, i, :].rearrange("p (c n) -> p c n", c=2)
            v = down_w.rearrange("(p c) n -> p c n", c=4)
            return [(s[:, c], v[:, 2 * (i - 4) + c, :]) for c in range(2)]

        def wait_slot_free(sp, last):
            if last.startswith("half"):
                sp.wait_ge(wo_half_used, int(last[4:]) + 1)
            else:
                sp.wait_ge(psum_full, full(last))

        block = ctx.enter_context(nc.Block())

        @block.sync
        def _(sp):
            sp.dma_start(xtile[:, 0, :], x_src[0]).then_inc(s_x[0], 16)
            sp.dma_start(const[:, :], a["const"]).then_inc(s_const, 16)
            sp.dma_start(xtile[:, 1, :], x_src[1]).then_inc(s_x[1], 16)
            sp.dma_start(xtile[0:64, 2, :], x_src[2]).then_inc(s_x[2], 16)
            used_by = {n: last for n, _, last in w1}
            for n, parts, _ in w1:
                if n >= SLOTS:
                    wait_slot_free(sp, used_by[n - SLOTS])
                for dst, src in parts:
                    sp.dma_start(dst, src).then_inc(slot_full[n % SLOTS], 16)
            for i in range(SLOTS):
                wait_slot_free(sp, used_by[W_END - SLOTS + i])
                for dst, src in expert_slot(i, a["w_gate"][0, 0], a["w_up"][0, 0], a["w_down"][0, 0]):
                    sp.dma_start(dst, src).then_inc(slot_full[i], 16)
            sp.wait_ge(routed, 3)
            with sp.Fori(1, NE) as e:
                before = sp.value_load(tables[0:1, 0, bass.ds(e, 1)], min_val=0, max_val=64)
                sp.wait_ge(extra_done, before + 1)
                for i in range(SLOTS):
                    sp.wait_ge(weights_used, e * SLOTS + (i + 1 - SLOTS))
                    w = [a[k][0, bass.ds(e, 1)].rearrange("a b c -> (a b) c") for k in ("w_gate", "w_up", "w_down")]
                    for dst, src in expert_slot(i, *w):
                        sp.dma_start(dst, src).then_inc(slot_full[i], 16)
            for i, (t0, tn) in enumerate(TILES):
                sp.wait_ge(fin_ready, i + 1)
                out = a["y_prompt"][0][t0:t0 + tn, :] if i < 2 else a["y_sample"][0]
                sp.dma_start(out, xtile[0:tn, i, :]).then_inc(s_final, 16)
            sp.wait_ge(s_final, 48)
            sp.wait_ge(s_out, 64)
            sp.wait_ge(s_stage, 64)

        @block.gpsimd
        def _(pool):
            pool.dma_start(cstage, a["cache_kv_latent"][0, 0].rearrange("(i p) l -> p i l", p=P)).then_inc(s_cache, 16)
            for k in range(2):
                pool.dma_start(ckrstage[:, :, ROPE * k:ROPE * (k + 1)],
                               a["cache_k_rope"][0, 0].rearrange("(i p) r -> p i r", p=P)).then_inc(s_cache, 16)
            pool.wait_ge(drained["act"], drain_count["okr"])
            pool.dma_start(a["kv_prompt"][0, 0].rearrange("(i p) l -> p i l", p=P), okv[:, 0:2, :]).then_inc(s_out, 16)
            pool.dma_start(a["kv_sample"][0, 0], okv[0:64, 2, :]).then_inc(s_out, 16)
            pool.dma_start(a["kr_prompt"][0, 0].rearrange("(i p) r -> p i r", p=P), okr[:, 0:2, :]).then_inc(s_out, 16)
            pool.dma_start(a["kr_sample"][0, 0], okr[0:64, 2, :]).then_inc(s_out, 16)
            pool.wait_ge(drained["act"], drain_count["ulast"])
            for s, name in enumerate(("conv_prompt", "conv_sample")):
                for k in range(2):
                    r = 2 * s + k
                    pool.dma_start(a[name][0, 0, k:k + 1].rearrange("a (c p) -> (a c) p", p=P),
                                   hreg[8 * r:8 * r + 8, 5120:5120 + P]).then_inc(s_stage, 16)
            pool.wait_ge(psum_full, full(f"K{H - 1}_1"))
            for i in range(4):
                v = a["w_router_group"][0].rearrange("(i p c) e -> i p c e", p=P, c=4)
                pool.dma_start(wr[:, 4 * i:4 * i + 4, 0:G], v[i]).then_inc(s_router, 16)
                v = a["w_router_expert"][0].rearrange("(i p c) g e -> i p c (g e)", p=P, c=4)
                pool.dma_start(wr[:, 4 * i:4 * i + 4, G:G + NE], v[i]).then_inc(s_router, 16)
            pool.dma_start(brow[:, 0:G], a["b_router_group"].to_broadcast([P, G])).then_inc(s_router, 16)
            pool.dma_start(brow[:, G:G + NE],
                           a["b_router_expert"].rearrange("a g e -> a (g e)").to_broadcast([P, NE])).then_inc(s_router, 16)
            pool.dma_start(gain, a["norm_ffn"].to_broadcast([P, D])).then_inc(s_gffn, 16)
            pool.wait_ge(psum_full, full(f"PV{H - 1}"))
            pool.wait_ge(s_stage, 64)
            for i, (t0, tn) in enumerate(TILES):
                pool.dma_start(xtile[0:tn, i, :], x_src[i]).then_inc(s_xagain, 16)
            pool.wait_ge(hg_ready, 12)
            pool.dma_start(gain, a["norm_final"].rearrange("(a d) -> a d", a=1).to_broadcast([P, D])).then_inc(s_gfin, 16)

        @block.tensor
        def _(pe):
            def wait_weights(n):
                pe.wait_ge(slot_full[n % SLOTS], slot_count(n))

            pe.wait_ge(s_const, 16)
            pe.wait_ge(s_par, 16 * 7)
            pe.transpose(claim(pe, "par")[:, 0:P_ALL], par_rows, ident[0:P_ALL, 0:P_ALL]).then_inc(psum_full, 1)
            for i, (t0, tn) in enumerate(TILES):
                pe.wait_ge(x_scaled, i + 1)
                for k in range(4):
                    b = claim(pe, f"xt{i}_{k}")
                    for c in range(4):
                        f = P * (4 * k + c)
                        last = pe.transpose(b[:, c * tn:(c + 1) * tn], xnorm[0:tn, i % 2, f:f + P], ident[0:tn, 0:tn])
                    last.then_inc(psum_full, 1)

            def project(name, n, col, width=P):
                b = claim(pe, name)
                w = wslot(n)[:, 0:KC * (256 if width == P else width)].rearrange("p (c n) -> p c n", c=KC)
                for c in range(KC):
                    last = pe.matmul(b[0:width, 0:T], w[:, c, col:col + width], xT[:, c, :], start=c == 0, stop=c == KC - 1)
                last.then_inc(psum_full, 1)

            def sum_squares(src, count):
                for m in range(count):
                    last = pe.matmul(ps[:, SSQ_BANK, 0:T], ones[:, :], src[:, m, :], start=m == 0, stop=m == count - 1)
                last.then_inc(ssq_full, 1)

            pe.wait_ge(drained["dve"], drain_count["xt2_3"])
            for m in range(LC):
                if m % 2 == 0:
                    wait_weights(W_CQ + m // 2)
                project(f"cq{m}", W_CQ + m // 2, P * (m % 2))
            for m in range(LC):
                if m % 2 == 0:
                    wait_weights(W_KV + m // 2)
                project(f"ckv{m}", W_KV + m // 2, P * (m % 2))
                if m == 0:
                    pe.wait_ge(s_ones, 2)
                    pe.wait_ge(drained["act"], drain_count["cq3"])
                    sum_squares(sq_q, LC)
            wait_weights(W_KR)
            project("kr", W_KR, 0, ROPE)
            pe.wait_ge(s_cache, 48)
            for i in range(2):
                b = claim(pe, f"cc{i}")
                for c in range(LC):
                    last = pe.transpose(b[:, P * c:P * (c + 1)], cstage[:, i, P * c:P * (c + 1)], ident)
                last.then_inc(psum_full, 1)
            b = claim(pe, "ckr")
            for i in range(2):
                last = pe.transpose(b[:, P * i:P * (i + 1)], ckrstage[:, i, :], ident)
            last.then_inc(psum_full, 1)
            pe.wait_ge(drained["act"], drain_count["ckv3"])
            pe.wait_ge(rooted, 1)
            sum_squares(sq_kv, LC)
            pe.wait_ge(drained["act"], drain_count["kr"])
            for name, col in (("krdup", C_DUP), ("krrot", C_DROT)):
                pe.matmul(claim(pe, name)[:, 0:T], const[0:ROPE, col:col + P], kraw, start=True, stop=True).then_inc(psum_full, 1)
            def conv_squares(c):
                pe.wait_ge(conv_squared, c + 1)
                last = pe.matmul(ps[:, ACC_BANK, 0:T], ones[:, :], sq[:, c % 2, :], start=c == 0, stop=c == NCH - 1)
                last.then_inc(conv_summed, 1)

            for j in range(NCH // 2):
                for k, name in enumerate("ChB"):
                    n = W_CONV + 3 * j + k
                    wait_weights(n)
                    for i in range(2):
                        project(f"{name}{2 * j + i}", n, P * i)
                        if j and k == 0:
                            conv_squares(2 * (j - 1) + i)
                if j == 0:
                    pe.wait_ge(normed, 2 * LC)
                    for i, (t0, tn) in enumerate(TILES):
                        b = claim(pe, f"okv{i}")
                        for m in range(LC):
                            last = pe.transpose(b[0:tn, P * m:P * (m + 1)], ckv[:, m, t0:t0 + tn], ident)
                        last.then_inc(psum_full, 1)
                    pe.wait_ge(kr_ready, 1)
                    b = claim(pe, "okr")
                    for i, (t0, tn) in enumerate(TILES):
                        last = pe.transpose(b[0:tn, ROPE * i:ROPE * (i + 1)], krt[0:ROPE, t0:t0 + tn], ident[0:ROPE, 0:ROPE])
                    last.then_inc(psum_full, 1)
            wait_weights(W_UV)
            wv = wslot(W_UV).rearrange("p (c n) -> p c n", c=LC)
            pe.wait_ge(drained["act"], drain_count["cc1"])
            for k, (k0, kn) in enumerate(KT):
                for v in range(2):
                    b = claim(pe, f"V{k}_{v}")
                    for c in range(LC):
                        last = pe.matmul(b[0:kn, :], ckv[:, c, k0:k0 + kn], wv[:, c, 512 * v:512 * v + 512], start=c == 0, stop=c == LC - 1)
                    last.then_inc(psum_full, 1)
                if k < 2:
                    conv_squares(NCH - 2 + k)
            pe.wait_ge(ulast_ready, 1)
            pe.transpose(claim(pe, "ulast")[0:32, 0:P], small[:, 0:32], ident).then_inc(psum_full, 1)

            def queries_and_keys(p):
                wait_weights(W_PAIR + p)
                wq = wslot(W_PAIR + p)[:, 0:1536].rearrange("p (c n) -> p c n", c=LC)
                wk = wslot(W_PAIR + p)[:, 1536:2560].rearrange("p (c n) -> p c n", c=LC)
                for i in range(2):
                    b = claim(pe, f"q{2 * p + i}")
                    for c in range(LC):
                        last = pe.matmul(b[:, 0:T], wq[:, c, QKD * i:QKD * i + NOPE], cq[:, c, :], start=c == 0, stop=c == LC - 1)
                    last.then_inc(psum_full, 1)
                b = claim(pe, f"qr{p}")
                for c in range(LC):
                    for i in range(2):
                        last = pe.matmul(b[64 * i:64 * i + 64, 0:T], wq[:, c, QKD * i + NOPE:QKD * (i + 1)], cq[:, c, :],
                                         start=c == 0, stop=c == LC - 1)
                last.then_inc(psum_full, 1)
                for i in range(2):
                    for s, (k0, kn) in enumerate(((0, 256), (256, 320))):
                        b = claim(pe, f"K{2 * p + i}_{s}")
                        for c in range(LC):
                            last = pe.matmul(b[:, 0:kn], wk[:, c, NOPE * i:NOPE * (i + 1)], ckv[:, c, k0:k0 + kn], start=c == 0, stop=c == LC - 1)
                        last.then_inc(psum_full, 1)
                pe.wait_ge(drained["act"], drain_count[f"qr{p}"])
                pe.matmul(claim(pe, f"qrot{p}")[:, 0:T], const[:, C_ROT:C_ROT + P], qraw, start=True, stop=True).then_inc(psum_full, 1)

            def scores(h):
                p, i = h // 2, h % 2
                q, k = qt[:, p % 2], kt[:, p % 2]
                pe.wait_ge(q_ready, p + 1)
                pe.wait_ge(drained["dve"], drain_count[f"K{h}_1"])

                def score(out, t0, tn, k0, kn):
                    pe.matmul(out, q[:, i, t0:t0 + tn], k[:, i, k0:k0 + kn], start=True, stop=False)
                    return pe.matmul(out, q[64 * i:64 * i + 64, 2, t0:t0 + tn], krt[64 * i:64 * i + 64, k0:k0 + kn], start=False, stop=True)

                b = claim(pe, f"S{h}a")
                score(b[:, 0:128], 0, 128, 0, 128)
                score(b[:, 128:384], 128, 128, 0, 256).then_inc(psum_full, 1)
                b = claim(pe, f"S{h}b")
                score(b[0:64, 0:320], 256, 64, 256, 320).then_inc(psum_full, 1)

            def head_squares(h):
                pe.wait_ge(drained["act"], drain_count[f"PV{h}"])
                if h == 0:
                    pe.wait_ge(rooted, 2)
                last = pe.matmul(ps[:, SSQ_BANK, 0:T], ones[:, :], sq[:, h % 2, :], start=h == 0, stop=h == H - 1)
                last.then_inc(ssq_full, 1)

            def attend(h):
                pe.wait_ge(p_ready, h + 1)
                b, pr = claim(pe, f"PT{h}a"), pb[h % 2]
                for k in range(3):
                    last = pe.transpose(b[:, P * k:P * (k + 1)], pr[:, P * k:P * (k + 1)], ident)
                last.then_inc(psum_full, 1)
                b = claim(pe, f"PT{h}b")
                for k in range(3):
                    kn = KT[2 + k][1]
                    last = pe.transpose(b[0:kn, 64 * k:64 * k + 64], pr[0:64, 384 + P * k:384 + P * k + kn], ident[0:64, 0:64])
                last.then_inc(psum_full, 1)
                b, pt = claim(pe, f"PV{h}"), ptb[h % 2]
                pe.wait_ge(drained["dve"], drain_count[f"PT{h}b"])
                v = vals[:, :, VD * h:VD * (h + 1)]
                pe.matmul(b[:, 0:128], v[:, 0, :], pt[:, 0:128], start=True, stop=True)
                for k in range(2):
                    pe.matmul(b[:, 128:256], v[:, k, :], pt[:, 128 * (k + 1):128 * (k + 2)], start=k == 0, stop=k == 1)
                for k in range(3):
                    kn = KT[2 + k][1]
                    last = pe.matmul(b[:, 256:320], v[0:kn, 2 + k, :], pt[0:kn, 384 + 64 * k:448 + 64 * k], start=k == 0, stop=k == 2)
                last.then_inc(psum_full, 1)
                if h:
                    head_squares(h - 1)

            pe.wait_ge(normed, 2 * LC)
            pe.wait_ge(kr_ready, 1)
            pe.wait_ge(drained["act"], drain_count["ckr"])
            queries_and_keys(0)
            for p in range(H // 2):
                scores(2 * p)
                scores(2 * p + 1)
                if p + 1 < H // 2:
                    queries_and_keys(p + 1)
                attend(2 * p)
                attend(2 * p + 1)
            head_squares(H - 1)

            def output(n):
                b = [claim(pe, f"wo{n}_{i}") for i in range(3)]
                for half in range(2):
                    wait_weights(W_O + 2 * n + half)
                    w = wslot(W_O + 2 * n + half).rearrange("p (c n) -> p c n", c=8)
                    if n == 0:
                        pe.wait_ge(normed, 16 + 8 * half)
                    for j in range(8):
                        c = 8 * (1 - half) + j
                        first, final = half == 0 and j == 0, half == 1 and j == 7
                        for i in range(2):
                            last = pe.matmul(b[i], mix[:, c, P * i:P * (i + 1)], w[:, j, :], start=first, stop=final)
                            if final:
                                last.then_inc(psum_full, 1)
                        if j % 2:
                            for k in range(2):
                                last = pe.matmul(b[2][64 * k:64 * k + 64, :], mix[:, c - 1 + k, 256:320], w[:, j - 1 + k, :],
                                                 start=half == 0 and j == 1, stop=final)
                            if final:
                                last.then_inc(psum_full, 1)
                            elif j == 7:
                                last.then_inc(wo_half_used, 1)

            def router_transpose(n, i):
                tn = TILES[i][1]
                pe.wait_ge(hg_ready, 3 * n + i + 1)
                b = claim(pe, f"rt{n}_{i}")
                for c in range(4):
                    last = pe.transpose(b[:, c * tn:(c + 1) * tn], xn[0:tn, i, 4 * n + c, :], ident[0:tn, 0:tn])
                last.then_inc(psum_full, 1)

            def router_logits(n, i):
                tn = TILES[i][1]
                pe.wait_ge(drained["act"], drain_count[f"rt{n}_{i}"])
                for c in range(4):
                    last = pe.matmul(ps[0:tn, ACC_BANK, 36 * i:36 * i + 36], rtb[(3 * n + i) % 2][:, c, 0:tn], wr[:, 4 * n + c, :],
                                     start=n == 0 and i == 0 and c == 0, stop=n == 3 and c == 3, skip_group_check=True)
                last.then_inc(logits_full, 1)

            def router(n):
                router_transpose(n, 0)
                router_transpose(n, 1)
                router_logits(n, 0)
                router_transpose(n, 2)
                router_logits(n, 1)
                router_logits(n, 2)

            for n in range(4):
                output(n)
                if n == 0:
                    pe.wait_ge(s_router, 160)
                    pe.wait_ge(rooted, 3)
                else:
                    router(n - 1)
            router(3)

            pe.wait_ge(hot_ready, 1)
            tri = const[:, C_TRI:C_TRI + P]
            b = ps[:, SSQ_BANK, :]
            pe.matmul(b[:, 0:32], tri, hot2[:, 0, :], start=True, stop=True)
            pe.matmul(b[:, 32:64], ones[:, :], hot2[:, 0, :], start=True, stop=False)
            pe.matmul(b[:, 32:64], tri, hot2[:, 1, :], start=False, stop=True)
            pe.matmul(b[0:64, 64:96], ones[:, 0:64], hot2[:, 0, :], start=True, stop=False)
            pe.matmul(b[0:64, 64:96], ones[:, 0:64], hot2[:, 1, :], start=False, stop=False)
            pe.matmul(b[0:64, 64:96], tri[0:64, 0:64], hot2[0:64, 2, :], start=False, stop=True)
            for i, (t0, tn) in enumerate(TILES):
                last = pe.matmul(b[:, 96:128], ones[0:tn, :], hot2[0:tn, i, :], start=i == 0, stop=i == 2)
            last.then_inc(route_pe, 1)

            def gather(pk, cols, signal):
                for i, (t0, tn) in enumerate(TILES):
                    for j in range(4):
                        last = pe.matmul(ps[B * j:B * (j + 1), 0, :], pk[0:tn, i, cols],
                                         xn[0:tn, i, 4 * j:4 * j + 4, :].rearrange("t c q -> t (c q)"), start=i == 0, stop=i == 2)
                last.then_inc(signal, 1)

            def gathered_T(signal):
                for c in range(4):
                    last = pe.transpose(ps[:, 1, P * c:P * (c + 1)], gsb[:, P * c:P * (c + 1)], ident)
                last.then_inc(signal, 1)

            def gates_T(src, width, signal):
                for i, (t0, tn) in enumerate(TILES):
                    last = pe.transpose(ps[0:width, 0, t0:t0 + tn], src[0:tn, i, :], ident[0:tn, 0:tn])
                last.then_inc(signal, 1)

            def gate_up(x, s):
                w = ring[:, s, :].rearrange("p (m c n) -> p m c n", m=2, c=4)
                for c in (0, 2):
                    for m in range(2):
                        for o in range(2):
                            r = B * (2 * m + o)
                            last = pe.matmul(ps[r:r + B, 2, :], x[:, c + o, s, :], w[:, m, c + o, :],
                                             start=s == 0 and c == 0, stop=s == 3 and c == 2)
                return last

            def fold(signal):
                for c in range(4):
                    last = pe.matmul(ps[:, 3, 64 * c:64 * c + 64], hsb[:, c, :], const[:, C_FOLD:C_FOLD + 64], start=True, stop=True)
                last.then_inc(signal, 1)

            def down(s):
                w = ring[:, s, :].rearrange("p (c n) -> p c n", c=2)
                for c in range(2):
                    for j in range(4):
                        last = pe.matmul(ps[B * j:B * (j + 1), 4, :], hT[:, 2 * (s - 4) + c, :], w[:, c, 512 * j:512 * j + 512],
                                         start=s == 4 and c == 0, stop=s == 5 and c == 1)
                return last

            def combine(gates, rows, full_sem, free_sem, value):
                for u in range(12):
                    i, n = u // 4, u % 4
                    t0, tn = TILES[i]
                    if u >= 3:
                        pe.wait_ge(free_sem, value(u - 2))
                    pe.matmul(ps[0:tn, 5 + u % 3, :], gates[:, t0:t0 + tn], rows[n], start=True, stop=True).then_inc(full_sem, 1)

            def extra_blocks(q, comb_before, e):
                count = pe.value_load(tables[0:1, 1, bass.ds(e, 1)], min_val=1, max_val=MAXB)
                with pe.If(count > 1):
                    before = pe.value_load(tables[0:1, 0, bass.ds(e, 1)], min_val=0, max_val=64)
                    with pe.Fori(1, count) as k:
                        x = before + k
                        pe.wait_ge(x_pick, x)
                        pe.wait_ge(gt_copied, q + 1)
                        gather(pickrx, slice(0, B), x_gathered)
                        pe.wait_ge(x_copied, x)
                        pe.wait_ge(xg_ready, e + 2)
                        gathered_T(x_transposed)
                        gates_T(gpickx, B, x_gtfull)
                        pe.wait_ge(x_ready, x)
                        for s in range(4):
                            last = gate_up(xx, s)
                        last.then_inc(x_gu, 1)
                        pe.wait_ge(x_hcopied, x)
                        fold(x_folded)
                        pe.wait_ge(x_hT, x)
                        pe.wait_ge(y_copied, e + 1)
                        for s in (4, 5):
                            last = down(s)
                        last.then_inc(extra_done, 1)
                        pe.wait_ge(x_ycopied, x)
                        pe.wait_ge(x_gtcopied, x)
                        pe.wait_ge(comb_added, comb_before)
                        pe.wait_ge(x_added, x * 12)
                        combine(gTx, yx, x_full, x_added, lambda v: x * 12 + v)

            pe.sem_inc(extra_done, 1)
            pe.wait_ge(pick_ready, 1)
            gather(pickr, slice(0, B), gathered)
            pe.wait_ge(g_copied, 1)
            gathered_T(transposed)
            pe.wait_ge(routed, 3)
            with pe.Fori(0, NE // 4) as q:
                comb_before = q * 12 + 1
                for b in range(4):
                    e = q * 4 + b
                    pe.wait_ge(xg_ready, e + 1)
                    for s in range(4):
                        pe.wait_ge(slot_full[s], e * 32 + slot_count(W_END + s))
                        gate_up(xg, s).then_inc(weights_used, 1)
                    if b == 3:
                        pe.wait_ge(pick_ready, q + 2)
                    cols = slice(B * ((b + 1) % 4), B * ((b + 1) % 4) + B)
                    if b == 1:
                        pe.wait_ge(gt_copied, q + 1)
                    gather(pickr, cols, gathered)
                    pe.wait_ge(h_copied, e + 1)
                    fold(folded)
                    pe.wait_ge(g_copied, e + 2)
                    gathered_T(transposed)
                    if b == 0:
                        gates_T(gpick, P, gt_full)
                    pe.wait_ge(hT_ready, e + 1)
                    for s in (4, 5):
                        pe.wait_ge(slot_full[s], e * 32 + slot_count(W_END + s))
                        if s == 4 and b:
                            pe.wait_ge(y_copied, e)
                        down(s).then_inc(weights_used, 1)
                    extra_blocks(q, comb_before, e)
                pe.wait_ge(y_copied, q * 4 + 4)
                pe.wait_ge(comb_added, comb_before)
                drained_extra = pe.value_load(tables[0:1, 2, bass.ds(q * 4 + 3, 1)], min_val=12, max_val=12 * 64)
                pe.wait_ge(x_added, drained_extra)
                combine(gT, [yg[:, 512 * n:512 * n + 512] for n in range(4)], comb_full, comb_added, lambda v: q * 12 + (v + 1))

        @block.scalar
        def _(act):
            def drain(name, ins):
                ins.then_inc(drained["act"], 1)

            loads = ((P_MIX, a["norm_mix"], 16), (P_Q, a["norm_q"], 4), (P_KV, a["norm_kv"], 4),
                     (P_AO, a["norm_attn_out"], 8), (P_CO, a["norm_conv_out"], 8))
            for first, src, n in loads:
                act.dma_start(par_rows[first:first + n, :], src.rearrange("a (c p) -> (a c) p", p=P)).then_inc(s_par, 16)
            act.dma_start(par_rows[P_CONV:P_CONV + 24, :],
                           a["conv_w"][0].rearrange("j (c p) -> (j c) p", p=P)).then_inc(s_par, 16)
            act.dma_start(par_rows[P_ST:P_ST + 16, :],
                           a["state_conv"][0, 0].rearrange("j (c p) -> (j c) p", p=P)).then_inc(s_par, 16)
            act.wait_ge(s_ones, 2)
            for i, (t0, tn) in enumerate(TILES):
                act.wait_ge(s_x[i], 16)
                if i == 2:
                    act.wait_ge(psum_full, full("xt0_3"))
                act.activation(xnorm[0:tn, i % 2, :], xtile[0:tn, i, :], ACT.Square, accum_out=xss[0:tn, i:i + 1]).then_inc(x_squared, 1)
                act.wait_ge(x_squared, i + 1)
                act.activation(xsd[0:tn, i:i + 1], xss[0:tn, i:i + 1], ACT.Sqrt, bias=eps_col[0:tn, :], scale=1.0 / D).then_inc(x_rooted, 1)

            act.wait_ge(psum_full, full("par"))
            drain("par", act.copy(par[:, :], bank("par")[:, 0:P_ALL]))

            def root_of(which, src, width):
                act.activation(rs, src, ACT.Sqrt, bias=eps_col[:, :], scale=1.0 / width).then_inc(rooted, 1)

            def latent(name, dst, sqd):
                for m in range(LC):
                    act.wait_ge(psum_full, full(f"{name}{m}"))
                    act.copy(dst[:, m, 0:T], bank(f"{name}{m}")[:, 0:T])
                    drain("", act.activation(sqd[:, m, :], bank(f"{name}{m}")[:, 0:T], ACT.Square))

            latent("cq", cq, sq_q)
            act.wait_ge(ssq_full, 1)
            root_of("q", ps[:, SSQ_BANK, 0:T], QL)
            latent("ckv", ckv, sq_kv)
            act.wait_ge(psum_full, full("kr"))
            drain("kr", act.copy(kraw, bank("kr")[0:ROPE, 0:T]))
            for i in range(2):
                act.wait_ge(psum_full, full(f"cc{i}"))
                drain("cc", act.copy(ckv[:, :, T + P * i:T + P * (i + 1)], bank(f"cc{i}").rearrange("p (c k) -> p c k", c=LC)))
            act.wait_ge(psum_full, full("ckr"))
            drain("ckr", act.copy(krt[:, T:T + 256], bank("ckr")[:, 0:256]))
            act.wait_ge(ssq_full, 2)
            act.wait_ge(normed, LC)
            root_of("kv", ps[:, SSQ_BANK, 0:T], KL)

            def conv_square(c):
                act.wait_ge(drained["dve"], drain_count[f"B{c}"])
                if c >= 2:
                    act.wait_ge(conv_summed, c - 1)
                act.activation(sq[:, c % 2, :], mix[:, 8 + c, :], ACT.Square).then_inc(conv_squared, 1)

            for j in range(NCH // 2):
                for i in range(2):
                    act.wait_ge(psum_full, full(f"C{2 * j + i}"))
                    if j:
                        act.wait_ge(drained["dve"], drain_count[f"h{2 * (j - 1) + i}"])
                    drain("C", act.copy(csb[:, i, :], bank(f"C{2 * j + i}")[:, 0:T]))
                    if j:
                        conv_square(2 * (j - 1) + i)
                if j == 0:
                    for i, (t0, tn) in enumerate(TILES):
                        act.wait_ge(psum_full, full(f"okv{i}"))
                        drain("okv", act.copy(okv[0:tn, i, :], bank(f"okv{i}")[0:tn, :]))
                    act.wait_ge(psum_full, full("okr"))
                    act.copy(okr[:, 0:2, :], bank("okr")[:, 0:2 * ROPE].rearrange("p (i r) -> p i r", i=2))
                    drain("okr", act.copy(okr[0:64, 2, :], bank("okr")[0:64, 2 * ROPE:3 * ROPE]))
            act.wait_ge(s_out, 64)
            for k, (k0, kn) in enumerate(KT):
                for v in range(2):
                    act.wait_ge(psum_full, full(f"V{k}_{v}"))
                    drain("V", act.copy(vals[0:kn, k, 512 * v:512 * v + 512], bank(f"V{k}_{v}")[0:kn, :]))
                if k < 1:
                    conv_square(NCH - 2)
                    conv_square(NCH - 1)
            act.wait_ge(conv_summed, NCH)
            act.wait_ge(normed, 2 * LC)
            root_of("conv", ps[:, ACC_BANK, 0:T], CH)
            act.wait_ge(psum_full, full("ulast"))
            drain("ulast", act.copy(oul, bank("ulast")[0:32, 0:P]))

            def queries(p):
                for i in range(2):
                    act.wait_ge(psum_full, full(f"q{2 * p + i}"))
                    drain("q", act.copy(qt[:, p % 2, i, :], bank(f"q{2 * p + i}")[:, 0:T]))
                act.wait_ge(psum_full, full(f"qr{p}"))
                if p:
                    act.wait_ge(q_ready, p)
                drain("qr", act.copy(qraw, bank(f"qr{p}")[:, 0:T]))

            def exps(h):
                i, pr = h % 2, pb[h % 2]
                a_, b_ = bank(f"S{h}a"), bank(f"S{h}b")
                act.wait_ge(max_ready, h + 1)
                if h >= 2:
                    act.wait_ge(psum_full, full(f"PT{h - 2}b"))

                def e(out, src, r0, rn, col):
                    return act.activation(out, src, ACT.Exp, bias=nb_[i][r0:r0 + rn, col:col + 1], scale=SCALE,
                                          accum_out=sm[i][r0:r0 + rn, col:col + 1])
                e(pr[0:64, 0:64], a_[0:64, 0:64], 0, 64, 0)
                e(pr[64:128, 0:128], a_[64:128, 0:128], 64, 64, 0)
                e(pr[0:64, 128:320], a_[0:64, 128:320], 0, 64, 1)
                drain("Sa", e(pr[64:128, 128:384], a_[64:128, 128:384], 64, 64, 1))
                drain("Sb", e(pr[0:64, 384:704], b_[0:64, 0:320], 0, 64, 2))

            def head_out(h):
                act.wait_ge(psum_full, full(f"PV{h}"))
                b = bank(f"PV{h}")
                act.copy(mix[:, h, :], b[:, 0:T])
                if h >= 2:
                    act.wait_ge(ssq_full, 2 + h - 1)
                drain("PV", act.activation(sq[:, h % 2, :], b[:, 0:T], ACT.Square))

            queries(0)
            for p in range(H // 2):
                exps(2 * p)
                exps(2 * p + 1)
                if p + 1 < H // 2:
                    queries(p + 1)
                head_out(2 * p)
                head_out(2 * p + 1)
            act.wait_ge(ssq_full, 2 + H)
            act.wait_ge(normed, 16)
            root_of("attn", ps[:, SSQ_BANK, 0:T], H * VD)

            def squares(n):
                for i, (t0, tn) in enumerate(TILES):
                    act.wait_ge(drained["dve"], drain_count[f"wo{n}_{i}"])
                    if n or i:
                        act.wait_ge(h_squared, 3 * n + i)
                    act.activation(junk[0:tn, :], xtile[0:tn, i, 512 * n:512 * n + 512], ACT.Square,
                                   accum_out=hss[0:tn, i, n:n + 1]).then_inc(h_squared, 1)

            def router_copies(n):
                for i, (t0, tn) in enumerate(TILES):
                    act.wait_ge(psum_full, full(f"rt{n}_{i}"))
                    u = 3 * n + i
                    if u >= 2:
                        act.wait_ge(logits_full, u - 1)
                    drain("rt", act.copy(rtb[u % 2][:, :, 0:tn], bank(f"rt{n}_{i}")[:, 0:4 * tn].rearrange("p (c t) -> p c t", c=4)))

            for n in range(4):
                if n:
                    squares(n - 1)
                    router_copies(n - 1)
            squares(3)
            router_copies(3)
            act.wait_ge(route_in, 1)
            act.activation(hsd, hsum, ACT.Sqrt, bias=eps_col[:, :], scale=1.0 / D).then_inc(route_act, 1)
            act.wait_ge(route_in, 2)
            act.activation(gx, gx, ACT.Exp).then_inc(route_act, 1)
            act.wait_ge(route_in, 3)
            act.activation(ev, dv, ACT.Exp).then_inc(route_act, 1)

            def copy_gathered(src_full, value, signal):
                act.wait_ge(src_full, value)
                act.copy(gsb, ps[:, 0, :]).then_inc(signal, 1)

            def copy_xT(dst, src_full, value, signal):
                act.wait_ge(src_full, value)
                act.copy(dst.rearrange("p c j s -> p (c j s)"), ps[:, 1, :]).then_inc(signal, 1)

            def copy_gate_up(signal):
                act.copy(hsb.rearrange("p c q -> p q c"), ps[:, 2, :].rearrange("p (q c) -> p q c", c=4)).then_inc(signal, 1)

            def silu(signal):
                act.activation(sil, ps[:, 3, 0:256].rearrange("p (c m s) -> p c m s", c=4, m=2)[:, :, 0, :], ACT.Silu).then_inc(signal, 1)

            def copy_result(rows, signal):
                for j in range(4):
                    last = act.copy(rows[j], ps[B * j:B * (j + 1), 4, :])
                last.then_inc(signal, 1)

            def extra_blocks(e):
                count = act.value_load(tables[0:1, 1, bass.ds(e, 1)], min_val=1, max_val=MAXB)
                with act.If(count > 1):
                    before = act.value_load(tables[0:1, 0, bass.ds(e, 1)], min_val=0, max_val=64)
                    with act.Fori(1, count) as k:
                        x = before + k
                        copy_gathered(x_gathered, x, x_copied)
                        copy_xT(xx, x_transposed, x, x_ready)
                        act.wait_ge(x_gtfull, x)
                        act.wait_ge(x_added, x * 12)
                        act.copy(gTx, ps[0:B, 0, 0:T]).then_inc(x_gtcopied, 1)
                        act.wait_ge(x_gu, x)
                        copy_gate_up(x_hcopied)
                        act.wait_ge(x_folded, x)
                        silu(x_silu)
                        act.wait_ge(extra_done, x + 1)
                        copy_result(yx, x_ycopied)

            copy_gathered(gathered, 1, g_copied)
            copy_xT(xg, transposed, 1, xg_ready)
            act.wait_ge(routed, 3)
            with act.Fori(0, NE // 4) as q:
                for b in range(4):
                    e = q * 4 + b
                    act.wait_ge(weights_used, e * 6 + 4)
                    copy_gate_up(h_copied)
                    copy_gathered(gathered, e + 2, g_copied)
                    act.wait_ge(folded, e + 1)
                    silu(silu_ready)
                    copy_xT(xg, transposed, e + 2, xg_ready)
                    if b == 0:
                        act.wait_ge(gt_full, q + 1)
                        act.wait_ge(comb_added, q * 12 + 1)
                        act.copy(gT, ps[:, 0, 0:T]).then_inc(gt_copied, 1)
                    act.wait_ge(weights_used, e * 6 + 6)
                    copy_result([yg[B * b:B * (b + 1), 512 * j:512 * j + 512] for j in range(4)], y_copied)
                    extra_blocks(e)

            act.wait_ge(comb_added, 12 * (NE // 4) + 1)
            used = act.value_load(tables[0:1, 2, NE - 1:NE], min_val=12, max_val=12 * 64)
            act.wait_ge(x_added, used)
            for i, (t0, tn) in enumerate(TILES):
                act.activation(r2[0:tn, D * i:D * (i + 1)], xtile[0:tn, i, :], ACT.Square, accum_out=xss[0:tn, i:i + 1]).then_inc(fin_squared, 1)
                act.wait_ge(fin_squared, i + 1)
                act.activation(xsd[0:tn, i:i + 1], xss[0:tn, i:i + 1], ACT.Sqrt, bias=eps_col[0:tn, :], scale=1.0 / D).then_inc(fin_rooted, 1)

        @block.vector
        def _(dve):
            step = [0]

            def link(ins):
                step[0] += 1
                ins.then_inc(dve_step, 1)
                dve.wait_ge(dve_step, step[0])

            def drain(name, ins):
                ins.then_inc(drained["dve"], 1)

            dve.memset(ones[:, :], 1.0).then_inc(s_ones, 1)
            dve.memset(eps_col, EPS).then_inc(s_ones, 1)

            def scale_x(i):
                tn = TILES[i][1]
                dve.wait_ge(x_rooted, i + 1)
                link(dve.reciprocal(xrs[0:tn, i:i + 1], xsd[0:tn, i:i + 1]))
                dve.tensor_scalar(xnorm[0:tn, i % 2, :], xtile[0:tn, i, :], xrs[0:tn, i:i + 1], None, ALU.mult).then_inc(x_scaled, 1)

            def xT_tile(i):
                t0, tn = TILES[i]
                for k in range(4):
                    dve.wait_ge(psum_full, full(f"xt{i}_{k}"))
                    drain("xt", dve.tensor_tensor(
                        xT[:, 4 * k:4 * k + 4, t0:t0 + tn], bank(f"xt{i}_{k}")[:, 0:4 * tn].rearrange("p (c t) -> p c t", c=4),
                        par[:, P_MIX + 4 * k:P_MIX + 4 * k + 4].unsqueeze(2).to_broadcast([P, 4, tn]), ALU.mult))

            scale_x(0)
            scale_x(1)
            dve.wait_ge(drained["act"], drain_count["par"])
            xT_tile(0)
            scale_x(2)
            xT_tile(1)
            xT_tile(2)

            def scale_chunks(which, chunks, gains):
                dve.wait_ge(rooted, which)
                link(dve.reciprocal(rs, rs))
                for m, dst in enumerate(chunks):
                    dve.scalar_tensor_tensor(dst, dst, par[:, gains + m:gains + m + 1], rs, ALU.mult, ALU.mult).then_inc(normed, 1)

            def rotate(out, plain, swapped, a_, b_, name):
                if name == "krrot":
                    dve.wait_ge(psum_full, full("krdup"))
                    drain("krdup", dve.tensor_tensor(a_, plain, cos, ALU.mult))
                else:
                    link(dve.tensor_tensor(a_, plain, cos, ALU.mult))
                dve.wait_ge(psum_full, full(name))
                drain(name, dve.tensor_tensor(b_, swapped, sin, ALU.mult))
                dve.wait_ge(drained["dve"], drain_count[name])
                return dve.tensor_tensor(out, a_, b_, ALU.add)

            scale_chunks(1, [cq[:, m, :] for m in range(LC)], P_Q)
            rotate(krt[:, 0:T], bank("krdup")[:, 0:T], bank("krrot")[:, 0:T], rot_a, rot_b, "krrot").then_inc(kr_ready, 1)
            scale_chunks(2, [ckv[:, m, 0:T] for m in range(LC)], P_KV)

            link(dve.memset(uext[:, :, 0:2], 0.0))
            for k in range(2):
                link(dve.tensor_copy(uext[:, :, SEQ + 2 + k], par[:, P_ST + NCH * k:P_ST + NCH * (k + 1)]))

            def conv_input(c):
                dve.wait_ge(psum_full, full(f"h{c}"))
                dve.wait_ge(drained["act"], drain_count[f"C{c}"])
                b = bank(f"h{c}")
                link(dve.tensor_tensor(uext[:, c, 2:SEQ + 2], b[:, 0:SEQ], csb[:, c % 2, 0:SEQ], ALU.mult))
                drain("h", dve.tensor_tensor(uext[:, c, SEQ + 4:UE], b[:, SEQ:T], csb[:, c % 2, SEQ:T], ALU.mult))
                dve.wait_ge(drained["dve"], drain_count[f"h{c}"])

            def conv(c):
                tap = [par[:, P_CONV + NCH * j + c:P_CONV + NCH * j + c + 1] for j in range(3)]
                link(dve.tensor_scalar(cv, uext[:, c, 2:UE], tap[2], None, ALU.mult))
                for j in (1, 0):
                    link(dve.scalar_tensor_tensor(cv, uext[:, c, j:j + UE - 2], tap[j], cv, ALU.mult, ALU.add))
                dve.wait_ge(psum_full, full(f"B{c}"))
                b = bank(f"B{c}")
                link(dve.tensor_tensor(mix[:, 8 + c, 0:SEQ], b[:, 0:SEQ], cv[:, 0:SEQ], ALU.mult))
                drain("B", dve.tensor_tensor(mix[:, 8 + c, SEQ:T], b[:, SEQ:T], cv[:, SEQ + 2:UE - 2], ALU.mult))
                dve.wait_ge(drained["dve"], drain_count[f"B{c}"])

            for j in range(NCH // 2):
                for c in (2 * j, 2 * j + 1):
                    conv_input(c)
                for c in (2 * j, 2 * j + 1):
                    conv(c)
            link(dve.tensor_copy(ulast[:, 0:2, :], uext[:, :, SEQ:SEQ + 2].rearrange("p c k -> p k c")))
            dve.tensor_copy(ulast[:, 2:4, :], uext[:, :, UE - 2:UE].rearrange("p c k -> p k c")).then_inc(ulast_ready, 1)
            dve.wait_ge(ulast_ready, 1)
            for k in range(2):
                link(dve.memset(pb[k][0:64, 64:128], 0.0))
                link(dve.memset(pb[k][0:64, 320:384], 0.0))
                link(dve.memset(mx[k], 0.0))
                link(dve.memset(sm[k], 1.0))
            scale_chunks(3, [mix[:, 8 + c, :] for c in range(NCH)], P_CO)

            def keys(p):
                for i in range(2):
                    for s, (k0, kn) in enumerate(((0, 256), (256, 320))):
                        name = f"K{2 * p + i}_{s}"
                        dve.wait_ge(psum_full, full(name))
                        drain(name, dve.tensor_copy(kt[:, p % 2, i, k0:k0 + kn], bank(name)[:, 0:kn]))
                dve.wait_ge(drained["act"], drain_count[f"qr{p}"])
                rotate(qt[:, p % 2, 2, :], qraw, bank(f"qrot{p}")[:, 0:T], att_a, att_b, f"qrot{p}").then_inc(q_ready, 1)

            def maxima(h):
                i = h % 2
                a_, b_ = bank(f"S{h}a"), bank(f"S{h}b")
                dve.wait_ge(psum_full, full(f"S{h}b"))
                for out, src in ((mx[i][0:64, 0:1], a_[0:64, 0:64]), (mx[i][64:128, 0:1], a_[64:128, 0:128]),
                                 (mx[i][0:64, 1:2], a_[0:64, 128:320]), (mx[i][64:128, 1:2], a_[64:128, 128:384])):
                    dve.tensor_reduce(out, src, AX, ALU.max)
                link(dve.tensor_reduce(mx[i][0:64, 2:3], b_[0:64, 0:320], AX, ALU.max))
                dve.tensor_scalar(nb_[i], mx[i], -SCALE, None, ALU.mult).then_inc(max_ready, 1)

            def normalise(h):
                i, pr = h % 2, pb[h % 2]
                dve.wait_ge(drained["act"], drain_count[f"S{h}b"])
                link(dve.reciprocal(sm[i], sm[i]))
                dve.tensor_scalar(pr[:, 0:128], pr[:, 0:128], sm[i][:, 0:1], None, ALU.mult)
                dve.tensor_scalar(pr[:, 128:384], pr[:, 128:384], sm[i][:, 1:2], None, ALU.mult)
                dve.tensor_scalar(pr[0:64, 384:704], pr[0:64, 384:704], sm[i][0:64, 2:3], None, ALU.mult).then_inc(p_ready, 1)

            def probs_T(h):
                pt = ptb[h % 2]
                dve.wait_ge(psum_full, full(f"PT{h}a"))
                drain("PTa", dve.tensor_copy(pt[:, 0:384], bank(f"PT{h}a")[:, 0:384]))
                dve.wait_ge(psum_full, full(f"PT{h}b"))
                dve.tensor_copy(pt[:, 384:512], bank(f"PT{h}b")[:, 0:128])
                drain("PTb", dve.tensor_copy(pt[0:64, 512:576], bank(f"PT{h}b")[0:64, 128:192]))

            keys(0)
            for p in range(H // 2):
                for h in (2 * p, 2 * p + 1):
                    maxima(h)
                for h in (2 * p, 2 * p + 1):
                    normalise(h)
                if p + 1 < H // 2:
                    keys(p + 1)
                for h in (2 * p, 2 * p + 1):
                    probs_T(h)
            scale_chunks(4, [mix[:, h, :] for h in range(H)], P_AO)

            dve.wait_ge(psum_full, full(f"PV{H - 1}"))
            link(dve.memset(work[:, 1024:2560], 0.0))
            dve.wait_ge(s_xagain, 48)
            dve.wait_ge(s_gffn, 16)
            for n in range(4):
                f = slice(512 * n, 512 * n + 512)
                for i, (t0, tn) in enumerate(TILES):
                    name = f"wo{n}_{i}"
                    dve.wait_ge(psum_full, full(name))
                    h, b = xtile[0:tn, i, f], bank(name)
                    if i < 2:
                        drain(name, dve.tensor_tensor(h, b, h, ALU.add))
                    else:
                        link(dve.tensor_tensor(h, b[0:64, :], h, ALU.add))
                        drain(name, dve.tensor_tensor(h, b[64:128, :], h, ALU.add))
                    dve.wait_ge(drained["dve"], drain_count[name])
                    dve.tensor_tensor(xn[0:tn, i, 4 * n:4 * n + 4, :].rearrange("t c q -> t q c"),
                                      h.rearrange("t (q c) -> t q c", c=4), gain[0:tn, f].rearrange("t (q c) -> t q c", c=4),
                                      ALU.mult).then_inc(hg_ready, 1)

            dve.wait_ge(h_squared, 12)
            dve.tensor_reduce(hsum, hss, AX, ALU.add).then_inc(route_in, 1)
            dve.wait_ge(route_act, 1)
            link(dve.reciprocal(hrs, hsd))
            link(dve.memset(lg, NEG))
            dve.wait_ge(logits_full, 12)
            for i, (t0, tn) in enumerate(TILES):
                b = ps[0:tn, ACC_BANK, 36 * i:36 * i + 36]
                for dst, c0, cn in ((lg, 0, G), (le, G, NE)):
                    link(dve.scalar_tensor_tensor(dst[0:tn, i, 0:cn], b[:, c0:c0 + cn], hrs[0:tn, i:i + 1],
                                                  brow[0:tn, c0:c0 + cn], ALU.mult, ALU.add))
            for i in range(3):
                link(dve.max(m8[:, i, :], lg[:, i, :]))
                link(dve.max_index(i8[:, 0, i, :], m8[:, i, :], lg[:, i, :]))
            dve.tensor_tensor(gx, lg[:, :, 0:G], m8[:, :, 0:1].to_broadcast([P, 3, G]), ALU.subtract).then_inc(route_in, 1)
            link(dve.tensor_copy(gidx, i8[:, 0, :, 0]))
            iota = const[:, C_IOTA:C_IOTA + NE]
            link(dve.tensor_tensor(ghot, iota[:, 0:G].unsqueeze(1).to_broadcast([P, 3, G]),
                                   gidx.unsqueeze(2).to_broadcast([P, 3, G]), ALU.is_equal))
            gsel = prod_flat[:, 0:96].rearrange("p (i g e) -> p i g e", i=3, g=G)
            link(dve.tensor_tensor(gsel, le.rearrange("p i (g e) -> p i g e", g=G),
                                   ghot.unsqueeze(3).to_broadcast([P, 3, G, EPG]), ALU.mult))
            link(dve.tensor_reduce(el, gsel.rearrange("p i g e -> p i e g"), AX, ALU.add))
            for i in range(3):
                link(dve.max(v8[:, i, :], el[:, i, :]))
                link(dve.max_index(i8[:, 1, i, :], v8[:, i, :], el[:, i, :]))
            dve.tensor_tensor(dv, v8[:, :, 1], v8[:, :, 0], ALU.subtract).then_inc(route_in, 1)
            link(dve.tensor_copy(eidx, i8[:, 1, :, 0:2]))
            link(dve.scalar_tensor_tensor(eid, gidx.unsqueeze(2).to_broadcast([P, 3, 2]), float(EPG), eidx, ALU.mult, ALU.add))
            link(dve.tensor_tensor(hot, iota.unsqueeze(1).unsqueeze(1).to_broadcast([P, 3, 2, NE]),
                                   eid.unsqueeze(3).to_broadcast([P, 3, 2, NE]), ALU.is_equal))
            dve.tensor_tensor(hot2, hot[:, :, 0, :], hot[:, :, 1, :], ALU.add).then_inc(hot_ready, 1)
            dve.wait_ge(route_act, 2)
            link(dve.tensor_reduce(gsum, gx, AX, ALU.add))
            link(dve.reciprocal(gp, gsum))
            dve.wait_ge(route_act, 3)
            link(dve.tensor_scalar(den, ev, 1.0, None, ALU.add))
            link(dve.reciprocal(rden, den))
            link(dve.tensor_tensor(gate[:, :, 0], gp, rden, ALU.mult))
            link(dve.tensor_tensor(gate[:, :, 1], gate[:, :, 0], ev, ALU.mult))
            dve.wait_ge(route_pe, 1)
            b = ps[:, SSQ_BANK, :]
            link(dve.tensor_tensor(cmp, b[:, 96:128].unsqueeze(2).to_broadcast([P, NE, MAXB - 1]),
                                   const[:, C_THR:C_THR + MAXB - 1].unsqueeze(1).to_broadcast([P, NE, MAXB - 1]), ALU.is_gt))
            link(dve.tensor_reduce(extra, cmp, AX, ALU.add))
            link(dve.tensor_tensor_scan(xincl, extra, extra, 0.0, ALU.add, ALU.bypass))
            link(dve.tensor_tensor(xexcl, xincl, extra, ALU.subtract))
            dve.tensor_copy(tables[0:1, 0, :], xexcl[0:1, :]).then_inc(routed, 1)
            dve.tensor_scalar(tables[0:1, 1, :], extra[0:1, :], 1.0, None, ALU.add).then_inc(routed, 1)
            dve.tensor_scalar(tables[0:1, 2, :], xincl[0:1, :], 12.0, 12.0, ALU.mult, ALU.add).then_inc(routed, 1)
            link(dve.tensor_copy(slot_of[:, 0:2, :], b[:, 0:64].rearrange("p (i e) -> p i e", i=2)))
            link(dve.tensor_copy(slot_of[0:64, 2, :], b[0:64, 64:96]))
            for k in range(2):
                link(dve.tensor_tensor(prod[:, :, k, :], hot[:, :, k, :], slot_of, ALU.mult))
            link(dve.tensor_reduce(rank, prod, AX, ALU.add))
            link(dve.tensor_scalar(high, rank, float(B), -1.0e6, ALU.is_ge, ALU.mult))
            link(dve.scalar_tensor_tensor(place, eid, float(B), rank, ALU.mult, ALU.add))
            link(dve.tensor_tensor(place, place, high, ALU.add))
            link(dve.scalar_tensor_tensor(placex, eid, 512.0, rank, ALU.mult, ALU.add))

            def pick_tokens(link, where, width, eq, pick, pickr, gpick, signal):
                link(dve.tensor_tensor(eq, const[:, C_IOTA:C_IOTA + width].unsqueeze(1).unsqueeze(1).to_broadcast([P, 3, 2, width]),
                                       where.unsqueeze(3).to_broadcast([P, 3, 2, width]), ALU.is_equal))
                link(dve.tensor_tensor(pick, eq[:, :, 0, :], eq[:, :, 1, :], ALU.add))
                link(dve.tensor_tensor(eq, eq, gate.unsqueeze(3).to_broadcast([P, 3, 2, width]), ALU.mult))
                link(dve.tensor_tensor(gpick, eq[:, :, 0, :], eq[:, :, 1, :], ALU.add))
                dve.tensor_tensor(pickr, pick, hrs.unsqueeze(2).to_broadcast([P, 3, width]), ALU.mult).then_inc(signal, 1)

            def add_results(full_sem, value, signal):
                for u in range(12):
                    i, n = u // 4, u % 4
                    tn = TILES[i][1]
                    dve.wait_ge(full_sem, value(u + 1))
                    h = xtile[0:tn, i, 512 * n:512 * n + 512]
                    dve.tensor_tensor(h, ps[0:tn, 5 + u % 3, :], h, ALU.add).then_inc(signal, 1)

            def times_up(signal):
                dve.tensor_tensor(hT, sil, ps[:, 3, 0:256].rearrange("p (c m s) -> p c m s", c=4, m=2)[:, :, 1, :],
                                  ALU.mult).then_inc(signal, 1)

            x_links = 5

            def extra_blocks(e):
                count = dve.value_load(tables[0:1, 1, bass.ds(e, 1)], min_val=1, max_val=MAXB)
                with dve.If(count > 1):
                    before = dve.value_load(tables[0:1, 0, bass.ds(e, 1)], min_val=0, max_val=64)
                    with dve.Fori(1, count) as k:
                        x = before + k
                        done = [0]

                        def link_x(ins):
                            done[0] += 1
                            ins.then_inc(x_step, 1)
                            dve.wait_ge(x_step, x * x_links + done[0])

                        link_x(dve.tensor_scalar(dest, dest, float(-B), None, ALU.add))
                        pick_tokens(link_x, dest, B, eqx, pickx, pickrx, gpickx, x_pick)
                        assert done[0] == x_links
                        dve.wait_ge(x_silu, x)
                        times_up(x_hT)
                        add_results(x_full, lambda v: before * 12 + (k * 12 + v - 12), x_added)

            pick_tokens(link, place, P, eq, pick, pickr, gpick, pick_ready)
            dve.sem_inc(comb_added, 1)
            dve.sem_inc(x_added, 12)
            dve.sem_inc(x_step, x_links)
            links = 13
            dve.wait_ge(routed, 3)
            with dve.Fori(0, NE // 4) as q:
                done = [0]

                def link_q(ins):
                    done[0] += 1
                    ins.then_inc(blk_step, 1)
                    dve.wait_ge(blk_step, q * links + done[0])

                for b in range(4):
                    e = q * 4 + b
                    link_q(dve.tensor_copy(dest, placex))
                    link_q(dve.tensor_scalar(placex, placex, -512.0, None, ALU.add))
                    if b == 3:
                        dve.wait_ge(gathered, q * 4 + 4)
                        dve.wait_ge(gt_full, q + 1)
                        link_q(dve.tensor_scalar(place, place, float(-P), None, ALU.add))
                        pick_tokens(link_q, place, P, eq, pick, pickr, gpick, pick_ready)
                    dve.wait_ge(silu_ready, e + 1)
                    times_up(hT_ready)
                    extra_blocks(e)
                assert done[0] == links, done
                add_results(comb_full, lambda v: q * 12 + v, comb_added)

            dve.wait_ge(s_gfin, 16)
            for i, (t0, tn) in enumerate(TILES):
                dve.wait_ge(fin_rooted, i + 1)
                link(dve.reciprocal(xrs[0:tn, i:i + 1], xsd[0:tn, i:i + 1]))
                dve.scalar_tensor_tensor(xtile[0:tn, i, :], xtile[0:tn, i, :], xrs[0:tn, i:i + 1], gain[0:tn, :],
                                         ALU.mult, ALU.mult).then_inc(fin_ready, 1)


def shape_constants():
    import numpy as np

    c = np.zeros((P, C_ALL), np.float32)
    c[:, C_ID:C_ID + P] = np.eye(P)
    half = ROPE // 2
    swap = np.zeros((ROPE, ROPE), np.float32)
    swap[np.arange(half) + half, np.arange(half)] = -1
    swap[np.arange(half), np.arange(half) + half] = 1
    for i in range(2):
        s = slice(ROPE * i, ROPE * (i + 1))
        c[s, C_ROT + ROPE * i:C_ROT + ROPE * (i + 1)] = swap
        c[0:ROPE, C_DUP + ROPE * i:C_DUP + ROPE * (i + 1)] = np.eye(ROPE)
        c[0:ROPE, C_DROT + ROPE * i:C_DROT + ROPE * (i + 1)] = swap
    c[:, C_TRI:C_TRI + P] = np.triu(np.ones((P, P)), 1)
    for q in range(4):
        c[B * q + np.arange(B), C_FOLD + B * (q // 2) + np.arange(B)] = 1
    c[:, C_IOTA:C_IOTA + P] = np.arange(P)
    c[:, C_THR:C_THR + MAXB - 1] = B * np.arange(1, MAXB)
    inv = np.float32(10000.0) ** (-np.arange(0, ROPE, 2, dtype=np.float32) / np.float32(ROPE))
    angle = np.arange(T, dtype=np.float32)[None, :] * inv[:, None]
    c[:, C_COS:C_COS + T] = np.tile(np.cos(angle), (4, 1))
    c[:, C_SIN:C_SIN + T] = np.tile(np.sin(angle), (4, 1))
    return c


_INS = ["x_prompt", "x_sample", "cache_kv_latent", "cache_k_rope", "state_conv", "norm_mix", "w_in", "norm_q",
        "w_uq", "norm_kv", "w_uk", "w_uv", "conv_w", "norm_attn_out", "norm_conv_out", "w_o", "norm_ffn",
        "w_router_group", "b_router_group", "w_router_expert", "b_router_expert", "w_gate", "w_up", "w_down",
        "norm_final"]
_OUTS = {
    "y_prompt": (1, SEQ, D), "y_sample": (1, DEC, D),
    "kv_prompt": (1, 1, SEQ, KL), "kr_prompt": (1, 1, SEQ, ROPE), "conv_prompt": (1, 1, 2, CH),
    "kv_sample": (1, 1, DEC, KL), "kr_sample": (1, 1, DEC, ROPE), "conv_sample": (1, 1, 2, CH),
}


def kernel(**inputs):
    import numpy as np
    import concourse.bacc as bacc
    from concourse.bass_utils import run_bass_kernel_spmd

    nc = bacc.Bacc("TRN2", target_bir_lowering=False, num_devices=1)
    arrays = {f"in_{name}": np.ascontiguousarray(inputs[name]) for name in _INS}
    arrays["in_const"] = shape_constants()
    a = {name[3:]: nc.dram_tensor(name, v.shape, mybir.dt.from_np(v.dtype), kind="ExternalInput").ap()
         for name, v in arrays.items()}
    for name, shape in _OUTS.items():
        a[name] = nc.dram_tensor(f"out_{name}", shape, F32, kind="ExternalOutput").ap()
    trunk_layer_kernel(nc, a)
    r = run_bass_kernel_spmd(nc, [arrays], core_ids=[0])
    return tuple(r.results[0][f"out_{name}"] for name in _OUTS)
```

```python
from contextlib import ExitStack

import concourse.bass as bass
from concourse import mybir

F32 = mybir.dt.float32
F32R = mybir.dt.float32r
I32 = mybir.dt.int32
U32 = mybir.dt.uint32
ALU = mybir.AluOpType
ACT = mybir.ActivationFunctionType
AX = mybir.AxisListType.X

P = 128
D = 2048
SEQ, DEC, PAST = 256, 64, 256
T = SEQ + DEC
TILES = ((0, 128), (128, 128), (256, 64))
CHUNK = 64
H = 8
NOPE, ROPE, VD = 128, 64, 128
QKD = NOPE + ROPE
QL, KL = 512, 512
CH = 1024
NCH = CH // P
KC = D // P
LC = QL // P
KEYS = T + PAST
G, EPG = 4, 8
NE = G * EPG
FF = 512
B = 32
MAXB = -(-T // B)
EPS = 1e-6
SCALE = float(QKD) ** -0.5
SLOTS = 6
SLOT = 4096
RB = 6
SSQ_BANK, ACC_BANK = 6, 7
NEG = -3.0e38

C_ID, C_ROT, C_TRI, C_DUP, C_DROT = 0, 128, 256, 384, 512
C_FOLD, C_THR, C_IOTA, C_COS = 640, 704, 704 + MAXB, 704 + MAXB + P
C_SIN = C_COS + T
C_ALL = C_SIN + T
P_MIX, P_Q, P_KV, P_CONV, P_AO, P_CO, P_ST = 0, 16, 20, 24, 48, 56, 64
P_ALL = 80

W_CQ, W_KV, W_KR, W_CONV, W_UV, W_PAIR, W_O = 0, 2, 4, 5, 17, 18, 22
W_END = 30
SPLIT_SLOTS = 4


def slot_of_item(n):
    return n % SPLIT_SLOTS if n < W_UV else (n - W_UV + 1) % (SPLIT_SLOTS - 1)


def projections():
    p = [(f"cq{m}", W_CQ + m // 2, P * (m % 2), P) for m in range(LC)]
    p += [(f"ckv{m}", W_KV + m // 2, P * (m % 2), P) for m in range(LC)]
    p += [("kr", W_KR, 0, ROPE)]
    for j in range(NCH // 2):
        p += [(f"{name}{2 * j + i}", W_CONV + 3 * j + k, P * i, P) for k, name in enumerate("ChB") for i in range(2)]
    return p

KT = ((0, 128), (128, 128), (256, 128), (384, 128), (512, 64))


def psum_jobs():
    jobs = [("par", "act")]
    jobs += [(f"xt{i}_{k}", "dve") for k in range(4) for i in range(3)]
    jobs += [(f"cq{m}", "act") for m in range(LC)] + [(f"ckv{m}", "act") for m in range(LC)]
    jobs += [("kr", "act"), ("cc0", "act"), ("cc1", "act"), ("ckr", "act"), ("krdup", "dve"), ("krrot", "dve")]
    for j in range(NCH // 2):
        jobs += [(f"C{2 * j + k}", "act") for k in range(2)]
        jobs += [(f"h{2 * j + k}", "dve") for k in range(2)]
        jobs += [(f"B{2 * j + k}", "dve") for k in range(2)]
        if j == 0:
            jobs += [("okv0", "act"), ("okv1", "act"), ("okv2", "act"), ("okr", "act")]
    jobs += [(f"V{t}_{v}", "act") for t in range(5) for v in range(2)]
    jobs += [("ulast", "act")]

    def pair_jobs(p):
        return ([(f"qr{p}", "act")] + [(f"q{2 * p + i}", "act") for i in range(2)]
                + [(f"K{2 * p}_0", "dve"), (f"qrot{p}", "dve"), (f"K{2 * p}_1", "dve")]
                + [(f"K{2 * p + 1}_{s}", "dve") for s in range(2)])

    jobs += pair_jobs(0)
    for p in range(H // 2):
        jobs += [(f"S{2 * p + i}{s}", "act") for i in range(2) for s in "ab"]
        if p + 1 < H // 2:
            jobs += pair_jobs(p + 1)
        jobs += [(f"PT{2 * p + i}{s}", "dve") for i in range(2) for s in "ab"]
        jobs += [(f"PV{2 * p + i}", "act") for i in range(2)]
    for n in range(4):
        jobs += [(f"wo{n}_{i}", "dve") for i in range(3)]
        if n >= 1:
            jobs += [(f"rt{n - 1}_{i}", "act") for i in range(3)]
    jobs += [(f"rt3_{i}", "act") for i in range(3)]
    return jobs


def trunk_layer_kernel(nc: bass.Bass, a):
    jobs = psum_jobs()
    job_index = {name: i for i, (name, _) in enumerate(jobs)}
    drain_count = {}
    for name, engine in jobs:
        drain_count[name] = 1 + sum(1 for n, e in jobs[:job_index[name]] if e == engine)
    splits = projections()
    split_index = {name: u for u, (name, _, _, _) in enumerate(splits)}

    with ExitStack() as ctx:
        def sb(name, shape, dt=F32):
            return ctx.enter_context(nc.sbuf_tensor(name, shape, dt))

        def sem(name):
            return ctx.enter_context(nc.semaphore(name))

        ring_at = -(-nc.sbuf_base // 32) * 32
        ring = sb("ring", [P, SLOTS, SLOT])
        assert nc.sbuf_base == ring_at + 4 * SLOTS * SLOT
        hreg = sb("hreg", [P, 3 * D])
        r2 = sb("r2", [P, 3 * D])
        assert nc.sbuf_base == ring_at + 4 * (SLOTS * SLOT + 6 * D)
        parts_at = ring_at + 4 * SPLIT_SLOTS * SLOT
        hreg_at = ring_at + 4 * SLOTS * SLOT
        w_hi = nc.alloc_sbuf_tensor_at("w_hi", [P, 2, KC, P], F32R, offset=parts_at)
        w_lo = nc.alloc_sbuf_tensor_at("w_lo", [P, 2, KC, P], F32R, offset=parts_at + 4 * 2 * KC * P)
        xT_lo = nc.alloc_sbuf_tensor_at("xT_lo", [P, KC, T], F32R, offset=hreg_at)
        xT_hi = nc.alloc_sbuf_tensor_at("xT_hi", [P, KC, T], F32R, offset=hreg_at + 4 * 3 * D)
        mix = sb("mix", [P, KC, T])
        assert nc.sbuf_base == ring_at + 4 * (SLOTS * SLOT + 6 * D + KC * T)
        ckv = sb("ckv", [P, LC, KEYS])
        cq = sb("cq", [P, LC, T])
        krt = sb("krt", [P, KEYS])
        const = sb("const", [P, C_ALL])
        par = sb("par", [P, P_ALL])
        ones = sb("ones", [P, P])
        work = sb("work", [P, 4960])
        small = sb("small", [P, 64])
        tables = sb("tables", [1, 4, NE], I32)

        ps = ctx.enter_context(nc.psum_tensor("ps", [P, 8, 512], F32))

        ident = const[:, C_ID:C_ID + P]
        cos, sin = const[:, C_COS:C_COS + T], const[:, C_SIN:C_SIN + T]
        xtile = hreg[:, :].rearrange("p (i d) -> p i d", i=3)
        mix_at = hreg_at + 4 * 6 * D
        o_hi = nc.alloc_sbuf_tensor_at("o_hi", [P, 4, 2, 512], F32R, offset=parts_at)
        o_lo = nc.alloc_sbuf_tensor_at("o_lo", [P, 4, 2, 512], F32R, offset=parts_at + 4 * SLOT)
        m_hi = nc.alloc_sbuf_tensor_at("m_hi", [P, KC, SEQ], F32R, offset=parts_at - 4 * SLOT)
        m_lo = nc.alloc_sbuf_tensor_at("m_lo", [P, KC, T], F32R, offset=mix_at)
        mflat = mix[:, :, :].rearrange("p c t -> p (c t)")
        xnorm = [mflat[:, 0:D], mflat[:, D:2 * D], work[:, 1408:1408 + D]]
        xT_raw = work[:, 3456:4480].rearrange("p (b c t) -> p b c t", b=2, c=4)
        sq_q = mix[:, 0:4, :]
        sq_kv = mix[:, 4:8, :]
        cstage = work[:, 0:2 * KL].rearrange("p (i l) -> p i l", i=2)
        ckrstage = work[:, 1024:1280].rearrange("p (i r) -> p i r", i=2)
        csb = work[:, 0:2 * T].rearrange("p (i t) -> p i t", i=2)
        UE = T + 4
        uext = work[:, 640:640 + NCH * UE].rearrange("p (c u) -> p c u", c=NCH)
        cv = work[:, 3232:3232 + UE - 2]
        sq = work[:, 3554:3554 + 2 * T].rearrange("p (i t) -> p i t", i=2)
        rs = work[:, 4194:4194 + T]
        rot_a = work[:, 4514:4514 + T]
        rot_b = mix[:, KC - 1, :]
        kraw = cv[0:ROPE, 0:T]
        ulast = small[:, 0:32].rearrange("p (r c) -> p r c", r=4)
        eps_col = small[:, 62:63]
        xss, xsd, xrs = small[:, 32:35], small[:, 35:38], small[:, 38:41]
        okv = mflat[:, 0:3 * KL].rearrange("p (i l) -> p i l", i=3)
        okr = mflat[:, 1536:1536 + 3 * ROPE].rearrange("p (i r) -> p i r", i=3)
        oul = hreg[0:32, 5120:5120 + P]
        acc_conv, acc_att = hreg[:, 5248:5248 + T], hreg[:, 5568:5568 + T]
        par_rows = work[0:P_ALL, 1280:1280 + P]
        vals = hreg[:, 0:5 * CH].rearrange("p (k v) -> p k v", k=5)
        qt = r2[:, 0:1920].rearrange("p (b i t) -> p b i t", b=2, i=3)
        kt = r2[:, 1920:4224].rearrange("p (b i k) -> p b i k", b=2, i=2)
        qraw = r2[:, 4224:4544]
        att_a = r2[:, 4544:4864]
        att_b = r2[:, 4864:5184]
        pb = [work[:, 0:704], work[:, 704:1408]]
        ptb = [work[:, 1408:1984], work[:, 1984:2560]]
        mx = [small[:, 44 + 3 * k:47 + 3 * k] for k in range(2)]
        nb_ = [small[:, 50 + 3 * k:53 + 3 * k] for k in range(2)]
        sm = [small[:, 56 + 3 * k:59 + 3 * k] for k in range(2)]
        xn = r2[:, :].rearrange("p (i c q) -> p i c q", i=3, c=KC)
        wr = cq[:, :, :].rearrange("p c t -> p (c t)")[:, 0:KC * 36].rearrange("p (c e) -> p c e", c=KC)
        brow = cq[:, :, :].rearrange("p c t -> p (c t)")[:, 576:612]
        gain = ckv[:, :, :].rearrange("p c t -> p (c t)")[:, 0:D]
        rtb = [work[:, 2560:3072].rearrange("p (c t) -> p c t", c=4), work[:, 0:512].rearrange("p (c t) -> p c t", c=4)]
        junk = work[:, 512:1024]
        w0 = 1024
        hss = work[:, w0:w0 + 12].rearrange("p (i n) -> p i n", i=3)
        hsum, hsd, hrs = (work[:, w0 + 12 + 3 * k:w0 + 15 + 3 * k] for k in range(3))
        w0 += 24
        lg = work[:, w0:w0 + 24].rearrange("p (i g) -> p i g", i=3)
        le = work[:, w0 + 24:w0 + 120].rearrange("p (i e) -> p i e", i=3)
        m8 = work[:, w0 + 120:w0 + 144].rearrange("p (i e) -> p i e", i=3)
        v8 = work[:, w0 + 144:w0 + 168].rearrange("p (i e) -> p i e", i=3)
        el = work[:, w0 + 168:w0 + 192].rearrange("p (i e) -> p i e", i=3)
        gx = work[:, w0 + 192:w0 + 204].rearrange("p (i g) -> p i g", i=3)
        ghot = work[:, w0 + 204:w0 + 216].rearrange("p (i g) -> p i g", i=3)
        gidx, gsum, gp, dv, ev, den, rden = (work[:, w0 + 216 + 3 * k:w0 + 219 + 3 * k] for k in range(7))
        eidx = work[:, w0 + 240:w0 + 246].rearrange("p (i k) -> p i k", i=3)
        eid = work[:, w0 + 246:w0 + 252].rearrange("p (i k) -> p i k", i=3)
        gate = work[:, w0 + 252:w0 + 258].rearrange("p (i k) -> p i k", i=3)
        dest, rank, high, place, placex = (
            work[:, w0 + 258 + 6 * k:w0 + 264 + 6 * k].rearrange("p (i k) -> p i k", i=3) for k in range(5))
        w0 += 288
        hot = work[:, w0:w0 + 192].rearrange("p (i k e) -> p i k e", i=3, k=2)
        hot2 = work[:, w0 + 192:w0 + 288].rearrange("p (i e) -> p i e", i=3)
        slot_of = work[:, w0 + 288:w0 + 384].rearrange("p (i e) -> p i e", i=3)
        prod_flat = work[:, w0 + 384:w0 + 576]
        prod = work[:, w0 + 384:w0 + 576].rearrange("p (i k e) -> p i k e", i=3, k=2)
        cmp = work[:, w0 + 576:w0 + 576 + NE * (MAXB - 1)].rearrange("p (e j) -> p e j", e=NE)
        w0 += 576 + NE * (MAXB - 1)
        extra, xincl, xexcl = (work[:, w0 + NE * k:w0 + NE * k + NE] for k in range(3))
        w0 += 3 * NE
        i8 = sb("i8", [P, 2, 3, 8], U32)
        assert w0 <= 2560, w0
        xg = mflat[:, 0:512].rearrange("p (c j s) -> p c j s", c=4, j=4)
        gsb = mflat[:, 512:1024]
        hsb = mflat[:, 1024:1536].rearrange("p (c q) -> p c q", c=4)
        hT = mflat[:, 1536:1664].rearrange("p (c s) -> p c s", c=4)
        sil = mflat[:, 1664:1792].rearrange("p (c s) -> p c s", c=4)
        yg = mflat[:, 1792:3840]
        gT = mflat[:, 3840:4160]
        xx = mflat[:, 4160:4672].rearrange("p (c j s) -> p c j s", c=4, j=4)
        gTx = mflat[:, 4672:4992]
        cqflat = cq[:, :, :].rearrange("p c t -> p (c t)")
        yx = cqflat[:, 0:512]
        eq = work[:, 2560:3328].rearrange("p (i k s) -> p i k s", i=3, k=2)
        pick = work[:, 3328:3712].rearrange("p (i s) -> p i s", i=3)
        pickr = work[:, 3712:4096].rearrange("p (i s) -> p i s", i=3)
        gpick = work[:, 4096:4480].rearrange("p (i s) -> p i s", i=3)
        eqx = work[:, 4480:4672].rearrange("p (i k s) -> p i k s", i=3, k=2)
        pickx = work[:, 4672:4768].rearrange("p (i s) -> p i s", i=3)
        pickrx = work[:, 4768:4864].rearrange("p (i s) -> p i s", i=3)
        gpickx = cqflat[:, 512:896].rearrange("p (i s) -> p i s", i=3)

        m_hi_ready, m_lo_ready = sem("m_hi_ready"), sem("m_lo_ready")
        o_hi_ready, o_lo_ready, o_used = sem("o_hi_ready"), sem("o_lo_ready"), sem("o_used")
        s_const, s_par, s_par_pool, s_cache = sem("s_const"), sem("s_par"), sem("s_par_pool"), sem("s_cache")
        s_x = [sem(f"s_x{i}") for i in range(3)]
        slot_full = [sem(f"slot_full{i}") for i in range(SLOTS)]
        psum_full = sem("psum_full")
        drained = {"act": sem("drained_act"), "dve": sem("drained_dve")}
        s_ones = sem("s_ones")
        xT_hi_ready, xT_lo_ready = sem("xT_hi_ready"), sem("xT_lo_ready")
        w_hi_ready, w_lo_ready = sem("w_hi_ready"), sem("w_lo_ready")
        x_squared, x_rooted, x_scaled = sem("x_squared"), sem("x_rooted"), sem("x_scaled")
        ssq_full, rooted, normed = sem("ssq_full"), sem("rooted"), sem("normed")
        kr_ready, conv_squared, heads_summed = sem("kr_ready"), sem("conv_squared"), sem("heads_summed")
        sq_summed, pool_step = sem("sq_summed"), sem("pool_step")
        ulast_ready = sem("ulast_ready")
        q_ready, max_ready, p_ready = sem("q_ready"), sem("max_ready"), sem("p_ready")
        wo_half_used = sem("wo_half_used")
        s_xagain, s_router, s_gffn, s_gfin = sem("s_xagain"), sem("s_router"), sem("s_gffn"), sem("s_gfin")
        hg_ready, h_squared, logits_full = sem("hg_ready"), sem("h_squared"), sem("logits_full")
        hot_ready, route_in, route_act, route_pe = sem("hot_ready"), sem("route_in"), sem("route_act"), sem("route_pe")
        routed = sem("routed")
        dve_step = sem("dve_step")
        conv_summed = sem("conv_summed")
        gates_ready, x_gates = sem("gates_ready"), sem("x_gates")
        pick_ready, gathered, g_copied, transposed = sem("pick_ready"), sem("gathered"), sem("g_copied"), sem("transposed")
        xg_ready, weights_used, h_copied, folded = sem("xg_ready"), sem("weights_used"), sem("h_copied"), sem("folded")
        silu_ready, hT_ready, y_copied = sem("silu_ready"), sem("hT_ready"), sem("y_copied")
        gt_full, gt_copied, comb_full, comb_added = sem("gt_full"), sem("gt_copied"), sem("comb_full"), sem("comb_added")
        x_pick, x_gathered, x_copied, x_transposed = sem("x_pick"), sem("x_gathered"), sem("x_copied"), sem("x_transposed")
        x_ready, x_hcopied, x_folded = sem("x_ready"), sem("x_hcopied"), sem("x_folded")
        x_silu, x_hT, x_ycopied, extra_used = sem("x_silu"), sem("x_hT"), sem("x_ycopied"), [sem(f"extra_used{s}") for s in range(SLOTS)]
        x_gtfull, x_gtcopied, x_full, x_added = sem("x_gtfull"), sem("x_gtcopied"), sem("x_full"), sem("x_added")
        blk_step, x_step = sem("blk_step"), sem("x_step")
        fin_squared, fin_rooted, fin_ready = sem("fin_squared"), sem("fin_rooted"), sem("fin_ready")
        s_out, s_stage, s_final = sem("s_out"), sem("s_stage"), sem("s_final")

        xp, xs = a["x_prompt"][0], a["x_sample"][0]
        x_src = (xp[0:128, :], xp[128:256, :], xs)
        w_in = a["w_in"][0].rearrange("(c p) n -> p c n", p=P)
        w_uq = a["w_uq"][0].rearrange("(c p) n -> p c n", p=P)
        w_uk = a["w_uk"][0].rearrange("(c p) h n -> p c (h n)", p=P)
        w_uv = a["w_uv"][0].rearrange("(c p) h n -> p c (h n)", p=P)
        w_o = a["w_o"][0].rearrange("(c p) n -> p c n", p=P)

        def bank(name):
            return ps[:, job_index[name] % RB, :]

        def full(name):
            return job_index[name] + 1

        def claim(pe, name):
            n = job_index[name] - RB
            if n >= 0:
                before, engine = jobs[n]
                pe.wait_ge(drained[engine], drain_count[before])
            return bank(name)

        def slot_count(n):
            return 32 * sum(1 for k in range(n + 1) if slot_of_item(k) == slot_of_item(n))

        def expert_count(s):
            return 32 * (1 + sum(1 for k in range(W_END) if slot_of_item(k) == s))

        def wslot(n):
            return ring[:, slot_of_item(n), :]

        def w_raw(u, half):
            _, n, col, width = splits[u]
            w = wslot(n)[:, 0:KC * (256 if width == P else width)].rearrange("p (c n) -> p c n", c=KC)
            return w[:, 8 * half:8 * half + 8, col:col + width]

        def o_raw(v):
            w = wslot(W_O + v // 4).rearrange("p (c n) -> p c n", c=8)
            return w[:, 2 * (v % 4):2 * (v % 4) + 2, :]

        def wait_pair_used(engine, v):
            if v % 8 == 7:
                engine.wait_ge(psum_full, full(f"wo{v // 8}_1"))
            else:
                engine.wait_ge(o_used, v + 1 - v // 8)

        def phase1_weights():
            def cols(n, first, count, last):
                v = wslot(n)[:, 0:KC * count].rearrange("p (c n) -> p c n", c=KC)
                return n, [(v[:, k:k + 8, :], w_in[:, k:k + 8, first:first + count]) for k in (0, 8)], last

            for m in range(2):
                yield cols(W_CQ + m, 256 * m, 256, f"cq{2 * m + 1}")
            for m in range(2):
                yield cols(W_KV + m, QL + 256 * m, 256, f"ckv{2 * m + 1}")
            yield cols(W_KR, QL + KL, ROPE, "kr")
            base = QL + KL + ROPE
            for j in range(NCH // 2):
                for k, (first, job) in enumerate(((base + CH, "C"), (base + 2 * CH, "h"), (base, "B"))):
                    yield cols(W_CONV + 3 * j + k, first + 256 * j, 256, f"{job}{2 * j + 1}")
            v = wslot(W_UV).rearrange("p (c n) -> p c n", c=LC)
            yield W_UV, [(v[:, k:k + 2, :], w_uv[:, k:k + 2, :]) for k in (0, 2)], "V4_1"
            for p in range(H // 2):
                s = wslot(W_PAIR + p)
                yield W_PAIR + p, [
                    (s[:, 0:1536].rearrange("p (c n) -> p c n", c=LC), w_uq[:, :, 2 * QKD * p:2 * QKD * (p + 1)]),
                    (s[:, 1536:2560].rearrange("p (c n) -> p c n", c=LC), w_uk[:, :, 256 * p:256 * (p + 1)]),
                ], f"K{2 * p + 1}_1"
            for n in range(4):
                for half in range(2):
                    v = wslot(W_O + 2 * n + half).rearrange("p (c n) -> p c n", c=8)
                    k0 = 8 * (1 - half)
                    yield W_O + 2 * n + half, [
                        (v[:, k:k + 4, :], w_o[:, k0 + k:k0 + k + 4, 512 * n:512 * n + 512]) for k in (0, 4)
                    ], (f"half{n}" if half == 0 else f"wo{n}_2")

        w1 = list(phase1_weights())
        assert [n for n, _, _ in w1] == list(range(W_END))

        def expert_slot(i, gate_w, up_w, down_w):
            if i < 4:
                s = ring[:, i, :].rearrange("p (m c n) -> p m c n", m=2, c=4)
                return [(s[:, m], w[512 * i:512 * i + 512, :].rearrange("(p c) n -> p c n", c=4))
                        for m, w in enumerate((gate_w, up_w))]
            s = ring[:, i, :].rearrange("p (c n) -> p c n", c=2)
            v = down_w.rearrange("(p c) n -> p c n", c=4)
            return [(s[:, c], v[:, 2 * (i - 4) + c, :]) for c in range(2)]

        def late_loads(sp):
            sp.wait_ge(psum_full, full(f"K{H - 1}_1"))
            for i in range(4):
                v = a["w_router_group"][0].rearrange("(i p c) e -> i p c e", p=P, c=4)
                sp.dma_start(wr[:, 4 * i:4 * i + 4, 0:G], v[i]).then_inc(s_router, 16)
                v = a["w_router_expert"][0].rearrange("(i p c) g e -> i p c (g e)", p=P, c=4)
                sp.dma_start(wr[:, 4 * i:4 * i + 4, G:G + NE], v[i]).then_inc(s_router, 16)
            sp.dma_start(brow[:, 0:G], a["b_router_group"].to_broadcast([P, G])).then_inc(s_router, 16)
            sp.dma_start(brow[:, G:G + NE],
                         a["b_router_expert"].rearrange("a g e -> a (g e)").to_broadcast([P, NE])).then_inc(s_router, 16)
            sp.dma_start(gain, a["norm_ffn"].to_broadcast([P, D])).then_inc(s_gffn, 16)
            sp.wait_ge(psum_full, full(f"PV{H - 1}"))
            sp.wait_ge(s_stage, 64)
            sp.wait_ge(ssq_full, 4)
            for i, (t0, tn) in enumerate(TILES):
                sp.dma_start(xtile[0:tn, i, :], x_src[i]).then_inc(s_xagain, 16)

        used_by = {n: last for n, _, last in w1}
        item_before = {}
        holder = {s: None for s in range(SLOTS)}
        for n in range(W_END):
            item_before[n] = holder[slot_of_item(n)]
            holder[slot_of_item(n)] = n

        def wait_slot_free(sp, last):
            if last in split_index:
                sp.wait_ge(w_lo_ready, 2 * split_index[last] + 2)
            elif last.startswith("half"):
                sp.wait_ge(wo_half_used, int(last[4:]) + 1)
            else:
                sp.wait_ge(psum_full, full(last))

        block = ctx.enter_context(nc.Block())

        @block.sync
        def _(sp):
            sp.dma_start(xtile[:, 0, :], x_src[0]).then_inc(s_x[0], 16)
            sp.dma_start(xtile[:, 1, :], x_src[1]).then_inc(s_x[1], 16)
            sp.dma_start(xtile[0:64, 2, :], x_src[2]).then_inc(s_x[2], 16)
            sp.dma_start(const[:, :], a["const"]).then_inc(s_const, 16)
            for n, parts, _ in w1:
                if item_before[n] is not None:
                    wait_slot_free(sp, used_by[item_before[n]])
                for dst, src in parts:
                    sp.dma_start(dst, src).then_inc(slot_full[slot_of_item(n)], 16)
                if n == W_O + 2:
                    late_loads(sp)
            for i in (2, 0, 1, 3, 4, 5):
                wait_slot_free(sp, used_by[holder[i]] if i < SPLIT_SLOTS - 1 else "wo3_2")
                for dst, src in expert_slot(i, a["w_gate"][0, 0], a["w_up"][0, 0], a["w_down"][0, 0]):
                    sp.dma_start(dst, src).then_inc(slot_full[i], 16)
            sp.wait_ge(routed, 4)
            with sp.Fori(1, NE) as e:
                used = sp.value_load(tables[0:1, 3, bass.ds(e, 1)], min_val=1, max_val=65)
                for i in range(SLOTS):
                    sp.wait_ge(weights_used, e * SLOTS + (i + 1 - SLOTS))
                    sp.wait_ge(extra_used[i], used)
                    w = [a[k][0, bass.ds(e, 1)].rearrange("a b c -> (a b) c") for k in ("w_gate", "w_up", "w_down")]
                    for dst, src in expert_slot(i, *w):
                        sp.dma_start(dst, src).then_inc(slot_full[i], 16)
            for i, (t0, tn) in enumerate(TILES):
                sp.wait_ge(fin_ready, i + 1)
                out = a["y_prompt"][0][t0:t0 + tn, :] if i < 2 else a["y_sample"][0]
                sp.dma_start(out, xtile[0:tn, i, :]).then_inc(s_final, 16)
            sp.wait_ge(s_final, 48)
            sp.wait_ge(s_out, 64)
            sp.wait_ge(s_stage, 64)

        @block.gpsimd
        def _(pool):
            pool.dma_start(par_rows[P_CO:P_CO + 8, :], a["norm_conv_out"].rearrange("a (c p) -> (a c) p", p=P)).then_inc(s_par_pool, 16)
            pool.dma_start(par_rows[P_CONV:P_CONV + 24, :],
                           a["conv_w"][0].rearrange("j (c p) -> (j c) p", p=P)).then_inc(s_par_pool, 16)
            pool.dma_start(par_rows[P_ST:P_ST + 16, :],
                           a["state_conv"][0, 0].rearrange("j (c p) -> (j c) p", p=P)).then_inc(s_par_pool, 16)
            pool.dma_start(cstage, a["cache_kv_latent"][0, 0].rearrange("(i p) l -> p i l", p=P)).then_inc(s_cache, 16)
            for k in range(2):
                pool.dma_start(ckrstage[:, :, ROPE * k:ROPE * (k + 1)],
                               a["cache_k_rope"][0, 0].rearrange("(i p) r -> p i r", p=P)).then_inc(s_cache, 16)
            steps = [0]

            for which, (squares, last) in enumerate(((sq_q, "cq3"), (sq_kv, "ckv3"))):
                pool.wait_ge(drained["act"], drain_count[last])
                for m in range(1, LC):
                    ins = pool.tensor_tensor(squares[:, 0, :], squares[:, 0, :], squares[:, m, :], ALU.add)
                    if m < LC - 1:
                        steps[0] += 1
                        ins.then_inc(pool_step, 1)
                        pool.wait_ge(pool_step, steps[0])
                ins.then_inc(sq_summed, 1)

            pool.wait_ge(drained["act"], drain_count["okr"])
            pool.dma_start(a["kv_prompt"][0, 0].rearrange("(i p) l -> p i l", p=P), okv[:, 0:2, :]).then_inc(s_out, 16)
            pool.dma_start(a["kv_sample"][0, 0], okv[0:64, 2, :]).then_inc(s_out, 16)
            pool.dma_start(a["kr_prompt"][0, 0].rearrange("(i p) r -> p i r", p=P), okr[:, 0:2, :]).then_inc(s_out, 16)
            pool.dma_start(a["kr_sample"][0, 0], okr[0:64, 2, :]).then_inc(s_out, 16)

            def running_sum(acc, count, ready, summed):
                for c in range(count):
                    ready(c)
                    src = sq[:, c % 2, :]
                    if c:
                        pool.wait_ge(summed, c)
                        ins = pool.tensor_tensor(acc, acc, src, ALU.add)
                    else:
                        ins = pool.tensor_copy(acc, src)
                    ins.then_inc(summed, 1)

            running_sum(acc_conv, NCH, lambda c: pool.wait_ge(conv_squared, c + 1), conv_summed)
            pool.wait_ge(drained["act"], drain_count["ulast"])
            for s, name in enumerate(("conv_prompt", "conv_sample")):
                for k in range(2):
                    r = 2 * s + k
                    pool.dma_start(a[name][0, 0, k:k + 1].rearrange("a (c p) -> (a c) p", p=P),
                                   hreg[8 * r:8 * r + 8, 5120:5120 + P]).then_inc(s_stage, 16)
            running_sum(acc_att, H, lambda h: pool.wait_ge(drained["act"], drain_count[f"PV{h}"]), heads_summed)
            pool.wait_ge(hg_ready, 12)
            pool.dma_start(gain, a["norm_final"].rearrange("(a d) -> a d", a=1).to_broadcast([P, D])).then_inc(s_gfin, 16)

        @block.tensor
        def _(pe):
            def wait_weights(n):
                pe.wait_ge(slot_full[slot_of_item(n)], slot_count(n))

            pe.wait_ge(s_const, 16)
            pe.wait_ge(s_par, 16 * 4)
            pe.wait_ge(s_par_pool, 16 * 3)
            pe.transpose(claim(pe, "par")[:, 0:P_ALL], par_rows, ident[0:P_ALL, 0:P_ALL]).then_inc(psum_full, 1)
            for k in range(4):
                for i, (t0, tn) in enumerate(TILES):
                    if k == 0:
                        pe.wait_ge(x_scaled, i + 1)
                    b = claim(pe, f"xt{i}_{k}")
                    for c in range(4):
                        f = P * (4 * k + c)
                        last = pe.transpose(b[:, c * tn:(c + 1) * tn], xnorm[i][0:tn, f:f + P], ident[0:tn, 0:tn])
                    last.then_inc(psum_full, 1)

            def project(name):
                b = claim(pe, name)
                u = split_index[name]
                width = splits[u][3]
                for c in range(KC):
                    if c % 8 == 0:
                        pe.wait_ge(w_lo_ready, 2 * u + 1 + c // 8)
                    if u == 0 and c % 4 == 0:
                        pe.wait_ge(xT_lo_ready, 3 * (c // 4) + 3)
                    hi, lo = w_hi[:, u % 2, c, 0:width], w_lo[:, u % 2, c, 0:width]
                    out = b[0:width, 0:T]
                    pe.matmul(out, hi, xT_hi[:, c, :], start=c == 0, stop=False)
                    pe.matmul(out, hi, xT_lo[:, c, :], start=False, stop=False)
                    last = pe.matmul(out, lo, xT_hi[:, c, :], start=False, stop=c == KC - 1)
                last.then_inc(psum_full, 1)

            def sum_squares(summed, count, src, bank):
                pe.wait_ge(summed, count)
                pe.matmul(ps[:, bank, 0:T], ones[:, :], src, start=True, stop=True).then_inc(ssq_full, 1)

            for m in range(LC):
                project(f"cq{m}")
            for m in range(LC):
                project(f"ckv{m}")
                if m == 1:
                    pe.wait_ge(s_ones, 2)
                    sum_squares(sq_summed, 1, sq_q[:, 0, :], SSQ_BANK)
            project("kr")
            pe.wait_ge(s_cache, 48)
            for i in range(2):
                b = claim(pe, f"cc{i}")
                for c in range(LC):
                    last = pe.transpose(b[:, P * c:P * (c + 1)], cstage[:, i, P * c:P * (c + 1)], ident)
                last.then_inc(psum_full, 1)
            b = claim(pe, "ckr")
            for i in range(2):
                last = pe.transpose(b[:, P * i:P * (i + 1)], ckrstage[:, i, :], ident)
            last.then_inc(psum_full, 1)
            pe.wait_ge(drained["act"], drain_count["kr"])
            for name, col in (("krdup", C_DUP), ("krrot", C_DROT)):
                pe.matmul(claim(pe, name)[:, 0:T], const[0:ROPE, col:col + P], kraw, start=True, stop=True).then_inc(psum_full, 1)
            for j in range(NCH // 2):
                for k, name in enumerate("ChB"):
                    for i in range(2):
                        project(f"{name}{2 * j + i}")
                        if j == k == i == 0:
                            sum_squares(sq_summed, 2, sq_kv[:, 0, :], ACC_BANK)
                if j == 0:
                    pe.wait_ge(normed, 2 * LC)
                    for i, (t0, tn) in enumerate(TILES):
                        b = claim(pe, f"okv{i}")
                        for m in range(LC):
                            last = pe.transpose(b[0:tn, P * m:P * (m + 1)], ckv[:, m, t0:t0 + tn], ident)
                        last.then_inc(psum_full, 1)
                    pe.wait_ge(kr_ready, 1)
                    b = claim(pe, "okr")
                    for i, (t0, tn) in enumerate(TILES):
                        last = pe.transpose(b[0:tn, ROPE * i:ROPE * (i + 1)], krt[0:ROPE, t0:t0 + tn], ident[0:ROPE, 0:ROPE])
                    last.then_inc(psum_full, 1)
            wait_weights(W_UV)
            wv = wslot(W_UV).rearrange("p (c n) -> p c n", c=LC)
            pe.wait_ge(drained["act"], drain_count["cc1"])
            for k, (k0, kn) in enumerate(KT):
                for v in range(2):
                    b = claim(pe, f"V{k}_{v}")
                    for c in range(LC):
                        last = pe.matmul(b[0:kn, :], ckv[:, c, k0:k0 + kn], wv[:, c, 512 * v:512 * v + 512], start=c == 0, stop=c == LC - 1)
                    last.then_inc(psum_full, 1)
                if k == 3:
                    pe.wait_ge(rooted, 1)
                    sum_squares(conv_summed, NCH, acc_conv, SSQ_BANK)
            pe.wait_ge(ulast_ready, 1)
            pe.transpose(claim(pe, "ulast")[0:32, 0:P], small[:, 0:32], ident).then_inc(psum_full, 1)

            def queries_and_keys(p):
                wait_weights(W_PAIR + p)
                wq = wslot(W_PAIR + p)[:, 0:1536].rearrange("p (c n) -> p c n", c=LC)
                wk = wslot(W_PAIR + p)[:, 1536:2560].rearrange("p (c n) -> p c n", c=LC)
                b = claim(pe, f"qr{p}")
                for c in range(LC):
                    for i in range(2):
                        last = pe.matmul(b[64 * i:64 * i + 64, 0:T], wq[:, c, QKD * i + NOPE:QKD * (i + 1)], cq[:, c, :],
                                         start=c == 0, stop=c == LC - 1)
                last.then_inc(psum_full, 1)
                for i in range(2):
                    b = claim(pe, f"q{2 * p + i}")
                    for c in range(LC):
                        last = pe.matmul(b[:, 0:T], wq[:, c, QKD * i:QKD * i + NOPE], cq[:, c, :], start=c == 0, stop=c == LC - 1)
                    last.then_inc(psum_full, 1)
                for i in range(2):
                    for s, (k0, kn) in enumerate(((0, 256), (256, 320))):
                        b = claim(pe, f"K{2 * p + i}_{s}")
                        for c in range(LC):
                            last = pe.matmul(b[:, 0:kn], wk[:, c, NOPE * i:NOPE * (i + 1)], ckv[:, c, k0:k0 + kn], start=c == 0, stop=c == LC - 1)
                        last.then_inc(psum_full, 1)
                        if i == s == 0:
                            pe.wait_ge(drained["act"], drain_count[f"qr{p}"])
                            pe.matmul(claim(pe, f"qrot{p}")[:, 0:T], const[:, C_ROT:C_ROT + P], qraw, start=True, stop=True).then_inc(psum_full, 1)

            def scores(h):
                p, i = h // 2, h % 2
                q, k = qt[:, p % 2], kt[:, p % 2]
                pe.wait_ge(q_ready, p + 1)
                pe.wait_ge(drained["dve"], drain_count[f"K{h}_1"])
                pe.wait_ge(drained["act"], drain_count[f"q{h}"])

                def score(out, t0, tn, k0, kn):
                    pe.matmul(out, q[:, i, t0:t0 + tn], k[:, i, k0:k0 + kn], start=True, stop=False)
                    return pe.matmul(out, q[64 * i:64 * i + 64, 2, t0:t0 + tn], krt[64 * i:64 * i + 64, k0:k0 + kn], start=False, stop=True)

                b = claim(pe, f"S{h}a")
                score(b[:, 0:128], 0, 128, 0, 128)
                score(b[:, 128:384], 128, 128, 0, 256).then_inc(psum_full, 1)
                b = claim(pe, f"S{h}b")
                score(b[0:64, 0:320], 256, 64, 256, 320).then_inc(psum_full, 1)

            def probabilities_T(h):
                pe.wait_ge(p_ready, h + 1)
                b, pr = claim(pe, f"PT{h}a"), pb[h % 2]
                for k in range(3):
                    last = pe.transpose(b[:, P * k:P * (k + 1)], pr[:, P * k:P * (k + 1)], ident)
                last.then_inc(psum_full, 1)
                b = claim(pe, f"PT{h}b")
                for k in range(3):
                    kn = KT[2 + k][1]
                    last = pe.transpose(b[0:kn, 64 * k:64 * k + 64], pr[0:64, 384 + P * k:384 + P * k + kn], ident[0:64, 0:64])
                last.then_inc(psum_full, 1)

            def attend(h):
                b, pt = claim(pe, f"PV{h}"), ptb[h % 2]
                pe.wait_ge(drained["dve"], drain_count[f"PT{h}b"])
                v = vals[:, :, VD * h:VD * (h + 1)]
                pe.matmul(b[:, 0:128], v[:, 0, :], pt[:, 0:128], start=True, stop=True)
                for k in range(2):
                    pe.matmul(b[:, 128:256], v[:, k, :], pt[:, 128 * (k + 1):128 * (k + 2)], start=k == 0, stop=k == 1)
                for k in range(3):
                    kn = KT[2 + k][1]
                    last = pe.matmul(b[:, 256:320], v[0:kn, 2 + k, :], pt[0:kn, 384 + 64 * k:448 + 64 * k], start=k == 0, stop=k == 2)
                last.then_inc(psum_full, 1)

            pe.wait_ge(normed, 2 * LC)
            pe.wait_ge(kr_ready, 1)
            pe.wait_ge(drained["act"], drain_count["ckr"])
            queries_and_keys(0)
            for p in range(H // 2):
                scores(2 * p)
                scores(2 * p + 1)
                if p + 1 < H // 2:
                    queries_and_keys(p + 1)
                for h in (2 * p, 2 * p + 1):
                    probabilities_T(h)
                for h in (2 * p, 2 * p + 1):
                    attend(h)

            def output(n):
                b = [claim(pe, f"wo{n}_{i}") for i in range(3)]
                for half in range(2):
                    wait_weights(W_O + 2 * n + half)
                    w = wslot(W_O + 2 * n + half).rearrange("p (c n) -> p c n", c=8)
                    if n == 0 and half == 0:
                        pe.wait_ge(m_lo_ready, NCH)
                    for j in range(8):
                        c = 8 * (1 - half) + j
                        v = 8 * n + 4 * half + j // 2
                        if n == half == 0 and j == 4:
                            pe.wait_ge(rooted, 3)
                            sum_squares(heads_summed, H, acc_att, SSQ_BANK)
                        if n == 0 and half == 1 and j % 2 == 0:
                            pe.wait_ge(m_lo_ready, NCH + j + 2)
                        if j % 2 == 0:
                            pe.wait_ge(o_lo_ready, v + 1)
                        first, final = half == 0 and j == 0, half == 1 and j == 7
                        for i in range(2):
                            rows = slice(P * i, P * (i + 1))
                            hi, lo = o_hi[:, v % 4, j % 2, :], o_lo[:, v % 4, j % 2, :]
                            pe.matmul(b[i], m_hi[:, c, rows], hi, start=first, stop=False)
                            pe.matmul(b[i], m_hi[:, c, rows], lo, start=False, stop=False)
                            last = pe.matmul(b[i], m_lo[:, c, rows], hi, start=False, stop=final)
                            if final:
                                last.then_inc(psum_full, 1)
                        if j % 2 and not final:
                            last.then_inc(o_used, 1)
                        if j % 2:
                            for k in range(2):
                                last = pe.matmul(b[2][64 * k:64 * k + 64, :], mix[:, c - 1 + k, 256:320], w[:, j - 1 + k, :],
                                                 start=half == 0 and j == 1, stop=final)
                            if final:
                                last.then_inc(psum_full, 1)
                            elif j == 7:
                                last.then_inc(wo_half_used, 1)

            def router_transpose(n, i):
                tn = TILES[i][1]
                pe.wait_ge(hg_ready, 3 * n + i + 1)
                b = claim(pe, f"rt{n}_{i}")
                for c in range(4):
                    last = pe.transpose(b[:, c * tn:(c + 1) * tn], xn[0:tn, i, 4 * n + c, :], ident[0:tn, 0:tn])
                last.then_inc(psum_full, 1)

            def router_logits(n, i):
                tn = TILES[i][1]
                pe.wait_ge(drained["act"], drain_count[f"rt{n}_{i}"])
                for c in range(4):
                    last = pe.matmul(ps[0:tn, ACC_BANK, 36 * i:36 * i + 36], rtb[(3 * n + i) % 2][:, c, 0:tn], wr[:, 4 * n + c, :],
                                     start=n == 0 and i == 0 and c == 0, stop=n == 3 and c == 3, skip_group_check=True)
                last.then_inc(logits_full, 1)

            def router(n):
                router_transpose(n, 0)
                router_transpose(n, 1)
                router_logits(n, 0)
                router_transpose(n, 2)
                router_logits(n, 1)
                router_logits(n, 2)

            for n in range(4):
                output(n)
                if n == 0:
                    pe.wait_ge(s_router, 160)
                    pe.wait_ge(rooted, 2)
                else:
                    router(n - 1)
            router(3)

            def keep_clock(count, b):
                for _ in range(count):
                    pe.matmul(ps[:, b, :], ident, const[:, 0:512], start=True, stop=True)

            keep_clock(4, SSQ_BANK)
            pe.wait_ge(hot_ready, 1)
            tri = const[:, C_TRI:C_TRI + P]
            b = ps[:, SSQ_BANK, :]
            pe.matmul(b[:, 0:32], tri, hot2[:, 0, :], start=True, stop=True)
            pe.matmul(b[:, 32:64], ones[:, :], hot2[:, 0, :], start=True, stop=False)
            pe.matmul(b[:, 32:64], tri, hot2[:, 1, :], start=False, stop=True)
            pe.matmul(b[0:64, 64:96], ones[:, 0:64], hot2[:, 0, :], start=True, stop=False)
            pe.matmul(b[0:64, 64:96], ones[:, 0:64], hot2[:, 1, :], start=False, stop=False)
            pe.matmul(b[0:64, 64:96], tri[0:64, 0:64], hot2[0:64, 2, :], start=False, stop=True).then_inc(route_pe, 1)
            for i, (t0, tn) in enumerate(TILES):
                last = pe.matmul(ps[:, ACC_BANK, 0:NE], ones[0:tn, :], hot2[0:tn, i, :], start=i == 0, stop=i == 2)
            last.then_inc(route_pe, 1)

            def gather(pk, cols, signal):
                for i, (t0, tn) in enumerate(TILES):
                    for j in range(4):
                        last = pe.matmul(ps[B * j:B * (j + 1), 0, :], pk[0:tn, i, cols],
                                         xn[0:tn, i, 4 * j:4 * j + 4, :].rearrange("t c q -> t (c q)"), start=i == 0, stop=i == 2)
                last.then_inc(signal, 1)

            def gathered_T(signal):
                for c in range(4):
                    last = pe.transpose(ps[:, 1, P * c:P * (c + 1)], gsb[:, P * c:P * (c + 1)], ident)
                last.then_inc(signal, 1)

            def gates_T(src, width, signal):
                for i, (t0, tn) in enumerate(TILES):
                    last = pe.transpose(ps[0:width, 0, t0:t0 + tn], src[0:tn, i, :], ident[0:tn, 0:tn])
                last.then_inc(signal, 1)

            def gate_up(x, s):
                w = ring[:, s, :].rearrange("p (m c n) -> p m c n", m=2, c=4)
                for c in (0, 2):
                    for m in range(2):
                        for o in range(2):
                            r = B * (2 * m + o)
                            last = pe.matmul(ps[r:r + B, 2, :], x[:, c + o, s, :], w[:, m, c + o, :],
                                             start=s == 0 and c == 0, stop=s == 3 and c == 2)
                return last

            def fold(signal):
                for c in range(4):
                    last = pe.matmul(ps[:, 3, 64 * c:64 * c + 64], hsb[:, c, :], const[:, C_FOLD:C_FOLD + 64], start=True, stop=True)
                last.then_inc(signal, 1)

            def down(s):
                w = ring[:, s, :].rearrange("p (c n) -> p c n", c=2)
                for c in range(2):
                    for j in range(4):
                        last = pe.matmul(ps[B * j:B * (j + 1), 4, :], hT[:, 2 * (s - 4) + c, :], w[:, c, 512 * j:512 * j + 512],
                                         start=s == 4 and c == 0, stop=s == 5 and c == 1)
                return last

            def combine(parts, full_sem, free_sem, value):
                for u in range(12):
                    i, n = u // 4, u % 4
                    t0, tn = TILES[i]
                    if u >= 3:
                        pe.wait_ge(free_sem, value(u - 2))
                    gates, rows = parts(n)
                    pe.matmul(ps[0:tn, 5 + u % 3, :], gates[:, t0:t0 + tn], rows, start=True, stop=True).then_inc(full_sem, 1)

            def extra_blocks(q, comb_before, e):
                count = pe.value_load(tables[0:1, 1, bass.ds(e, 1)], min_val=1, max_val=MAXB)
                with pe.If(count > 1):
                    before = pe.value_load(tables[0:1, 0, bass.ds(e, 1)], min_val=0, max_val=64)
                    with pe.Fori(1, count) as k:
                        x = before + k
                        pe.wait_ge(x_pick, x)
                        pe.wait_ge(gt_copied, q + 1)
                        gather(pickrx, slice(0, B), x_gathered)
                        pe.wait_ge(x_copied, x)
                        pe.wait_ge(xg_ready, e + 2)
                        gathered_T(x_transposed)
                        pe.wait_ge(x_gates, x)
                        gates_T(gpickx, P, x_gtfull)
                        pe.wait_ge(x_ready, x)
                        for s in range(4):
                            gate_up(xx, s).then_inc(extra_used[s], 1)
                        pe.wait_ge(x_hcopied, x)
                        fold(x_folded)
                        pe.wait_ge(x_hT, x)
                        pe.wait_ge(y_copied, e + 1)
                        for s in (4, 5):
                            down(s).then_inc(extra_used[s], 1)
                        pe.wait_ge(x_ycopied, x)
                        pe.wait_ge(x_gtcopied, x)
                        pe.wait_ge(comb_added, comb_before)
                        pe.wait_ge(x_added, x * 12)
                        combine(lambda n: (gTx[B * n:B * (n + 1), :], yx[B * n:B * (n + 1), :]), x_full, x_added, lambda v: x * 12 + v)

            for s in range(SLOTS):
                pe.sem_inc(extra_used[s], 1)
            keep_clock(3, 5)
            pe.wait_ge(pick_ready, 1)
            gather(pickr, slice(0, B), gathered)
            pe.wait_ge(g_copied, 1)
            gathered_T(transposed)
            pe.wait_ge(routed, 3)
            with pe.Fori(0, NE // 4) as q:
                comb_before = q * 12 + 1
                for b in range(4):
                    e = q * 4 + b
                    pe.wait_ge(xg_ready, e + 1)
                    for s in range(4):
                        pe.wait_ge(slot_full[s], e * 32 + expert_count(s))
                        gate_up(xg, s).then_inc(weights_used, 1)
                    if b == 3:
                        pe.wait_ge(pick_ready, q + 2)
                    cols = slice(B * ((b + 1) % 4), B * ((b + 1) % 4) + B)
                    if b == 1:
                        pe.wait_ge(gt_copied, q + 1)
                    gather(pickr, cols, gathered)
                    pe.wait_ge(h_copied, e + 1)
                    fold(folded)
                    pe.wait_ge(g_copied, e + 2)
                    gathered_T(transposed)
                    if b == 0:
                        pe.wait_ge(gates_ready, q + 1)
                        gates_T(gpick, P, gt_full)
                    pe.wait_ge(hT_ready, e + 1)
                    for s in (4, 5):
                        pe.wait_ge(slot_full[s], e * 32 + expert_count(s))
                        if s == 4 and b:
                            pe.wait_ge(y_copied, e)
                        down(s).then_inc(weights_used, 1)
                    extra_blocks(q, comb_before, e)
                pe.wait_ge(y_copied, q * 4 + 4)
                pe.wait_ge(comb_added, comb_before)
                drained_extra = pe.value_load(tables[0:1, 2, bass.ds(q * 4 + 3, 1)], min_val=12, max_val=12 * 64)
                pe.wait_ge(x_added, drained_extra)
                combine(lambda n: (gT, yg[:, 512 * n:512 * n + 512]), comb_full, comb_added, lambda v: q * 12 + (v + 1))

        @block.scalar
        def _(act):
            def drain(name, ins):
                ins.then_inc(drained["act"], 1)

            loads = ((P_MIX, a["norm_mix"], 16), (P_Q, a["norm_q"], 4), (P_KV, a["norm_kv"], 4),
                     (P_AO, a["norm_attn_out"], 8))
            for first, src, n in loads:
                act.dma_start(par_rows[first:first + n, :], src.rearrange("a (c p) -> (a c) p", p=P)).then_inc(s_par, 16)
            act.wait_ge(s_ones, 2)
            act.activation(small[:, 63:64], eps_col, ACT.Sqrt)
            for i, (t0, tn) in enumerate(TILES):
                act.wait_ge(s_x[i], 16)
                act.activation(xnorm[i][0:tn, :], xtile[0:tn, i, :], ACT.Square, accum_out=xss[0:tn, i:i + 1]).then_inc(x_squared, 1)
                act.wait_ge(x_squared, i + 1)
                act.activation(xsd[0:tn, i:i + 1], xss[0:tn, i:i + 1], ACT.Sqrt, bias=eps_col[0:tn, :], scale=1.0 / D).then_inc(x_rooted, 1)

            act.wait_ge(psum_full, full("par"))
            drain("par", act.copy(par[:, :], bank("par")[:, 0:P_ALL]))

            def split_hi(u):
                if u >= len(splits):
                    return
                _, n, _, width = splits[u]
                act.wait_ge(slot_full[slot_of_item(n)], slot_count(n))
                if u >= 2:
                    act.wait_ge(psum_full, full(splits[u - 2][0]))
                for half in range(2):
                    act.copy(w_hi[:, u % 2, 8 * half:8 * half + 8, 0:width], w_raw(u, half)).then_inc(w_hi_ready, 1)

            for k in range(4):
                for i, (t0, tn) in enumerate(TILES):
                    act.wait_ge(drained["dve"], drain_count[f"xt{i}_{k}"])
                    act.copy(xT_hi[:, 4 * k:4 * k + 4, t0:t0 + tn], xT_raw[:, (3 * k + i) % 2, :, 0:tn]).then_inc(xT_hi_ready, 1)
                if k in (1, 3):
                    split_hi(k // 2)

            def root_of(which, src, width):
                act.activation(rs, src, ACT.Sqrt, bias=eps_col[:, :], scale=1.0 / width).then_inc(rooted, 1)

            def latent(name, dst, sqd):
                for m in range(LC):
                    split_hi(split_index[f"{name}{m}"] + 2)
                    if name == "ckv" and m == 3:
                        act.wait_ge(ssq_full, 1)
                        root_of("q", ps[:, SSQ_BANK, 0:T], QL)
                    act.wait_ge(psum_full, full(f"{name}{m}"))
                    act.copy(dst[:, m, 0:T], bank(f"{name}{m}")[:, 0:T])
                    drain("", act.activation(sqd[:, m, :], bank(f"{name}{m}")[:, 0:T], ACT.Square))

            latent("cq", cq, sq_q)
            latent("ckv", ckv, sq_kv)
            split_hi(split_index["kr"] + 2)
            act.wait_ge(psum_full, full("kr"))
            drain("kr", act.copy(kraw, bank("kr")[0:ROPE, 0:T]))
            for i in range(2):
                act.wait_ge(psum_full, full(f"cc{i}"))
                drain("cc", act.copy(ckv[:, :, T + P * i:T + P * (i + 1)], bank(f"cc{i}").rearrange("p (c k) -> p c k", c=LC)))
            act.wait_ge(psum_full, full("ckr"))
            drain("ckr", act.copy(krt[:, T:T + 256], bank("ckr")[:, 0:256]))
            def conv_square(c):
                act.wait_ge(drained["dve"], drain_count[f"B{c}"])
                if c >= 2:
                    act.wait_ge(conv_summed, c - 1)
                act.activation(sq[:, c % 2, :], mix[:, 8 + c, :], ACT.Square).then_inc(conv_squared, 1)

            for j in range(NCH // 2):
                for i in range(2):
                    split_hi(split_index[f"C{2 * j + i}"] + 2)
                    act.wait_ge(psum_full, full(f"C{2 * j + i}"))
                    if j:
                        act.wait_ge(drained["dve"], drain_count[f"h{2 * (j - 1) + i}"])
                    drain("C", act.copy(csb[:, i, :], bank(f"C{2 * j + i}")[:, 0:T]))
                    if j == i == 0:
                        act.wait_ge(ssq_full, 2)
                        act.wait_ge(normed, LC)
                        root_of("kv", ps[:, ACC_BANK, 0:T], KL)
                    if j:
                        conv_square(2 * (j - 1) + i)
                for name in "hB":
                    for i in range(2):
                        split_hi(split_index[f"{name}{2 * j + i}"] + 2)
                if j == 0:
                    for i, (t0, tn) in enumerate(TILES):
                        act.wait_ge(psum_full, full(f"okv{i}"))
                        drain("okv", act.copy(okv[0:tn, i, :], bank(f"okv{i}")[0:tn, :]))
                    act.wait_ge(psum_full, full("okr"))
                    act.copy(okr[:, 0:2, :], bank("okr")[:, 0:2 * ROPE].rearrange("p (i r) -> p i r", i=2))
                    drain("okr", act.copy(okr[0:64, 2, :], bank("okr")[0:64, 2 * ROPE:3 * ROPE]))
            for k, (k0, kn) in enumerate(KT):
                for v in range(2):
                    act.wait_ge(psum_full, full(f"V{k}_{v}"))
                    drain("V", act.copy(vals[0:kn, k, 512 * v:512 * v + 512], bank(f"V{k}_{v}")[0:kn, :]))
                if k < 1:
                    conv_square(NCH - 2)
                    conv_square(NCH - 1)
            act.wait_ge(ssq_full, 3)
            act.wait_ge(normed, 2 * LC)
            root_of("conv", ps[:, SSQ_BANK, 0:T], CH)
            act.wait_ge(psum_full, full("ulast"))
            drain("ulast", act.copy(oul, bank("ulast")[0:32, 0:P]))

            def queries(p):
                act.wait_ge(psum_full, full(f"qr{p}"))
                if p:
                    act.wait_ge(q_ready, p)
                drain("qr", act.copy(qraw, bank(f"qr{p}")[:, 0:T]))
                for i in range(2):
                    act.wait_ge(psum_full, full(f"q{2 * p + i}"))
                    drain("q", act.copy(qt[:, p % 2, i, :], bank(f"q{2 * p + i}")[:, 0:T]))

            def exps(h):
                i, pr = h % 2, pb[h % 2]
                a_, b_ = bank(f"S{h}a"), bank(f"S{h}b")
                act.wait_ge(max_ready, h + 1)
                if h >= 2:
                    act.wait_ge(psum_full, full(f"PT{h - 2}b"))

                def e(out, src, r0, rn, col):
                    return act.activation(out, src, ACT.Exp, bias=nb_[i][r0:r0 + rn, col:col + 1], scale=SCALE,
                                          accum_out=sm[i][r0:r0 + rn, col:col + 1])
                e(pr[0:64, 0:64], a_[0:64, 0:64], 0, 64, 0)
                e(pr[64:128, 0:128], a_[64:128, 0:128], 64, 64, 0)
                e(pr[0:64, 128:320], a_[0:64, 128:320], 0, 64, 1)
                drain("Sa", e(pr[64:128, 128:384], a_[64:128, 128:384], 64, 64, 1))
                drain("Sb", e(pr[0:64, 384:704], b_[0:64, 0:320], 0, 64, 2))

            def head_out(h):
                if h == 0:
                    act.wait_ge(s_out, 64)
                act.wait_ge(psum_full, full(f"PV{h}"))
                b = bank(f"PV{h}")
                act.copy(mix[:, h, :], b[:, 0:T])
                if h >= 2:
                    act.wait_ge(heads_summed, h - 1)
                drain("PV", act.activation(sq[:, h % 2, :], b[:, 0:T], ACT.Square))

            def mix_hi(c):
                act.copy(m_hi[:, c, :], mix[:, c, 0:SEQ]).then_inc(m_hi_ready, 1)

            def w_o_hi(first, end):
                for v in range(first, end):
                    act.wait_ge(slot_full[slot_of_item(W_O + v // 4)], slot_count(W_O + v // 4))
                    if v >= 4:
                        wait_pair_used(act, v - 4)
                    act.copy(o_hi[:, v % 4], o_raw(v)).then_inc(o_hi_ready, 1)

            queries(0)
            for p in range(H // 2):
                exps(2 * p)
                exps(2 * p + 1)
                if p == 0:
                    act.wait_ge(normed, 2 * LC + NCH)
                if p + 1 < H // 2:
                    queries(p + 1)
                mix_hi(NCH + 2 * p)
                mix_hi(NCH + 2 * p + 1)
                if p in (1, 2):
                    w_o_hi(2 * p - 2, 2 * p)
                head_out(2 * p)
                head_out(2 * p + 1)
            act.wait_ge(ssq_full, 4)
            act.wait_ge(normed, 16)
            root_of("attn", ps[:, SSQ_BANK, 0:T], H * VD)
            for p in range(H // 2):
                w_o_hi(4 + p, 5 + p)
                for h in (2 * p, 2 * p + 1):
                    act.wait_ge(normed, 16 + h + 1)
                    mix_hi(h)

            def squares(n):
                for i, (t0, tn) in enumerate(TILES):
                    act.wait_ge(drained["dve"], drain_count[f"wo{n}_{i}"])
                    if n or i:
                        act.wait_ge(h_squared, 3 * n + i)
                    act.activation(junk[0:tn, :], xtile[0:tn, i, 512 * n:512 * n + 512], ACT.Square,
                                   accum_out=hss[0:tn, i, n:n + 1]).then_inc(h_squared, 1)

            def router_copies(n):
                for i, (t0, tn) in enumerate(TILES):
                    act.wait_ge(psum_full, full(f"rt{n}_{i}"))
                    u = 3 * n + i
                    if u >= 2:
                        act.wait_ge(logits_full, u - 1)
                    drain("rt", act.copy(rtb[u % 2][:, :, 0:tn], bank(f"rt{n}_{i}")[:, 0:4 * tn].rearrange("p (c t) -> p c t", c=4)))

            for n in range(1, 4):
                w_o_hi(8 * n + (3 if n > 1 else 0), 8 * n + 4)
                squares(n - 1)
                w_o_hi(8 * n + 4, min(8 * n + 11, 32))
                router_copies(n - 1)
            squares(3)
            router_copies(3)
            act.wait_ge(route_in, 1)
            act.activation(hsd, hsum, ACT.Sqrt, bias=eps_col[:, :], scale=1.0 / D).then_inc(route_act, 1)
            act.wait_ge(route_in, 2)
            act.activation(gx, gx, ACT.Exp).then_inc(route_act, 1)
            act.wait_ge(route_in, 3)
            act.activation(ev, dv, ACT.Exp).then_inc(route_act, 1)

            def copy_gathered(src_full, value, signal):
                act.wait_ge(src_full, value)
                act.copy(gsb, ps[:, 0, :]).then_inc(signal, 1)

            def copy_xT(dst, src_full, value, signal):
                act.wait_ge(src_full, value)
                act.copy(dst.rearrange("p c j s -> p (c j s)"), ps[:, 1, :]).then_inc(signal, 1)

            def copy_gate_up(signal):
                act.copy(hsb.rearrange("p c q -> p q c"), ps[:, 2, :].rearrange("p (q c) -> p q c", c=4)).then_inc(signal, 1)

            def silu(signal):
                act.activation(sil, ps[:, 3, 0:256].rearrange("p (c m s) -> p c m s", c=4, m=2)[:, :, 0, :], ACT.Silu).then_inc(signal, 1)

            def copy_result(rows, signal):
                for j in range(4):
                    last = act.copy(rows[j], ps[B * j:B * (j + 1), 4, :])
                last.then_inc(signal, 1)

            def extra_blocks(e):
                count = act.value_load(tables[0:1, 1, bass.ds(e, 1)], min_val=1, max_val=MAXB)
                with act.If(count > 1):
                    before = act.value_load(tables[0:1, 0, bass.ds(e, 1)], min_val=0, max_val=64)
                    with act.Fori(1, count) as k:
                        x = before + k
                        copy_gathered(x_gathered, x, x_copied)
                        copy_xT(xx, x_transposed, x, x_ready)
                        act.wait_ge(x_gtfull, x)
                        act.wait_ge(x_added, x * 12)
                        act.copy(gTx, ps[:, 0, 0:T]).then_inc(x_gtcopied, 1)
                        act.wait_ge(extra_used[3], x + 1)
                        copy_gate_up(x_hcopied)
                        act.wait_ge(x_folded, x)
                        silu(x_silu)
                        act.wait_ge(extra_used[5], x + 1)
                        act.copy(yx, ps[:, 4, :]).then_inc(x_ycopied, 1)

            copy_gathered(gathered, 1, g_copied)
            copy_xT(xg, transposed, 1, xg_ready)
            act.wait_ge(routed, 3)
            with act.Fori(0, NE // 4) as q:
                for b in range(4):
                    e = q * 4 + b
                    act.wait_ge(weights_used, e * 6 + 4)
                    copy_gate_up(h_copied)
                    copy_gathered(gathered, e + 2, g_copied)
                    act.wait_ge(folded, e + 1)
                    silu(silu_ready)
                    copy_xT(xg, transposed, e + 2, xg_ready)
                    if b == 0:
                        act.wait_ge(gt_full, q + 1)
                        act.wait_ge(comb_added, q * 12 + 1)
                        act.copy(gT, ps[:, 0, 0:T]).then_inc(gt_copied, 1)
                    act.wait_ge(weights_used, e * 6 + 6)
                    copy_result([yg[B * b:B * (b + 1), 512 * j:512 * j + 512] for j in range(4)], y_copied)
                    extra_blocks(e)

            used = act.value_load(tables[0:1, 2, NE - 1:NE], min_val=12, max_val=12 * 64)
            act.wait_ge(x_added, used)
            for i, (t0, tn) in enumerate(TILES):
                act.wait_ge(comb_added, 12 * (NE // 4 - 1) + 4 * (i + 1) + 1)
                act.activation(r2[0:tn, D * i:D * (i + 1)], xtile[0:tn, i, :], ACT.Square, accum_out=xss[0:tn, i:i + 1]).then_inc(fin_squared, 1)
                act.wait_ge(fin_squared, i + 1)
                act.activation(xsd[0:tn, i:i + 1], xss[0:tn, i:i + 1], ACT.Sqrt, bias=eps_col[0:tn, :], scale=1.0 / D).then_inc(fin_rooted, 1)

        @block.vector
        def _(dve):
            step = [0]

            def link(ins):
                step[0] += 1
                ins.then_inc(dve_step, 1)
                dve.wait_ge(dve_step, step[0])

            def drain(name, ins):
                ins.then_inc(drained["dve"], 1)

            dve.memset(ones[:, :], 1.0).then_inc(s_ones, 1)
            dve.memset(eps_col, EPS).then_inc(s_ones, 1)

            def scale_x(i):
                tn = TILES[i][1]
                dve.wait_ge(x_rooted, i + 1)
                link(dve.reciprocal(xrs[0:tn, i:i + 1], xsd[0:tn, i:i + 1]))
                dve.tensor_scalar(xnorm[i][0:tn, :], xtile[0:tn, i, :], xrs[0:tn, i:i + 1], None, ALU.mult).then_inc(x_scaled, 1)

            def xT_low(v):
                k, i = v // 3, v % 3
                t0, tn = TILES[i]
                dve.wait_ge(xT_hi_ready, v + 1)
                dve.tensor_tensor(xT_lo[:, 4 * k:4 * k + 4, t0:t0 + tn], xT_raw[:, v % 2, :, 0:tn],
                                  xT_hi[:, 4 * k:4 * k + 4, t0:t0 + tn].bitcast(F32), ALU.subtract).then_inc(xT_lo_ready, 1)

            def xT_jobs(first, end):
                for v in range(first, end):
                    k, i = v // 3, v % 3
                    tn = TILES[i][1]
                    if v >= 2:
                        dve.wait_ge(xT_lo_ready, v - 1)
                    dve.wait_ge(psum_full, full(f"xt{i}_{k}"))
                    drain("xt", dve.tensor_tensor(
                        xT_raw[:, v % 2, :, 0:tn], bank(f"xt{i}_{k}")[:, 0:4 * tn].rearrange("p (c t) -> p c t", c=4),
                        par[:, P_MIX + 4 * k:P_MIX + 4 * k + 4].unsqueeze(2).to_broadcast([P, 4, tn]), ALU.mult))
                    if v:
                        xT_low(v - 1)

            def split_lo(u):
                if u >= len(splits):
                    return
                width = splits[u][3]
                for half in range(2):
                    dve.wait_ge(w_hi_ready, 2 * u + half + 1)
                    f = slice(8 * half, 8 * half + 8)
                    dve.tensor_tensor(w_lo[:, u % 2, f, 0:width], w_raw(u, half), w_hi[:, u % 2, f, 0:width].bitcast(F32),
                                      ALU.subtract).then_inc(w_lo_ready, 1)

            scale_x(0)
            scale_x(1)
            scale_x(2)
            dve.wait_ge(drained["act"], drain_count["par"])
            xT_jobs(0, 6)
            split_lo(0)
            xT_jobs(6, 12)
            xT_low(11)
            for u in range(1, split_index["kr"] + 1):
                split_lo(u)

            def scale_chunks(which, chunks, gains):
                dve.wait_ge(rooted, which)
                link(dve.reciprocal(rs, rs))
                for m, dst in enumerate(chunks):
                    dve.scalar_tensor_tensor(dst, dst, par[:, gains + m:gains + m + 1], rs, ALU.mult, ALU.mult).then_inc(normed, 1)

            def rotate(out, plain, swapped, a_, b_, name):
                if name == "krrot":
                    dve.wait_ge(psum_full, full("krdup"))
                    drain("krdup", dve.tensor_tensor(a_, plain, cos, ALU.mult))
                else:
                    link(dve.tensor_tensor(a_, plain, cos, ALU.mult))
                dve.wait_ge(psum_full, full(name))
                drain(name, dve.tensor_tensor(b_, swapped, sin, ALU.mult))
                dve.wait_ge(drained["dve"], drain_count[name])
                return dve.tensor_tensor(out, a_, b_, ALU.add)

            scale_chunks(1, [cq[:, m, :] for m in range(LC)], P_Q)
            split_lo(split_index["C0"])
            split_lo(split_index["C1"])
            rotate(krt[:, 0:T], bank("krdup")[:, 0:T], bank("krrot")[:, 0:T], rot_a, rot_b, "krrot").then_inc(kr_ready, 1)
            split_lo(split_index["h0"])
            scale_chunks(2, [ckv[:, m, 0:T] for m in range(LC)], P_KV)
            split_lo(split_index["h1"])

            link(dve.memset(uext[:, :, 0:2], 0.0))
            for k in range(2):
                link(dve.tensor_copy(uext[:, :, SEQ + 2 + k], par[:, P_ST + NCH * k:P_ST + NCH * (k + 1)]))

            def conv_input(c):
                dve.wait_ge(psum_full, full(f"h{c}"))
                dve.wait_ge(drained["act"], drain_count[f"C{c}"])
                b = bank(f"h{c}")
                link(dve.tensor_tensor(uext[:, c, 2:SEQ + 2], b[:, 0:SEQ], csb[:, c % 2, 0:SEQ], ALU.mult))
                drain("h", dve.tensor_tensor(uext[:, c, SEQ + 4:UE], b[:, SEQ:T], csb[:, c % 2, SEQ:T], ALU.mult))
                dve.wait_ge(drained["dve"], drain_count[f"h{c}"])

            def conv(c):
                tap = [par[:, P_CONV + NCH * j + c:P_CONV + NCH * j + c + 1] for j in range(3)]
                link(dve.tensor_scalar(cv, uext[:, c, 2:UE], tap[2], None, ALU.mult))
                for j in (1, 0):
                    link(dve.scalar_tensor_tensor(cv, uext[:, c, j:j + UE - 2], tap[j], cv, ALU.mult, ALU.add))
                dve.wait_ge(psum_full, full(f"B{c}"))
                b = bank(f"B{c}")
                link(dve.tensor_tensor(mix[:, 8 + c, 0:SEQ], b[:, 0:SEQ], cv[:, 0:SEQ], ALU.mult))
                drain("B", dve.tensor_tensor(mix[:, 8 + c, SEQ:T], b[:, SEQ:T], cv[:, SEQ + 2:UE - 2], ALU.mult))
                dve.wait_ge(drained["dve"], drain_count[f"B{c}"])

            for j in range(NCH // 2):
                if j:
                    for c in (2 * j, 2 * j + 1):
                        split_lo(split_index[f"C{c}"] + 2)
                for c in (2 * j, 2 * j + 1):
                    split_lo(split_index[f"h{c}"] + 2)
                    conv_input(c)
                for c in (2 * j, 2 * j + 1):
                    split_lo(split_index[f"B{c}"] + 2)
                    conv(c)
            link(dve.tensor_copy(ulast[:, 0:2, :], uext[:, :, SEQ:SEQ + 2].rearrange("p c k -> p k c")))
            dve.tensor_copy(ulast[:, 2:4, :], uext[:, :, UE - 2:UE].rearrange("p c k -> p k c")).then_inc(ulast_ready, 1)
            dve.wait_ge(ulast_ready, 1)
            for k in range(2):
                link(dve.memset(pb[k][0:64, 64:128], 0.0))
                link(dve.memset(pb[k][0:64, 320:384], 0.0))
                link(dve.memset(mx[k], 0.0))
                link(dve.memset(sm[k], 1.0))
            scale_chunks(3, [mix[:, 8 + c, :] for c in range(NCH)], P_CO)

            def keys(p):
                for i in range(2):
                    for s, (k0, kn) in enumerate(((0, 256), (256, 320))):
                        name = f"K{2 * p + i}_{s}"
                        dve.wait_ge(psum_full, full(name))
                        drain(name, dve.tensor_copy(kt[:, p % 2, i, k0:k0 + kn], bank(name)[:, 0:kn]))
                        if i == s == 0:
                            dve.wait_ge(drained["act"], drain_count[f"qr{p}"])
                            rotate(qt[:, p % 2, 2, :], qraw, bank(f"qrot{p}")[:, 0:T], att_a, att_b, f"qrot{p}").then_inc(q_ready, 1)

            def mix_low(v):
                c = (v + NCH) % KC
                dve.wait_ge(m_hi_ready, v + 1)
                dve.tensor_tensor(m_lo[:, c, 0:SEQ], mix[:, c, 0:SEQ], m_hi[:, c, :].bitcast(F32), ALU.subtract).then_inc(m_lo_ready, 1)

            def w_o_low(first, end):
                for v in range(first, end):
                    dve.wait_ge(o_hi_ready, v + 1)
                    dve.tensor_tensor(o_lo[:, v % 4], o_raw(v), o_hi[:, v % 4].bitcast(F32), ALU.subtract).then_inc(o_lo_ready, 1)

            def maxima(h):
                i = h % 2
                a_, b_ = bank(f"S{h}a"), bank(f"S{h}b")
                dve.wait_ge(psum_full, full(f"S{h}b"))
                for out, src in ((mx[i][0:64, 0:1], a_[0:64, 0:64]), (mx[i][64:128, 0:1], a_[64:128, 0:128]),
                                 (mx[i][0:64, 1:2], a_[0:64, 128:320]), (mx[i][64:128, 1:2], a_[64:128, 128:384])):
                    dve.tensor_reduce(out, src, AX, ALU.max)
                link(dve.tensor_reduce(mx[i][0:64, 2:3], b_[0:64, 0:320], AX, ALU.max))
                dve.tensor_scalar(nb_[i], mx[i], -SCALE, None, ALU.mult).then_inc(max_ready, 1)

            def normalise(h):
                i, pr = h % 2, pb[h % 2]
                dve.wait_ge(drained["act"], drain_count[f"S{h}b"])
                link(dve.reciprocal(sm[i], sm[i]))
                dve.tensor_scalar(pr[:, 0:128], pr[:, 0:128], sm[i][:, 0:1], None, ALU.mult)
                dve.tensor_scalar(pr[:, 128:384], pr[:, 128:384], sm[i][:, 1:2], None, ALU.mult)
                dve.tensor_scalar(pr[0:64, 384:704], pr[0:64, 384:704], sm[i][0:64, 2:3], None, ALU.mult).then_inc(p_ready, 1)

            def probs_T(h):
                pt = ptb[h % 2]
                dve.wait_ge(psum_full, full(f"PT{h}a"))
                drain("PTa", dve.tensor_copy(pt[:, 0:384], bank(f"PT{h}a")[:, 0:384]))
                dve.wait_ge(psum_full, full(f"PT{h}b"))
                dve.tensor_copy(pt[:, 384:512], bank(f"PT{h}b")[:, 0:128])
                drain("PTb", dve.tensor_copy(pt[0:64, 512:576], bank(f"PT{h}b")[0:64, 128:192]))

            keys(0)
            for p in range(H // 2):
                for h in (2 * p, 2 * p + 1):
                    maxima(h)
                for h in (2 * p, 2 * p + 1):
                    normalise(h)
                if p + 1 < H // 2:
                    keys(p + 1)
                for h in (2 * p, 2 * p + 1):
                    probs_T(h)
                mix_low(2 * p)
                mix_low(2 * p + 1)
                if p in (1, 2):
                    w_o_low(2 * p - 2, 2 * p)
            scale_chunks(4, [mix[:, h, :] for h in range(H)], P_AO)
            for p in range(H // 2):
                w_o_low(4 + p, 5 + p)
                mix_low(NCH + 2 * p)
                mix_low(NCH + 2 * p + 1)

            dve.wait_ge(psum_full, full(f"PV{H - 1}"))
            link(dve.memset(work[:, 1024:2560], 0.0))
            dve.wait_ge(s_xagain, 48)
            dve.wait_ge(s_gffn, 16)
            for n in range(4):
                f = slice(512 * n, 512 * n + 512)
                w_o_low(8 * n + (3 if n else 8), min(8 * n + 11, 32))
                for i, (t0, tn) in enumerate(TILES):
                    name = f"wo{n}_{i}"
                    dve.wait_ge(psum_full, full(name))
                    h, b = xtile[0:tn, i, f], bank(name)
                    if i < 2:
                        drain(name, dve.tensor_tensor(h, b, h, ALU.add))
                    else:
                        link(dve.tensor_tensor(h, b[0:64, :], h, ALU.add))
                        drain(name, dve.tensor_tensor(h, b[64:128, :], h, ALU.add))
                    dve.wait_ge(drained["dve"], drain_count[name])
                    dve.tensor_tensor(xn[0:tn, i, 4 * n:4 * n + 4, :].rearrange("t c q -> t q c"),
                                      h.rearrange("t (q c) -> t q c", c=4), gain[0:tn, f].rearrange("t (q c) -> t q c", c=4),
                                      ALU.mult).then_inc(hg_ready, 1)

            dve.wait_ge(h_squared, 12)
            dve.tensor_reduce(hsum, hss, AX, ALU.add).then_inc(route_in, 1)
            dve.wait_ge(route_act, 1)
            link(dve.reciprocal(hrs, hsd))
            link(dve.memset(lg, NEG))
            dve.wait_ge(logits_full, 12)
            for i, (t0, tn) in enumerate(TILES):
                b = ps[0:tn, ACC_BANK, 36 * i:36 * i + 36]
                for dst, c0, cn in ((lg, 0, G), (le, G, NE)):
                    last = dve.scalar_tensor_tensor(dst[0:tn, i, 0:cn], b[:, c0:c0 + cn], hrs[0:tn, i:i + 1],
                                                    brow[0:tn, c0:c0 + cn], ALU.mult, ALU.add)
            link(last)
            for i in range(3):
                last = dve.max(m8[:, i, :], lg[:, i, :])
            link(last)
            for i in range(3):
                last = dve.max_index(i8[:, 0, i, :], m8[:, i, :], lg[:, i, :])
            link(last)
            dve.tensor_tensor(gx, lg[:, :, 0:G], m8[:, :, 0:1].to_broadcast([P, 3, G]), ALU.subtract).then_inc(route_in, 1)
            link(dve.tensor_copy(gidx, i8[:, 0, :, 0]))
            iota = const[:, C_IOTA:C_IOTA + NE]
            link(dve.tensor_tensor(ghot, iota[:, 0:G].unsqueeze(1).to_broadcast([P, 3, G]),
                                   gidx.unsqueeze(2).to_broadcast([P, 3, G]), ALU.is_equal))
            gsel = prod_flat[:, 0:96].rearrange("p (i g e) -> p i g e", i=3, g=G)
            link(dve.tensor_tensor(gsel, le.rearrange("p i (g e) -> p i g e", g=G),
                                   ghot.unsqueeze(3).to_broadcast([P, 3, G, EPG]), ALU.mult))
            link(dve.tensor_reduce(el, gsel.rearrange("p i g e -> p i e g"), AX, ALU.add))
            for i in range(3):
                last = dve.max(v8[:, i, :], el[:, i, :])
            link(last)
            for i in range(3):
                last = dve.max_index(i8[:, 1, i, :], v8[:, i, :], el[:, i, :])
            link(last)
            dve.tensor_tensor(dv, v8[:, :, 1], v8[:, :, 0], ALU.subtract).then_inc(route_in, 1)
            link(dve.tensor_copy(eidx, i8[:, 1, :, 0:2]))
            link(dve.scalar_tensor_tensor(eid, gidx.unsqueeze(2).to_broadcast([P, 3, 2]), float(EPG), eidx, ALU.mult, ALU.add))
            link(dve.tensor_tensor(hot, iota.unsqueeze(1).unsqueeze(1).to_broadcast([P, 3, 2, NE]),
                                   eid.unsqueeze(3).to_broadcast([P, 3, 2, NE]), ALU.is_equal))
            dve.tensor_tensor(hot2, hot[:, :, 0, :], hot[:, :, 1, :], ALU.add).then_inc(hot_ready, 1)
            dve.wait_ge(route_act, 2)
            link(dve.tensor_reduce(gsum, gx, AX, ALU.add))
            link(dve.reciprocal(gp, gsum))
            dve.wait_ge(route_act, 3)
            link(dve.tensor_scalar(den, ev, 1.0, None, ALU.add))
            link(dve.reciprocal(rden, den))
            link(dve.tensor_tensor(gate[:, :, 0], gp, rden, ALU.mult))
            link(dve.tensor_tensor(gate[:, :, 1], gate[:, :, 0], ev, ALU.mult))
            dve.wait_ge(route_pe, 1)
            b = ps[:, SSQ_BANK, :]
            dve.tensor_copy(slot_of[:, 0:2, :], b[:, 0:64].rearrange("p (i e) -> p i e", i=2))
            link(dve.tensor_copy(slot_of[0:64, 2, :], b[0:64, 64:96]))
            link(dve.tensor_tensor(prod, hot, slot_of.unsqueeze(2).to_broadcast([P, 3, 2, NE]), ALU.mult))
            link(dve.tensor_reduce(rank, prod, AX, ALU.add))
            dve.scalar_tensor_tensor(place, eid, float(B), rank, ALU.mult, ALU.add)
            link(dve.tensor_scalar(high, rank, float(B), -1.0e6, ALU.is_ge, ALU.mult))
            link(dve.tensor_tensor(place, place, high, ALU.add))

            def pick_tokens(link, where, width, eq, pick, pickr, gpick, signal, gates_signal):
                link(dve.tensor_tensor(eq, const[:, C_IOTA:C_IOTA + width].unsqueeze(1).unsqueeze(1).to_broadcast([P, 3, 2, width]),
                                       where.unsqueeze(3).to_broadcast([P, 3, 2, width]), ALU.is_equal))
                link(dve.tensor_tensor(pick, eq[:, :, 0, :], eq[:, :, 1, :], ALU.add))
                dve.tensor_tensor(pickr, pick, hrs.unsqueeze(2).to_broadcast([P, 3, width]), ALU.mult).then_inc(signal, 1)
                link(dve.tensor_tensor(eq, eq, gate.unsqueeze(3).to_broadcast([P, 3, 2, width]), ALU.mult))
                g = [eq[:, :, k, :] for k in range(2)]
                if width == B:
                    g = [v.unsqueeze(2).to_broadcast([P, 3, 4, B]) for v in g]
                    gpick = gpick.rearrange("p i (r s) -> p i r s", r=4)
                dve.tensor_tensor(gpick, g[0], g[1], ALU.add).then_inc(gates_signal, 1)

            def add_results(full_sem, value, signal):
                for u in range(12):
                    i, n = u // 4, u % 4
                    tn = TILES[i][1]
                    dve.wait_ge(full_sem, value(u + 1))
                    h = xtile[0:tn, i, 512 * n:512 * n + 512]
                    dve.tensor_tensor(h, ps[0:tn, 5 + u % 3, :], h, ALU.add).then_inc(signal, 1)

            def times_up(signal):
                dve.tensor_tensor(hT, sil, ps[:, 3, 0:256].rearrange("p (c m s) -> p c m s", c=4, m=2)[:, :, 1, :],
                                  ALU.mult).then_inc(signal, 1)

            x_links = 4

            def extra_blocks(e):
                count = dve.value_load(tables[0:1, 1, bass.ds(e, 1)], min_val=1, max_val=MAXB)
                with dve.If(count > 1):
                    before = dve.value_load(tables[0:1, 0, bass.ds(e, 1)], min_val=0, max_val=64)
                    with dve.Fori(1, count) as k:
                        x = before + k
                        done = [0]

                        def link_x(ins):
                            done[0] += 1
                            ins.then_inc(x_step, 1)
                            dve.wait_ge(x_step, x * x_links + done[0])

                        link_x(dve.tensor_scalar(dest, dest, float(-B), None, ALU.add))
                        pick_tokens(link_x, dest, B, eqx, pickx, pickrx, gpickx, x_pick, x_gates)
                        assert done[0] == x_links
                        dve.wait_ge(x_silu, x)
                        times_up(x_hT)
                        add_results(x_full, lambda v: before * 12 + (k * 12 + v - 12), x_added)

            pick_tokens(link, place, P, eq, pick, pickr, gpick, pick_ready, gates_ready)
            dve.wait_ge(route_pe, 2)
            link(dve.tensor_tensor(cmp, ps[:, ACC_BANK, 0:NE].unsqueeze(2).to_broadcast([P, NE, MAXB - 1]),
                                   const[:, C_THR:C_THR + MAXB - 1].unsqueeze(1).to_broadcast([P, NE, MAXB - 1]), ALU.is_gt))
            link(dve.tensor_reduce(extra, cmp, AX, ALU.add))
            link(dve.tensor_tensor_scan(xincl, extra, extra, 0.0, ALU.add, ALU.bypass))
            link(dve.tensor_tensor(xexcl, xincl, extra, ALU.subtract))
            dve.tensor_copy(tables[0:1, 0, :], xexcl[0:1, :]).then_inc(routed, 1)
            dve.tensor_scalar(tables[0:1, 1, :], extra[0:1, :], 1.0, None, ALU.add).then_inc(routed, 1)
            dve.tensor_scalar(tables[0:1, 2, :], xincl[0:1, :], 12.0, 12.0, ALU.mult, ALU.add).then_inc(routed, 1)
            dve.tensor_scalar(tables[0:1, 3, :], xexcl[0:1, :], 1.0, None, ALU.add).then_inc(routed, 1)
            link(dve.scalar_tensor_tensor(placex, eid, 512.0, rank, ALU.mult, ALU.add))
            dve.sem_inc(comb_added, 1)
            dve.sem_inc(x_added, 12)
            dve.sem_inc(x_step, x_links)
            links = 12
            dve.wait_ge(routed, 3)
            with dve.Fori(0, NE // 4) as q:
                done = [0]

                def link_q(ins):
                    done[0] += 1
                    ins.then_inc(blk_step, 1)
                    dve.wait_ge(blk_step, q * links + done[0])

                for b in range(4):
                    e = q * 4 + b
                    link_q(dve.tensor_copy(dest, placex))
                    link_q(dve.tensor_scalar(placex, placex, -512.0, None, ALU.add))
                    if b == 3:
                        dve.wait_ge(gathered, q * 4 + 4)
                        dve.wait_ge(gt_full, q + 1)
                        link_q(dve.tensor_scalar(place, place, float(-P), None, ALU.add))
                        pick_tokens(link_q, place, P, eq, pick, pickr, gpick, pick_ready, gates_ready)
                    dve.wait_ge(silu_ready, e + 1)
                    times_up(hT_ready)
                    extra_blocks(e)
                assert done[0] == links, done
                add_results(comb_full, lambda v: q * 12 + v, comb_added)

            dve.wait_ge(s_gfin, 16)
            for i, (t0, tn) in enumerate(TILES):
                dve.wait_ge(fin_rooted, i + 1)
                link(dve.reciprocal(xrs[0:tn, i:i + 1], xsd[0:tn, i:i + 1]))
                dve.scalar_tensor_tensor(xtile[0:tn, i, :], xtile[0:tn, i, :], xrs[0:tn, i:i + 1], gain[0:tn, :],
                                         ALU.mult, ALU.mult).then_inc(fin_ready, 1)


def shape_constants():
    import numpy as np

    c = np.zeros((P, C_ALL), np.float32)
    c[:, C_ID:C_ID + P] = np.eye(P)
    half = ROPE // 2
    swap = np.zeros((ROPE, ROPE), np.float32)
    swap[np.arange(half) + half, np.arange(half)] = -1
    swap[np.arange(half), np.arange(half) + half] = 1
    for i in range(2):
        s = slice(ROPE * i, ROPE * (i + 1))
        c[s, C_ROT + ROPE * i:C_ROT + ROPE * (i + 1)] = swap
        c[0:ROPE, C_DUP + ROPE * i:C_DUP + ROPE * (i + 1)] = np.eye(ROPE)
        c[0:ROPE, C_DROT + ROPE * i:C_DROT + ROPE * (i + 1)] = swap
    c[:, C_TRI:C_TRI + P] = np.triu(np.ones((P, P)), 1)
    for q in range(4):
        c[B * q + np.arange(B), C_FOLD + B * (q // 2) + np.arange(B)] = 1
    c[:, C_IOTA:C_IOTA + P] = np.arange(P)
    c[:, C_THR:C_THR + MAXB - 1] = B * np.arange(1, MAXB)
    inv = np.float32(10000.0) ** (-np.arange(0, ROPE, 2, dtype=np.float32) / np.float32(ROPE))
    angle = np.arange(T, dtype=np.float32)[None, :] * inv[:, None]
    c[:, C_COS:C_COS + T] = np.tile(np.cos(angle), (4, 1))
    c[:, C_SIN:C_SIN + T] = np.tile(np.sin(angle), (4, 1))
    return c


_INS = ["x_prompt", "x_sample", "cache_kv_latent", "cache_k_rope", "state_conv", "norm_mix", "w_in", "norm_q",
        "w_uq", "norm_kv", "w_uk", "w_uv", "conv_w", "norm_attn_out", "norm_conv_out", "w_o", "norm_ffn",
        "w_router_group", "b_router_group", "w_router_expert", "b_router_expert", "w_gate", "w_up", "w_down",
        "norm_final"]
_OUTS = {
    "y_prompt": (1, SEQ, D), "y_sample": (1, DEC, D),
    "kv_prompt": (1, 1, SEQ, KL), "kr_prompt": (1, 1, SEQ, ROPE), "conv_prompt": (1, 1, 2, CH),
    "kv_sample": (1, 1, DEC, KL), "kr_sample": (1, 1, DEC, ROPE), "conv_sample": (1, 1, 2, CH),
}


def kernel(**inputs):
    import numpy as np
    import concourse.bacc as bacc
    from concourse.bass_utils import run_bass_kernel_spmd

    nc = bacc.Bacc("TRN2", target_bir_lowering=False, num_devices=1)
    arrays = {f"in_{name}": np.ascontiguousarray(inputs[name]) for name in _INS}
    arrays["in_const"] = shape_constants()
    a = {name[3:]: nc.dram_tensor(name, v.shape, mybir.dt.from_np(v.dtype), kind="ExternalInput").ap()
         for name, v in arrays.items()}
    for name, shape in _OUTS.items():
        a[name] = nc.dram_tensor(f"out_{name}", shape, F32, kind="ExternalOutput").ap()
    trunk_layer_kernel(nc, a)
    r = run_bass_kernel_spmd(nc, [arrays], core_ids=[0])
    return tuple(r.results[0][f"out_{name}"] for name in _OUTS)
```
